# Optimizing a Trainium2 kernel written in Bass

```python
import math
import jax
import jax.numpy as jnp
from jax import lax
import numpy as np

D_MODEL = 2048
BATCH = 1
SEQ = 512
DEPTH = 1
DEC_BATCH = 8
DEC_SEQ = 8
PAST_LEN = 4096
PAGE_SIZE = 128

MIX_WIDTH = D_MODEL
LRU_WIDTH = MIX_WIDTH // 2
LRU_HEADS = 8
LRU_BLOCK = LRU_WIDTH // LRU_HEADS
LRU_C = 8.0
CONV_W = 4
DN_WIDTH = MIX_WIDTH - LRU_WIDTH
DN_HEADS = 8
DN_DK = 128
DN_DV = DN_WIDTH // DN_HEADS
DN_KEY = DN_HEADS * DN_DK
DN_CONV_CH = 2 * DN_KEY + DN_WIDTH
DN_CHUNK = 64
IN_COLS = 2 * LRU_WIDTH + DN_CONV_CH + DN_WIDTH + 2 * DN_HEADS
PEER_HEADS = 8
PEER_NKEYS = 128
PEER_N_EXPERTS = PEER_NKEYS * PEER_NKEYS
PEER_QDIM = 256
PEER_HALF = PEER_QDIM // 2
PEER_TOPK = 16
PEER_BLOCK = 128
NORM_EPS = 1e-6

kernel_name = 'hymba_rglru_gdn_peer_adaln_step'

def _rmsnorm(x, w):
    xf = x.astype(jnp.float32)
    y = xf * lax.rsqrt(jnp.mean(xf * xf, axis=-1, keepdims=True) + NORM_EPS)
    return (y * w.astype(jnp.float32)).astype(x.dtype)

def _l2norm(x):
    return x * lax.rsqrt(jnp.sum(x * x, axis=-1, keepdims=True) + NORM_EPS)

def _causal_conv(x, buf, w, b=None):
    T = x.shape[1]
    xp = jnp.concatenate([buf.astype(x.dtype), x], axis=1)
    y = sum(xp[:, k:k + T] * w[k] for k in range(CONV_W))
    if b is not None:
        y = y + b
    return y, xp[:, -(CONV_W - 1):]

def _rg_lru(x, h0, wa, ba, wx, bx, lam, reset_first):
    Bn, T, W = x.shape
    xb = x.reshape(Bn, T, LRU_HEADS, LRU_BLOCK)
    r = jax.nn.sigmoid((jnp.einsum('bthi,hij->bthj', xb, wa).reshape(Bn, T, W) + ba).astype(jnp.float32))
    i = jax.nn.sigmoid((jnp.einsum('bthi,hij->bthj', xb, wx).reshape(Bn, T, W) + bx).astype(jnp.float32))
    log_a = -LRU_C * r * jax.nn.softplus(-lam.astype(jnp.float32))
    a = jnp.exp(log_a)
    mult = jnp.sqrt(jnp.maximum(-jnp.expm1(2.0 * log_a), 0.0))
    if reset_first:
        mult = mult.at[:, 0].set(1.0)
    u = mult * i * x.astype(jnp.float32)

    def step(h, inp):
        a_t, u_t = inp
        h = a_t * h + u_t
        return h, h

    hT, hs = lax.scan(step, h0.astype(jnp.float32), (jnp.swapaxes(a, 0, 1), jnp.swapaxes(u, 0, 1)))
    return jnp.swapaxes(hs, 0, 1), hT

def _gated_delta(q, k, v, g, beta, S0):
    Bn, T, H, _ = q.shape
    C = min(DN_CHUNK, T)
    n = -(-T // C)
    pad = n * C - T
    f32 = jnp.float32
    q = _l2norm(q.astype(f32)) * (DN_DK ** -0.5)
    k = _l2norm(k.astype(f32))
    v = v.astype(f32)

    def blocks(t):
        t = jnp.pad(t, [(0, 0), (0, pad)] + [(0, 0)] * (t.ndim - 2))
        t = jnp.swapaxes(t, 1, 2)
        return t.reshape(t.shape[:2] + (n, C) + t.shape[3:])

    q, k, v, g, beta = blocks(q), blocks(k), blocks(v), blocks(g), blocks(beta)
    g = jnp.cumsum(g, axis=-1)
    tri = jnp.tril(jnp.ones((C, C), bool))
    strict = jnp.tril(jnp.ones((C, C), bool), -1)
    diff = g[..., :, None] - g[..., None, :]
    decay = jnp.where(tri, jnp.exp(jnp.where(tri, diff, 0.0)), 0.0)
    kb = k * beta[..., None]
    vb = v * beta[..., None]
    L = jnp.where(strict, jnp.einsum('bhncd,bhnsd->bhncs', kb, k) * decay, 0.0)
    A = L + jnp.eye(C, dtype=f32)
    rhs = jnp.concatenate([vb, kb * jnp.exp(g)[..., None]], axis=-1)
    sol = lax.linalg.triangular_solve(A, rhs, left_side=True, lower=True, unit_diagonal=True)
    u, w = sol[..., :DN_DV], sol[..., DN_DV:]
    attn = jnp.where(tri, jnp.einsum('bhncd,bhnsd->bhncs', q, k) * decay, 0.0)

    def step(S, inp):
        q_i, k_i, u_i, w_i, g_i, a_i = inp
        v_new = u_i - jnp.einsum('bhcd,bhde->bhce', w_i, S)
        o = jnp.einsum('bhcd,bhde->bhce', q_i * jnp.exp(g_i)[..., None], S) + jnp.einsum('bhcs,bhse->bhce', a_i, v_new)
        g_last = g_i[..., -1]
        S = S * jnp.exp(g_last)[..., None, None] + jnp.einsum(
            'bhcd,bhce->bhde', k_i * jnp.exp(g_last[..., None] - g_i)[..., None], v_new)
        return S, o

    xs = tuple(jnp.moveaxis(t, 2, 0) for t in (q, k, u, w, g, attn))
    S_T, o = lax.scan(step, S0.astype(f32), xs)
    o = jnp.moveaxis(o, 0, 2).reshape(Bn, H, n * C, DN_DV)
    return jnp.swapaxes(o, 1, 2)[:, :T], S_T

def _mixer(h, lru_conv, lru_h, dn_conv, dn_S, reset_first, p):
    Bn, T, _ = h.shape
    f32 = jnp.float32
    proj = h @ p['w_in']
    o1 = LRU_WIDTH
    o2 = 2 * LRU_WIDTH
    o3 = o2 + DN_CONV_CH
    o4 = o3 + DN_WIDTH
    o5 = o4 + DN_HEADS
    x_l, y_l, qkv, z, b_dn, a_dn = jnp.split(proj, [o1, o2, o3, o4, o5], axis=-1)
    xc, new_lru_conv = _causal_conv(x_l, lru_conv, p['lru_conv_w'], p['lru_conv_b'])
    hs, new_lru_h = _rg_lru(xc, lru_h, p['lru_wa'], p['lru_ba'], p['lru_wx'], p['lru_bx'], p['lru_lambda'], reset_first)
    out_lru = (hs * jax.nn.gelu(y_l.astype(f32))).astype(h.dtype)
    qkv_c, new_dn_conv = _causal_conv(qkv, dn_conv, p['dn_conv_w'])
    qkv_c = jax.nn.silu(qkv_c)
    q, k, v = jnp.split(qkv_c, [DN_KEY, 2 * DN_KEY], axis=-1)
    q = q.reshape(Bn, T, DN_HEADS, DN_DK)
    k = k.reshape(Bn, T, DN_HEADS, DN_DK)
    v = v.reshape(Bn, T, DN_HEADS, DN_DV)
    beta = jax.nn.sigmoid(b_dn.astype(f32))
    g = -jnp.exp(p['dn_A_log'].astype(f32)) * jax.nn.softplus(a_dn.astype(f32) + p['dn_dt_bias'].astype(f32))
    o, new_dn_S = _gated_delta(q, k, v, g, beta, dn_S)
    o = _rmsnorm(o, p['dn_norm_w']) * jax.nn.silu(z.reshape(Bn, T, DN_HEADS, DN_DV).astype(f32))
    out_dn = o.reshape(Bn, T, DN_WIDTH).astype(h.dtype)
    mix = jnp.concatenate([out_lru, out_dn], axis=-1) @ p['w_out']
    return mix, (new_lru_conv, new_lru_h, new_dn_conv, new_dn_S)

def _peer(h, p):
    Bn, T, D = h.shape
    N = Bn * T
    nb = -(-N // PEER_BLOCK)
    xt = jnp.pad(h.reshape(N, D), ((0, nb * PEER_BLOCK - N), (0, 0))).reshape(nb, PEER_BLOCK, D)

    def block_fn(xb):
        qry = (xb @ p['peer_wq']).reshape(PEER_BLOCK, PEER_HEADS, 2, PEER_HALF)
        s = jnp.einsum('phsd,hsnd->phsn', qry, p['peer_subkeys']).astype(jnp.float32)
        s1, i1 = lax.top_k(s[:, :, 0], PEER_TOPK)
        s2, i2 = lax.top_k(s[:, :, 1], PEER_TOPK)
        cand = (s1[..., :, None] + s2[..., None, :]).reshape(PEER_BLOCK, PEER_HEADS, PEER_TOPK * PEER_TOPK)
        cidx = (i1[..., :, None] * PEER_NKEYS + i2[..., None, :]).reshape(PEER_BLOCK, PEER_HEADS, PEER_TOPK * PEER_TOPK)
        top_s, pos = lax.top_k(cand, PEER_TOPK)
        idx = jnp.take_along_axis(cidx, pos, axis=-1)
        gates = jax.nn.softmax(top_s, axis=-1)
        u_rows = p['peer_u'][idx]
        act = jax.nn.gelu(jnp.einsum('phkd,pd->phk', u_rows, xb).astype(jnp.float32))
        coef = (gates * act).astype(xb.dtype)
        return jnp.einsum('phk,phkd->pd', coef, p['peer_v'][idx])

    out = lax.map(block_fn, xt).reshape(nb * PEER_BLOCK, D)[:N]
    return out.reshape(Bn, T, D)

def _layer(x, c, lru_conv, lru_h, dn_conv, dn_S, reset_first, p):
    mod = jax.nn.silu(c) @ p['w_ada'] + p['b_ada']
    sh1, sc1, g1, sh2, sc2, g2 = jnp.split(mod, 6, axis=-1)
    h = _rmsnorm(x, p['norm_mix_w']) * (1.0 + sc1[:, None]) + sh1[:, None]
    mix, new_states = _mixer(h, lru_conv, lru_h, dn_conv, dn_S, reset_first, p)
    x = x + g1[:, None] * mix
    h = _rmsnorm(x, p['norm_ffn_w']) * (1.0 + sc2[:, None]) + sh2[:, None]
    x = x + g2[:, None] * _peer(h, p)
    return x, new_states

def setup_inputs(seed: int = 0) -> dict:
    key = jax.random.key(seed)
    ks = jax.random.split(key, 32)
    nrm = jax.random.normal
    f32 = jnp.float32
    L, D = DEPTH, D_MODEL
    lam_a = jax.random.uniform(ks[10], (L, LRU_WIDTH), f32, 0.9, 0.999) ** (1.0 / LRU_C)
    dt = jnp.exp(jax.random.uniform(ks[14], (L, DN_HEADS), f32, math.log(1e-3), math.log(1e-1)))
    return {
        'x_prompt': nrm(ks[0], (BATCH, SEQ, D), f32),
        'x_sample': nrm(ks[1], (DEC_BATCH, DEC_SEQ, D), f32),
        'state_lru_conv': nrm(ks[2], (L, DEC_BATCH, CONV_W - 1, LRU_WIDTH), f32),
        'state_lru_h': 0.5 * nrm(ks[3], (L, DEC_BATCH, LRU_WIDTH), f32),
        'state_dn_conv': nrm(ks[4], (L, DEC_BATCH, CONV_W - 1, DN_CONV_CH), f32),
        'state_dn_S': 0.1 * nrm(ks[5], (L, DEC_BATCH, DN_HEADS, DN_DK, DN_DV), f32),
        'c_prompt': nrm(ks[6], (BATCH, D), f32),
        'c_sample': nrm(ks[7], (DEC_BATCH, D), f32),
        'w_ada': 0.5 * D ** -0.5 * nrm(ks[8], (L, D, 6 * D), f32),
        'b_ada': 0.01 * nrm(ks[9], (L, 6 * D), f32),
        'norm_mix_w': 1.0 + 0.02 * nrm(ks[11], (L, D), f32),
        'norm_ffn_w': 1.0 + 0.02 * nrm(ks[12], (L, D), f32),
        'w_in': D ** -0.5 * nrm(ks[13], (L, D, IN_COLS), f32),
        'lru_conv_w': CONV_W ** -0.5 * nrm(ks[15], (L, CONV_W, LRU_WIDTH), f32),
        'lru_conv_b': 0.01 * nrm(ks[16], (L, LRU_WIDTH), f32),
        'lru_wa': LRU_BLOCK ** -0.5 * nrm(ks[17], (L, LRU_HEADS, LRU_BLOCK, LRU_BLOCK), f32),
        'lru_ba': 0.1 * nrm(ks[18], (L, LRU_WIDTH), f32),
        'lru_wx': LRU_BLOCK ** -0.5 * nrm(ks[19], (L, LRU_HEADS, LRU_BLOCK, LRU_BLOCK), f32),
        'lru_bx': 0.1 * nrm(ks[20], (L, LRU_WIDTH), f32),
        'lru_lambda': jnp.log(lam_a) - jnp.log1p(-lam_a),
        'dn_conv_w': CONV_W ** -0.5 * nrm(ks[21], (L, CONV_W, DN_CONV_CH), f32),
        'dn_A_log': jnp.log(jax.random.uniform(ks[22], (L, DN_HEADS), f32, 1.0, 16.0)),
        'dn_dt_bias': dt + jnp.log(-jnp.expm1(-dt)),
        'dn_norm_w': 1.0 + 0.02 * nrm(ks[23], (L, DN_DV), f32),
        'w_out': MIX_WIDTH ** -0.5 * nrm(ks[24], (L, MIX_WIDTH, D), f32),
        'peer_wq': D ** -0.5 * nrm(ks[25], (L, D, PEER_HEADS * PEER_QDIM), f32),
        'peer_subkeys': PEER_HALF ** -0.5 * nrm(ks[26], (L, PEER_HEADS, 2, PEER_NKEYS, PEER_HALF), f32),
        'peer_u': D ** -0.5 * nrm(ks[27], (L, PEER_N_EXPERTS, D), f32),
        'peer_v': PEER_HEADS ** -0.5 * nrm(ks[28], (L, PEER_N_EXPERTS, D), f32),
        'final_norm_w': 1.0 + 0.02 * nrm(ks[29], (D,), f32),
    }

def reference(x_prompt, x_sample, state_lru_conv, state_lru_h, state_dn_conv, state_dn_S, c_prompt, c_sample,
              w_ada, b_ada, norm_mix_w, norm_ffn_w, w_in, lru_conv_w, lru_conv_b, lru_wa, lru_ba, lru_wx, lru_bx,
              lru_lambda, dn_conv_w, dn_A_log, dn_dt_bias, dn_norm_w, w_out, peer_wq, peer_subkeys, peer_u, peer_v,
              final_norm_w):
    Bp = x_prompt.shape[0]
    xp, xs = x_prompt, x_sample
    p_lc, p_lh, p_dc, p_dS = [], [], [], []
    s_lc, s_lh, s_dc, s_dS = [], [], [], []
    for l in range(DEPTH):
        p = {'w_ada': w_ada[l], 'b_ada': b_ada[l], 'norm_mix_w': norm_mix_w[l], 'norm_ffn_w': norm_ffn_w[l],
             'w_in': w_in[l], 'lru_conv_w': lru_conv_w[l], 'lru_conv_b': lru_conv_b[l], 'lru_wa': lru_wa[l],
             'lru_ba': lru_ba[l], 'lru_wx': lru_wx[l], 'lru_bx': lru_bx[l], 'lru_lambda': lru_lambda[l],
             'dn_conv_w': dn_conv_w[l], 'dn_A_log': dn_A_log[l], 'dn_dt_bias': dn_dt_bias[l],
             'dn_norm_w': dn_norm_w[l], 'w_out': w_out[l], 'peer_wq': peer_wq[l],
             'peer_subkeys': peer_subkeys[l], 'peer_u': peer_u[l], 'peer_v': peer_v[l]}
        xp, (lc, lh, dc, dS) = _layer(
            xp, c_prompt,
            jnp.zeros((Bp, CONV_W - 1, LRU_WIDTH), xp.dtype), jnp.zeros((Bp, LRU_WIDTH), jnp.float32),
            jnp.zeros((Bp, CONV_W - 1, DN_CONV_CH), xp.dtype), jnp.zeros((Bp, DN_HEADS, DN_DK, DN_DV), jnp.float32),
            True, p)
        p_lc.append(lc); p_lh.append(lh); p_dc.append(dc); p_dS.append(dS)
        xs, (lc, lh, dc, dS) = _layer(xs, c_sample, state_lru_conv[l], state_lru_h[l], state_dn_conv[l],
                                      state_dn_S[l], False, p)
        s_lc.append(lc); s_lh.append(lh); s_dc.append(dc); s_dS.append(dS)
    y_prompt = _rmsnorm(xp, final_norm_w)
    y_sample = _rmsnorm(xs, final_norm_w)
    return (y_prompt, y_sample,
            jnp.stack(p_lc), jnp.stack(p_lh), jnp.stack(p_dc), jnp.stack(p_dS),
            jnp.stack(s_lc), jnp.stack(s_lh), jnp.stack(s_dc), jnp.stack(s_dS))


_drawn_inputs = setup_inputs


def setup_inputs(seed=0):
    import zlib

    import numpy as np

    out = dict(_drawn_inputs(seed))
    spreads = {}
    factors = {'norm_ffn_w': 7.32, 'lru_ba': 3.463, 'dn_norm_w': 8.0, 'final_norm_w': 2.842}
    for name, (base, spread) in spreads.items():
        noise = np.random.default_rng([zlib.crc32(name.encode()), seed]).standard_normal(out[name].shape)
        drawn = base * np.exp(spread * noise) if base else spread * noise
        out[name] = jnp.asarray(drawn.astype(out[name].dtype))
    for name, factor in factors.items():
        out[name] = (out[name] * factor).astype(out[name].dtype)
    return out
```

```python
from contextlib import ExitStack

import numpy as np

import concourse.bass as bass
from concourse import mybir

ALU = mybir.AluOpType
ACT = mybir.ActivationFunctionType
AX = mybir.AxisListType
F32 = mybir.dt.float32
F32R = mybir.dt.float32r
U32 = mybir.dt.uint32

P = 128
D = 2048
KT = D // P
TP = 512
NB, NS = 8, 8
TS = NB * NS
T = TP + TS
HT = T // 2
NC = 1 + NB
H = 8
CW = 4
PL = CW - 1
SP = PL + NS
PADW = PL + TP + NB * SP
CONVW = PADW - PL
SB0 = PL + TP
CH = 128
NCH = TP // CH
NTT = NCH + 1
EPS = 1e-6
NM = 6 * D // P
HALF = 8 * P
NKEY = 128
TOPK = 16
NG = 4
NGRP = NKEY // NG
GB = 72
NGB = T // GB
PACK = 5 * CW + 4 * NB * PL + 2 * P + NB
ACT_STEPS_A_TURN = 27
DVE_STEPS_A_TURN = 81
LOW = -3.0e38
NBANK = 512

C_ID, C_LEVEL, C_INCL, C_SINCL, C_BM, C_IOTA, CONSTS = 0, 128, 128 + 7 * 128, 1152, 1216, 1224, 1352
LEVELS = 7


def constants():
    c = np.zeros((P, CONSTS), np.float32)
    j, i = np.meshgrid(np.arange(P), np.arange(P), indexing="ij")
    c[:, C_ID:C_ID + P] = np.eye(P)
    for n in range(LEVELS):
        s = 1 << n
        c[:, C_LEVEL + n * P:C_LEVEL + (n + 1) * P] = (i // (2 * s) == j // (2 * s)) & (i // s % 2 == 1) & (j // s % 2 == 0)
    c[:, C_INCL:C_INCL + P] = j <= i
    c[:TS, C_SINCL:C_SINCL + TS] = ((j <= i) & (j // NS == i // NS))[:TS, :TS]
    for b in range(NB):
        c[b * NS:(b + 1) * NS, C_BM + b] = 1
    c[:, C_IOTA:C_IOTA + P] = np.arange(P)[None, :]
    return c


class Chain:

    def __init__(self, eng, sem, total, carry=None):
        self.eng, self.sem, self.total, self.base, self.n, self.carry = eng, sem, total, total[0], 0, carry

    def __call__(self, ins):
        ins.then_inc(self.sem, 1)
        self.n += 1
        self.eng.wait_ge(self.sem, self.base + self.n)
        if isinstance(self.base, int):
            self.total[0] = self.base + self.n
        if self.carry:
            self.carry()

    def enter(self, i, steps):
        self.start, self.steps = self.base + self.n, steps
        self.base, self.n = self.start + i * steps, 0

    def leave(self, turns):
        assert self.n == self.steps, f"{self.n} steps in a turn"
        self.base, self.n = self.start + turns * self.steps, 0
        self.total[0] = self.base


class Sems:
    pass


class Nth:

    def __init__(self, c, i=0, per=0):
        self.c, self.i, self.per = c, i, per
        self.n = c + i * per
        self.raw, self.slot = c % 2, c % 4
        assert per % 4 == 0

    def plus(self, j):
        return Nth(self.c + j, self.i, self.per)

    def loads(self):
        return 16 * (self.c // 2 + 1) + self.i * (8 * self.per)


def row(t, i):
    if isinstance(i, int):
        return t[i]
    r = t[bass.ds(i, 1)]
    return r.rearrange("a p f -> (a p) f") if len(t.shape) == 3 else r.rearrange("a p k f -> (a p) k f")


def build(nc, a):
    stack = ExitStack()
    with stack:
        base = [(nc.sbuf_base + 31) // 32 * 32]

        def sb(name, shape, dt=F32, at=None):
            at = base if at is None else at
            n = 4
            for x in shape[1:]:
                n *= x
            t = nc.alloc_sbuf_tensor_at(name, list(shape), dt, offset=at[0])
            at[0] += (n + 31) // 32 * 32
            assert at[0] <= nc.sbuf_usable_end, (name, at[0])
            return t

        def ps(name, shape):
            return stack.enter_context(nc.psum_tensor(name, list(shape), F32))

        const = sb("const", [P, CONSTS])
        ones = sb("ones", [P, P])
        modT = sb("modT", [P, NM, NC])
        vecs = sb("vecs", [P, NM + 3 * KT + 1])
        eps = sb("eps", [P, 1])
        raw_at = base[0]
        raw = sb("raw", [P, 2, HALF])
        whi = sb("whi", [P, 4, HALF], F32R)
        wlo = sb("wlo", [P, 4, HALF], F32R)
        ident = const[:, C_ID:C_ID + P]
        bada = vecs[:, 0:NM]
        normw = [vecs[:, NM + n * KT:NM + (n + 1) * KT] for n in range(3)]
        dnw = vecs[:, NM + 3 * KT:NM + 3 * KT + 1]
        act_hi = sb("act_hi", [P, KT, T], F32R)
        act_lo = sb("act_lo", [P, KT, T], F32R)
        after = base[0]
        act_at = after - 2 * KT * T * 4

        gps = ps("gps", [P, 4, NBANK])
        dps = ps("dps", [P, 4, NBANK])

        mixD = nc.dram_tensor("mixD", [2 * H, P, T], F32, kind="Internal").ap()
        x1D = nc.dram_tensor("x1D", [P, KT, T], F32, kind="Internal").ap()
        rowsD = nc.dram_tensor("rowsD", [H, 4, T], F32, kind="Internal").ap()
        gateD = nc.dram_tensor("gateD", [NGB, P, NKEY, GB], F32, kind="Internal").ap()

        def sems(ctx, *names):
            return [ctx.enter_context(nc.semaphore(n)) for n in names]

        W = Sems()
        W.loaded0, W.loaded1, W.hi, W.lo, W.used = sems(stack, "w_loaded0", "w_loaded1", "w_hi", "w_lo", "w_used")
        W.act_steps, W.dve_steps = sems(stack, "w_act_steps", "w_dve_steps")
        act_total, dve_total = [0], [0]
        w_loaded = [W.loaded0, W.loaded1]

        def load_half(sp, src, k):
            if not (isinstance(k.n, int) and k.n < 2):
                sp.wait_ge(W.lo, k.n - 1)
            sp.dma_start(raw[:, k.raw, :], src).then_inc(w_loaded[k.raw], 16)

        def split_hi(act, k):
            act.wait_ge(w_loaded[k.raw], k.loads())
            if not (isinstance(k.n, int) and k.n < 4):
                act.wait_ge(W.used, k.n - 3)
            act.copy(whi[:, k.slot, :], raw[:, k.raw, :]).then_inc(W.hi, 1)

        def split_lo(pool, k):
            pool.wait_ge(W.hi, k.n + 1)
            pool.tensor_tensor(wlo[:, k.slot, :], raw[:, k.raw, :], whi[:, k.slot, :].bitcast(F32),
                               ALU.subtract).then_inc(W.lo, 1)

        def gemm_part(pe, k, half, pair, first, count):
            if first == 0:
                pe.wait_ge(W.lo, k.n + 1)
            for kk in range(first, first + count):
                kt = half * 8 + kk
                hi, lo = (w[:, k.slot, kk * P:(kk + 1) * P] for w in (whi, wlo))
                for n, (w, x) in enumerate(((hi, act_hi), (hi, act_lo), (lo, act_hi))):
                    for th in range(2):
                        m = pe.matmul(gps[:, 2 * pair + th, 0:HT], w, x[:, kt, th * HT:(th + 1) * HT],
                                      start=(kt == 0 and n == 0), stop=(kt == KT - 1 and n == 2))
            if first + count == 8:
                m.then_inc(W.used, 1)
            return m

        def bc(ap, shape):
            return ap.broadcast_to(list(shape))

        def samples(ap):
            return ap[:, TP:T].rearrange("p (b s) -> p b s", b=NB)

        def padded(ap, first, count):
            return ap[:, SB0:SB0 + NB * SP].rearrange("p (b s) -> p b s", b=NB)[:, :, first:first + count]

        ctx0 = stack.enter_context(ExitStack())
        S = Sems()
        S.consts, S.x, S.c, S.silu, S.ones = sems(ctx0, "p0_consts", "p0_x", "p0_c", "p0_silu", "p0_ones")
        S.sq, S.sqpe, S.stat, S.wada0, S.wada1 = sems(ctx0, "p0_sq", "p0_sqpe", "p0_stat", "p0_wada0", "p0_wada1")
        S.mm, S.rows, S.tr, S.added, S.eps = sems(ctx0, "p0_mm", "p0_rows", "p0_tr", "p0_added", "p0_eps")
        S.zero, = sems(ctx0, "p0_zero")
        at0 = [act_at]
        wada = sb("wada", [P, 2, KT, NBANK], at=at0)
        at0 = [after]
        xT = sb("xT", [P, KT, T], at=at0)
        rB = sb("rB", [P, T], at=at0)
        amod = sb("amod", [P, KT, NC], at=at0)
        tmp = sb("tmp", [P, 2, T], at=at0)
        p1at = at0[0]
        arow = sb("arow", [P, 2, NBANK], at=at0)
        ct = sb("ct", [P, KT, NC], at=at0)
        cs = sb("cs", [P, KT, NC], at=at0)
        sq = sb("sq", [P, 2, T], at=at0)
        s_wada = [S.wada0, S.wada1]
        NGA = 6 * D // NBANK
        w_ada_v = a["w_ada"].rearrange("(k p) n -> p k n", p=P)

        with nc.Block() as block:
            @block.sync
            def _(sp):
                sp.dma_start(const[:, :], a["consts"]).then_inc(S.consts, 16)
                sp.dma_start(vecs[:, :], a["vecs"]).then_inc(S.consts, 16)
                sp.dma_start(ct[:, :, :], a["c_t"]).then_inc(S.c, 16)
                sp.dma_start(xT[:, :, :], a["x_t"]).then_inc(S.x, 16)

                def load(g, slot):
                    sp.dma_start(wada[:, slot], w_ada_v[:, :, bass.ds(g * NBANK, NBANK)]).then_inc(s_wada[slot], 16)

                load(0, 0)
                load(1, 1)
                with sp.Fori(1, NGA // 2) as i:
                    for s in range(2):
                        sp.wait_ge(S.mm, i * 2 + (s - 1))
                        load(i * 2 + s, s)

            @block.scalar
            def _(act):
                ch = Chain(act, W.act_steps, act_total)
                act.wait_ge(S.c, 16)
                act.activation(cs[:, :, :], ct[:, :, :], ACT.Silu).then_inc(S.silu, 1)
                act.wait_ge(S.x, 16)
                for k in range(KT):
                    if k >= 2:
                        act.wait_ge(S.sqpe, k - 1)
                    act.activation(sq[:, k % 2, :], xT[:, k, :], ACT.Square).then_inc(S.sq, 1)
                act.wait_ge(S.eps, 1)
                act.wait_ge(S.stat, 1)
                for th in range(2):
                    ch(act.activation(rB[:, th * HT:(th + 1) * HT], dps[:, th, 0:HT], ACT.Ln, bias=eps[:, :],
                                      scale=1.0 / D))
                ch(act.activation(rB[:, :], rB[:, :], ACT.Exp, scale=-0.5))

            @block.tensor
            def _(pe):
                pe.wait_ge(S.ones, 1)
                for k in range(KT):
                    pe.wait_ge(S.sq, k + 1)
                    for th in range(2):
                        m = pe.matmul(dps[:, th, 0:HT], ones[:, :], sq[:, k % 2, th * HT:(th + 1) * HT],
                                      start=(k == 0), stop=(k == KT - 1))
                    m.then_inc(S.sqpe, 1)
                pe.matmul(dps[:, 3, 0:1], ones[:, :], ones[:, 0:1], start=True, stop=True).then_inc(S.stat, 1)
                pe.wait_ge(S.silu, 1)
                pe.wait_ge(S.consts, 32)

                def products(g, slot, half):
                    pe.wait_ge(s_wada[slot], half)
                    if not (isinstance(g, int) and g < 2):
                        pe.wait_ge(S.rows, g - 1)
                    for k in range(KT):
                        m = pe.matmul(gps[0:NC, slot, :], cs[:, k, :], wada[:, slot, k, :],
                                      start=(k == 0), stop=(k == KT - 1))
                    m.then_inc(S.mm, 1)

                def turn(g, slot):
                    pe.wait_ge(S.rows, g + 1)
                    if not (isinstance(g, int) and g < 2):
                        pe.wait_ge(S.added, g - 1)
                    for c in range(4):
                        m = pe.transpose(gps[:, 2 + slot, c * P:(c + 1) * P],
                                         arow[:, slot, c * P:(c + 1) * P], ident)
                    m.then_inc(S.tr, 1)

                products(0, 0, 16)
                products(1, 1, 16)
                turn(0, 0)
                with pe.Fori(1, NGA // 2) as i:
                    products(i * 2, 0, i * 16 + 16)
                    turn(i * 2 - 1, 1)
                    products(i * 2 + 1, 1, i * 16 + 16)
                    turn(i * 2, 0)
                turn(NGA - 1, 1)

            @block.vector
            def _(dve):
                dve.memset(ones[:, :], 1.0).then_inc(S.ones, 1)
                dve.memset(eps[:, :], EPS).then_inc(S.eps, 1)
                dve.memset(arow[:, :, :], 0.0).then_inc(S.zero, 1)
                dve.wait_ge(S.zero, 1)
                dve.wait_ge(S.consts, 32)

                def copy_row(g, slot):
                    dve.wait_ge(S.mm, g + 1)
                    if not (isinstance(g, int) and g < 2):
                        dve.wait_ge(S.tr, g - 1)
                    dve.tensor_copy(arow[0:NC, slot, :], gps[0:NC, slot, :]).then_inc(S.rows, 1)

                def add_bias(g, slot):
                    dve.wait_ge(S.tr, g + 1)
                    turned = gps[:, 2 + slot, :].rearrange("p (c n) -> p c n", n=P)[:, :, 0:NC]
                    dve.tensor_tensor(modT[:, bass.ds(g * 4, 4), :], turned,
                                      bc(bada[:, bass.ds(g * 4, 4)].unsqueeze(2), [P, 4, NC]),
                                      ALU.add).then_inc(S.added, 1)

                copy_row(0, 0)
                copy_row(1, 1)
                add_bias(0, 0)
                with dve.Fori(1, NGA // 2) as i:
                    copy_row(i * 2, 0)
                    add_bias(i * 2 - 1, 1)
                    copy_row(i * 2 + 1, 1)
                    add_bias(i * 2, 0)
                add_bias(NGA - 1, 1)
                dve.wait_ge(S.added, NGA)

        M = Sems()
        M.h, M.hi, M.lo = sems(stack, "mod_h", "mod_hi", "mod_lo")

        def modulate(before, src, rstd, amod, tmp, weight, shift, scale):
            with nc.Block() as block:
                @block.vector
                def _(dve):
                    ch = Chain(dve, W.dve_steps, dve_total)
                    ch(dve.tensor_scalar(amod[:, :, :], modT[:, scale:scale + KT, :], 1.0, None, ALU.add))
                    ch(dve.tensor_tensor(amod[:, :, :], amod[:, :, :],
                                         bc(weight.unsqueeze(2), [P, KT, NC]), ALU.mult))
                    for k in range(KT):
                        t = tmp[:, k % 2, :]
                        if k >= 2:
                            dve.wait_ge(M.lo, before + k - 1)
                        ch(dve.tensor_tensor(t, src[:, k, :], rstd[:, :], ALU.mult))
                        ch(dve.tensor_tensor(samples(t), samples(t),
                                             bc(amod[:, k, 1:NC].unsqueeze(2), [P, NB, NS]), ALU.mult))
                        ch(dve.tensor_tensor(samples(t), samples(t),
                                             bc(modT[:, shift + k, 1:NC].unsqueeze(2), [P, NB, NS]), ALU.add))
                        dve.tensor_scalar(t[:, 0:TP], t[:, 0:TP], amod[:, k, 0:1],
                                          modT[:, shift + k, 0:1], ALU.mult, ALU.add).then_inc(M.h, 1)

                @block.scalar
                def _(act):
                    for k in range(KT):
                        act.wait_ge(M.h, before + k + 1)
                        act.copy(act_hi[:, k, :], tmp[:, k % 2, :]).then_inc(M.hi, 1)

                @block.gpsimd
                def _(pool):
                    for k in range(KT):
                        pool.wait_ge(M.hi, before + k + 1)
                        pool.tensor_tensor(act_lo[:, k, :], tmp[:, k % 2, :], act_hi[:, k, :].bitcast(F32),
                                           ALU.subtract).then_inc(M.lo, 1)

        modulate(0, xT, rB, amod, tmp, normw[0], 0, KT)
        ctx0.close()

        at2 = [after]
        gcol = sb("gcol", [P, H, NTT], at=at2)
        sp16 = sb("sp16", [P, H], at=at2)
        p3at = at2[0]
        with ExitStack() as c2:
            S = Sems()
            S.in_, S.mm, S.beta, S.araw, S.ea = sems(c2, "p2_in_", "p2_mm", "p2_beta", "p2_araw", "p2_ea")
            S.el, S.eg, S.rows, S.out, S.tr = sems(c2, "p2_el", "p2_eg", "p2_rows", "p2_out", "p2_tr")
            S.gsummed, S.alog, S.edl = sems(c2, "p2_gsummed", "p2_alog", "p2_edl")
            lam = sb("lam", [P, H], at=at2)
            headv = sb("headv", [P, 2], at=at2)
            big = [sb(f"big{n}", [P, T], at=at2) for n in range(6)]
            small = [sb(f"small{n}", [P, H], at=at2) for n in range(5)]
            rowT = sb("rowT", [P, 4, T], at=at2)
            with nc.Block() as block:
                @block.sync
                def _(sp):
                    sp.dma_start(lam[:, :], a["lam_t"]).then_inc(S.in_, 16)
                    sp.dma_start(headv[0:H, :], a["head_v"]).then_inc(S.in_, 16)
                    for n in range(2):
                        load_half(sp, a["w_ba"][n], Nth(n))
                    sp.wait_ge(S.rows, 1)
                    sp.dma_start(rowsD, rowT[0:H, :, :]).then_inc(S.out, 16)
                    sp.wait_ge(S.out, 16)

                @block.gpsimd
                def _(pool):
                    for n in range(2):
                        split_lo(pool, Nth(n))

                @block.tensor
                def _(pe):
                    for n in range(2):
                        m = gemm_part(pe, Nth(n), n, 0, 0, 8)
                    pe.matmul(dps[:, 3, 0:1], ones[:, :], ones[:, 0:1], start=True, stop=True).then_inc(S.mm, 1)
                    pe.wait_ge(S.gsummed, 1)
                    for t in range(NTT):
                        n = min(CH, T - t * CH)
                        m = pe.transpose(dps[0:n, 0, t * H:(t + 1) * H], rowT[0:H, 0, t * CH:t * CH + n],
                                         const[0:H, 0:H])
                    m.then_inc(S.tr, 1)

                @block.scalar
                def _(act):
                    ch = Chain(act, W.act_steps, act_total)
                    act.wait_ge(S.in_, 32)
                    for n in range(2):
                        split_hi(act, Nth(n))
                    act.activation(headv[0:H, 0:1], headv[0:H, 0:1], ACT.Exp).then_inc(S.alog, 1)
                    ch(act.activation(small[0][:, :], lam[:, :], ACT.Abs))
                    act.activation(small[0][:, :], small[0][:, :], ACT.Exp, scale=-1.0).then_inc(S.el, 1)
                    act.wait_ge(S.mm, 1)
                    for th in range(2):
                        cols = slice(th * HT, (th + 1) * HT)
                        act.activation(rowT[0:H, 1, cols], gps[0:H, th, 0:HT], ACT.Sigmoid).then_inc(S.beta, 1)
                        act.copy(big[0][0:H, cols], gps[32:32 + H, th, 0:HT]).then_inc(S.araw, 1)
                    act.wait_ge(S.ea, 1)
                    ch(act.activation(big[1][0:H, :], big[0][0:H, :], ACT.Abs))
                    act.activation(big[1][0:H, :], big[1][0:H, :], ACT.Exp, scale=-1.0).then_inc(S.ea, 1)
                    act.wait_ge(S.gsummed, 1)
                    act.activation(rowT[0:H, 2, :], rowT[0:H, 0, :], ACT.Exp).then_inc(S.eg, 1)
                    act.wait_ge(S.edl, 1)
                    ch(act.activation(rowT[0:H, 3, :], rowT[0:H, 3, :], ACT.Exp))
                    act.wait_ge(S.eg, 1)
                    act.wait_ge(S.beta, 2)
                    act.activation(big[5][0:H, 0:1], rowT[0:H, 3, 0:1], ACT.Copy).then_inc(S.rows, 1)

                @block.vector
                def _(dve):
                    ch = Chain(dve, W.dve_steps, dve_total)

                    def log1p(e, s, s2, p, out):
                        ch(dve.tensor_scalar(s, e, 2.0, None, ALU.add))
                        ch(dve.reciprocal(s, s))
                        ch(dve.tensor_tensor(s, s, e, ALU.mult))
                        ch(dve.tensor_tensor(s2, s, s, ALU.mult))
                        ch(dve.tensor_scalar(p, s2, 1.0 / 17, None, ALU.mult))
                        for n in range(15, 1, -2):
                            ch(dve.scalar_tensor_tensor(p, p, 1.0 / n, s2, ALU.add, ALU.mult))
                        ch(dve.scalar_tensor_tensor(p, p, 1.0, s, ALU.add, ALU.mult))
                        ch(dve.tensor_scalar(out, p, 2.0, None, ALU.mult))

                    dve.wait_ge(S.in_, 32)
                    dve.wait_ge(S.el, 1)
                    s = [t[:, :] for t in small]
                    log1p(s[0], s[1], s[2], s[3], s[4])
                    ch(dve.tensor_scalar(s[1], lam[:, :], -1.0, 0.0, ALU.mult, ALU.max))
                    ch(dve.tensor_tensor(s[1], s[1], s[4], ALU.add))
                    ch(dve.tensor_scalar(sp16[:, :], s[1], 16.0, None, ALU.mult))
                    dve.wait_ge(S.araw, 2)
                    b = [t[0:H, :] for t in big]
                    dve.tensor_scalar(b[0], b[0], headv[0:H, 1:2], None, ALU.add).then_inc(S.ea, 1)
                    dve.wait_ge(S.ea, 2)
                    log1p(b[1], b[2], b[3], b[4], b[5])
                    ch(dve.scalar_tensor_tensor(b[1], b[0], 0.0, b[5], ALU.max, ALU.add))
                    dve.wait_ge(S.alog, 1)
                    ch(dve.tensor_scalar(b[1], b[1], headv[0:H, 0:1], -1.0, ALU.mult, ALU.mult))
                    ch(dve.memset(b[2], 1.0))
                    ch(dve.memset(b[2][:, 0:TP].rearrange("p (c t) -> p c t", t=CH)[:, :, 0:1], 0.0))
                    ch(dve.memset(samples(b[2])[:, :, 0:1], 0.0))
                    dve.tensor_tensor_scan(rowT[0:H, 0, :], b[2], b[1], 0.0, ALU.mult, ALU.add).then_inc(S.gsummed, 1)
                    dve.wait_ge(S.gsummed, 1)
                    for src, out, w in ((rowT[0:H, 0, 0:TP], rowT[0:H, 3, 0:TP], CH),
                                        (rowT[0:H, 0, TP:T], rowT[0:H, 3, TP:T], NS)):
                        v = src.rearrange("p (c t) -> p c t", t=w)
                        ch(dve.tensor_tensor(out.rearrange("p (c t) -> p c t", t=w),
                                             bc(v[:, :, w - 1:w], v.shape), v, ALU.subtract))
                    dve.engine_nop().then_inc(S.edl, 1)
                    dve.wait_ge(S.tr, 1)
                    ch(dve.memset(gcol[:, :, :], 0.0))
                    ch(dve.tensor_copy(gcol[:, :, 0:NCH].rearrange("p h t -> p t h"),
                                       dps[:, 0, 0:NCH * H].rearrange("p (t h) -> p t h", h=H)))
                    ch(dve.tensor_copy(gcol[0:TS, :, NCH], dps[0:TS, 0, NCH * H:NTT * H]))

        at3 = [p3at]
        rows = sb("rows", [P, 4, T], at=at3)
        pack = sb("pack", [P, PACK], at=at3)
        pads = sb("pads", [P, 2, PADW], at=at3)
        qkvz = sb("qkvz", [P, 4, T], at=at3)
        gy = sb("gy", [P, T], at=at3)
        xc, ry, iu, la, e2, em = (sb(n, [P, PADW], at=at3) for n in ("xc", "ry", "iu", "la", "e2", "em"))
        convs = sb("convs", [P, 4, NC, PL], at=at3)
        hlast = sb("hlast", [P, NC], at=at3)
        sqs = sb("sqs", [P, 2, T], at=at3)
        kb = sb("kb", [P, T], at=at3)
        nkeg = sb("nkeg", [P, T], at=at3)
        qg = sb("qg", [P, T], at=at3)
        kgd = sb("kgd", [P, T], at=at3)
        nkq = sb("nkq", [P, NB, 2, NS], at=at3)
        eglast = sb("eglast", [P, NCH + NB], at=at3)
        dec = sb("dec", [P, NCH + 1, CH], at=at3)
        lt = sb("lt", [P, T], at=at3)
        att = sb("att", [P, T], at=at3)
        ktok = sb("ktok", [P, NTT, P], at=at3)
        tm = sb("tm", [P, T], at=at3)
        qm = sb("qm", [P, T], at=at3)
        um = sb("um", [P, NTT * P], at=at3)
        vmask = sb("vmask", [P, NB, P], at=at3)
        st = sb("st", [P, P], at=at3)
        sst = sb("sst", [P, NB, P], at=at3)
        rs = sb("rs", [P, 2, P], at=at3)
        vn = sb("vn", [P, 2, P], at=at3)
        rst = sb("rst", [P, P], at=at3)
        qc, kc, vc, zc = (qkvz[:, n, :] for n in range(4))
        lmask = dec

        TILE = "xyqkvz"
        with ExitStack() as c3:
            S = Sems()
            S.pack, S.evx, S.convx, S.gr, S.gi = sems(c3, "p3_pack", "p3_evx", "p3_convx", "p3_gr", "p3_gi")
            S.sigr, S.sigi, S.gely, S.lruexp, S.ydone = \
                sems(c3, "p3_sigr", "p3_sigi", "p3_gely", "p3_lruexp", "p3_ydone")
            S.emdone, S.sqrt, S.scan, S.lruout, S.lrust = \
                sems(c3, "p3_emdone", "p3_sqrt", "p3_scan", "p3_lruout", "p3_lrust")
            S.evq, S.evk, S.evv, S.evz, S.cvq = sems(c3, "p3_evq", "p3_evk", "p3_evv", "p3_evz", "p3_cvq")
            S.cvk, S.cvv, S.slq, S.slk, S.slv = sems(c3, "p3_cvk", "p3_cvv", "p3_slq", "p3_slk", "p3_slv")
            S.rowsl, S.sq, S.nrm, S.invn, S.prod = sems(c3, "p3_rowsl", "p3_sq", "p3_nrm", "p3_invn", "p3_prod")
            S.gram, S.mind, S.expd, S.ktk, S.uinit = sems(c3, "p3_gram", "p3_mind", "p3_expd", "p3_ktk", "p3_uinit")
            S.tini, S.tcop, S.lm, S.qlev, S.qcop = sems(c3, "p3_tini", "p3_tcop", "p3_lm", "p3_qlev", "p3_qcop")
            S.dlev, S.upd, S.xs, S.rts, S.rtt = sems(c3, "p3_dlev", "p3_upd", "p3_xs", "p3_rts", "p3_rtt")
            S.rcs, S.vsm, S.vms, S.ats, S.oss = sems(c3, "p3_rcs", "p3_vsm", "p3_vms", "p3_ats", "p3_oss")
            S.dss0, S.dss1, S.sup0, S.sup1, S.rp = sems(c3, "p3_dss0", "p3_dss1", "p3_sup0", "p3_sup1", "p3_rp")
            S.rcp, S.vp, S.vcp, S.op, S.sup = sems(c3, "p3_rcp", "p3_vp", "p3_vcp", "p3_op", "p3_sup")
            S.ocp, S.osq, S.onrm, S.oinv, S.oout = sems(c3, "p3_ocp", "p3_osq", "p3_onrm", "p3_oinv", "p3_oout")
            S.sload, S.stcl, S.o_out, S.st_out, S.sst_out = \
                sems(c3, "p3_sload", "p3_stcl", "p3_o_out", "p3_st_out", "p3_sst_out")
            S.conv_out, = sems(c3, "p3_conv_out")
            NL = LEVELS - 1
            SLOTS = 48

            def do_turns(eng, body, sem=None, total=None, steps=0):
                ch = Chain(eng, sem, total or [0])
                body(0, None, ch)
                with eng.Fori(1, H - 1) as i:
                    ch.enter(i - 1, steps)
                    body(i, i - 1, ch)
                ch.leave(H - 2)
                body(H - 1, H - 2, ch)
                body(None, H - 1, ch)

            def head_half(h, j):
                return Nth(2 + 12 * h + j) if isinstance(h, int) else Nth(2 + j, h, 12)

            packD = a["pack"]

            with nc.Block() as block:
                @block.sync
                def _(sp):
                    def body(h, g, ch):
                        A, B = h is not None, g is not None
                        for j in range(12):
                            if j == 2 and A:
                                if not isinstance(h, int) or h:
                                    sp.wait_ge(S.cvv, h)
                                    sp.wait_ge(S.scan, h)
                                sp.dma_start(pack[:, :], row(a["pack"], h)).then_inc(S.pack, 16)
                            if j == 1 and B:
                                sp.wait_ge(S.sst_out, g * 16 + 16)
                                sp.dma_start(sst[:, :, :], a["dn_s"][:, bass.ds(g, 1)].rearrange(
                                    "b h p v -> p (b h) v")).then_inc(S.sload, 16)
                            if A:
                                load_half(sp, row(a["w_in"], h * 12 + j), head_half(h, j))
                            if j == 9 and A:
                                sp.wait_ge(S.lruout, h + 1)
                                sp.dma_start(row(mixD, h), gy[:, :]).then_inc(S.lrust, 16)
                                sp.dma_start(row(a["lru_h_t"], h), hlast[:, :]).then_inc(S.lrust, 16)
                                if B:
                                    sp.wait_ge(S.prod, g + 1)
                                r = rowsD[h:h + 1] if isinstance(h, int) else rowsD[bass.ds(h, 1)]
                                sp.dma_start(rows[:, :, :].rearrange("p r t -> p (r t)"),
                                             r.rearrange("h r t -> h (r t)").broadcast_to([P, 4 * T])
                                             ).then_inc(S.rowsl, 16)

                    do_turns(sp, body)

                @block.gpsimd
                def _(pool):
                    def body(h, g, ch):
                        if h is not None:
                            for j in range(12):
                                split_lo(pool, head_half(h, j))

                    do_turns(pool, body)

                @block.tensor
                def _(pe):
                    def body(h, g, ch):
                        A, B = h is not None, g is not None

                        for e in range(SLOTS):
                            tile, part = e // 8, e % 8
                            pair = tile % 2
                            if A:
                                if part == 0:
                                    if tile < 2:
                                        if not isinstance(h, int) or h:
                                            pe.wait_ge((S.evv, S.evz)[tile], h)
                                    else:
                                        pe.wait_ge((S.sigr, S.sigi, S.evq, S.evk)[tile - 2], h + 1)
                                gemm_part(pe, head_half(h, tile * 2 + part // 4), part // 4, pair, part % 4 * 2, 2)
                            if e == 1 and B:
                                pe.wait_ge(S.sq, g + 1)
                                for n in range(2):
                                    for th in range(2):
                                        m = pe.matmul(dps[:, 2 * n + th, 0:HT], ones[:, :],
                                                      sqs[:, n, th * HT:(th + 1) * HT], start=True, stop=True)
                                m.then_inc(S.nrm, 1)
                            if e == 7 and B:
                                pe.wait_ge(S.prod, g + 1)
                                for t in range(NTT):
                                    n = CH if t < NCH else TS
                                    c = slice(t * CH, t * CH + n)
                                    o = (dps[:, 0, c], dps[:, 1, c], dps[:, 3, c]) if t < NCH else (
                                        dps[0:TS, 2, 0:TS], dps[0:TS, 2, TS:2 * TS], dps[0:TS, 2, 2 * TS:2 * TS + P])
                                    pe.matmul(o[0], kc[:, c], kb[:, c], start=True, stop=True)
                                    pe.matmul(o[1], kc[:, c], qc[:, c], start=True, stop=True)
                                    m = pe.transpose(o[2], kgd[:, c], ident)
                                m.then_inc(S.gram, 1)
                            if e == 12 and A:
                                pe.wait_ge(S.convx, h + 1)
                                pe.wait_ge(S.evx, h + 1)
                                for th in range(2):
                                    m = pe.matmul(gps[:, th, 0:CONVW // 2], pack[:, 116:244],
                                                  xc[:, th * (CONVW // 2):(th + 1) * (CONVW // 2)], start=True, stop=True)
                                m.then_inc(S.gr, 1)
                            if e == 12 and B:
                                pe.wait_ge(S.uinit, g + 1)
                                pe.wait_ge(S.ktk, g + 1)
                                for t in range(NCH):
                                    c = slice(t * CH, (t + 1) * CH)
                                    pe.transpose(dps[:, 0, c], um[:, c], ident)
                                pe.transpose(dps[0:TS, 3, 0:TS], um[0:TS, TP:T], const[0:TS, 0:TS]).then_inc(S.tini, 1)
                            if e == 13 and B:
                                pe.wait_ge(S.sload, g * 16 + 16)
                                pe.wait_ge(S.tcop, g + 1)
                                for b in range(NB):
                                    m = pe.matmul(dps[:, 3, 192 + b * 16:192 + (b + 1) * 16], sst[:, b, :],
                                                  nkq[:, b, :, :], start=True, stop=True)
                                m.then_inc(S.xs, 1)
                            for l in range(1, LEVELS):
                                if e == 12 + 3 * (l - 1) + 2 and B:
                                    pe.wait_ge(S.lm, g * (LEVELS - 1) + l)
                                    if l == 1:
                                        pe.wait_ge(S.rts, g + 1)
                                    else:
                                        pe.wait_ge(S.upd, g * (LEVELS - 1) + l - 1)
                                    for t in range(NCH + (l < 3)):
                                        n, c = (CH, slice(t * CH, (t + 1) * CH)) if t < NCH else (TS, slice(TP, T))
                                        o = dps[:, 0, c] if t < NCH else dps[0:TS, 3, 0:TS]
                                        m = pe.matmul(o, lmask[0:n, t, 0:n], tm[0:n, c], start=True, stop=True)
                                    m.then_inc(S.qlev, 1)
                                if e == 12 + 3 * (l - 1) + 3 and B:
                                    pe.wait_ge(S.qcop, g * (LEVELS - 1) + l)
                                    for t in range(NCH + (l < 3)):
                                        n, c = (CH, slice(t * CH, (t + 1) * CH)) if t < NCH else (TS, slice(TP, T))
                                        o = (dps[:, 1, c], dps[:, 2, c]) if t < NCH else (
                                            dps[0:TS, 3, TS:2 * TS], dps[0:TS, 3, 2 * TS:3 * TS])
                                        if l < LEVELS - 1:
                                            pe.matmul(o[0], um[0:n, c], qm[0:n, c], start=True, stop=True)
                                        m = pe.matmul(o[1], qm[0:n, c], um[0:n, c], start=True, stop=True)
                                    m.then_inc(S.dlev, 1)
                            if e == 18 and A:
                                pe.wait_ge(S.gely, h + 1)
                                for th in range(2):
                                    m = pe.matmul(gps[:, 2 + th, 0:CONVW // 2], pack[:, 244:372],
                                                  xc[:, th * (CONVW // 2):(th + 1) * (CONVW // 2)], start=True, stop=True)
                                m.then_inc(S.gi, 1)
                            if e == 19 and B:
                                pe.wait_ge(S.upd, g * NL + 2)
                                pe.transpose(dps[:, 3, 320:320 + P], rst[:, :], ident).then_inc(S.rtt, 1)
                            if e == 22 and B:
                                pe.wait_ge(S.rcs, g + 1)
                                pe.wait_ge(S.upd, g * (LEVELS - 1) + 2)
                                pe.matmul(dps[:, 3, 192:192 + P], um[0:TS, TP:TP + P], rs[0:TS, 1, :], start=True,
                                          stop=True).then_inc(S.vsm, 1)
                            if e == 25 and B:
                                pe.wait_ge(S.vms, g + 1)
                                pe.matmul(dps[:, 3, 448:512], vn[0:TS, 1, :], att[0:TS, TP:T], start=True,
                                          stop=True).then_inc(S.ats, 1)
                            for t in range(NCH):
                                if e == 31 + 4 * t and B:
                                    c = slice(t * CH, (t + 1) * CH)
                                    pe.matmul(dps[:, 0, 0:P], vc[:, c], ident, start=True, stop=False)
                                    pe.wait_ge(S.stcl if t == 0 else S.sup, g + 1 if t == 0 else g * NCH + t)
                                    pe.matmul(dps[:, 0, 0:P], nkeg[:, c], st[:, :], start=False,
                                              stop=True).then_inc(S.rp, 1)
                                if e == 32 + 4 * t and B:
                                    pe.wait_ge(S.rcp, g * NCH + t + 1)
                                    c = slice(t * CH, (t + 1) * CH)
                                    if t == 0:
                                        pe.wait_ge(S.upd, g * (LEVELS - 1) + LEVELS - 1)
                                    pe.matmul(dps[:, 1, 0:P], um[:, c], rs[:, 0, :], start=True,
                                              stop=True).then_inc(S.vp, 1)
                                if e == 33 + 4 * t and B:
                                    pe.wait_ge(S.vcp, g * NCH + t + 1)
                                    c = slice(t * CH, (t + 1) * CH)
                                    pe.matmul(dps[:, 2, c], st[:, :], qg[:, c], start=True, stop=False)
                                    pe.matmul(dps[:, 2, c], vn[:, 0, :], att[:, c], start=False, stop=True)
                                    if t == 0:
                                        pe.wait_ge(S.sup1, g + 1)
                                    pe.matmul(dps[:, 3, 0:P], ktok[:, t, :], vn[:, 0, :], start=True,
                                              stop=True).then_inc(S.op, 1)
                            for n, e_n in ((0, 27), (1, 29)):
                                if e == e_n and B:
                                    if n == 0:
                                        pe.wait_ge(S.oss, g + 1)
                                    else:
                                        pe.wait_ge(S.sup0, g + 1)
                                    pe.matmul(dps[:, 3, :], ktok[0:TS, NCH, :], vmask[0:TS, n * 4:n * 4 + 4, :],
                                              start=True, stop=True).then_inc((S.dss0, S.dss1)[n], 1)
                            if e == 46 and B:
                                pe.wait_ge(S.osq, g + 1)
                                pe.wait_ge(S.sup, g * NCH + NCH)
                                for th in range(2):
                                    m = pe.matmul(dps[:, th, 0:HT], ones[:, :], sqs[:, 0, th * HT:(th + 1) * HT],
                                                  start=True, stop=True)
                                m.then_inc(S.onrm, 1)

                    do_turns(pe, body)

                @block.scalar
                def _(act):
                    def split(h, j):
                        split_hi(act, head_half(h, j))

                    def body(h, g, ch):
                        A, B = h is not None, g is not None
                        later = not isinstance(h, int) or h > 0
                        last = isinstance(h, int) and h == H - 1

                        def tile_done(tile):
                            act.wait_ge(W.used, head_half(h, 2 * tile + 1).n + 1)

                        def evacuate(tile, n, before, done):
                            tile_done(tile)
                            if before is not None:
                                act.wait_ge(*before)
                            pr = 2 * (tile % 2)
                            ch(act.copy(pads[:, n, PL:PL + HT], gps[:, pr, 0:HT]))
                            ch(act.copy(pads[:, n, PL + HT:PL + TP], gps[:, pr + 1, 0:TP - HT]))
                            act.copy(padded(pads[:, n, :], PL, NS),
                                     gps[:, pr + 1, TP - HT:HT].rearrange("p (b s) -> p b s", b=NB)).then_inc(done, 1)

                        def silu(src, n, conv, done):
                            act.wait_ge(conv, h + 1)
                            if B:
                                act.wait_ge(S.gram if n < 2 else S.rp, g + 1 if n < 2 else g * NCH + NCH)
                            ch(act.activation(qkvz[:, n, 0:TP], src[:, 0:TP], ACT.Silu))
                            act.activation(samples(qkvz[:, n, :]), padded(src, 0, NS), ACT.Silu).then_inc(done, 1)

                        if A and not later:
                            split(0, 0)
                            split(0, 1)
                        for e in range(SLOTS):
                            if A and e % 4 == 0 and not (last and e >= 40):
                                split(h, e // 4 + 2)
                            if e == 0 and B:
                                ch(act.activation(sqs[:, 0, :], qc, ACT.Square))
                                act.activation(sqs[:, 1, :], kc, ACT.Square).then_inc(S.sq, 1)
                            if e == 2 and B:
                                act.wait_ge(S.nrm, g + 1)
                                for n in range(2):
                                    for th in range(2):
                                        ch(act.activation(sqs[:, n, th * HT:(th + 1) * HT], dps[:, 2 * n + th, 0:HT],
                                                          ACT.Ln, bias=eps[:, :]))
                                act.activation(sqs[:, :, :], sqs[:, :, :], ACT.Exp, scale=-0.5).then_inc(S.invn, 1)
                            if e == 6 and B:
                                act.wait_ge(S.mind, g + 1)
                                ch(act.activation(dec[:, 0:NCH, :], dec[:, 0:NCH, :], ACT.Exp))
                                act.activation(dec[0:TS, NCH, 0:TS], dec[0:TS, NCH, 0:TS], ACT.Exp).then_inc(S.expd, 1)
                            if e == 8 and A:
                                evacuate(0, 0, (S.cvk, h) if later else None, S.evx)
                            if e == 9 and B:
                                act.wait_ge(S.gram, g + 1)
                                act.copy(ktok[:, 0:NCH, :], dps[:, 3, :].rearrange("p (t d) -> p t d", d=P)
                                         ).then_inc(S.ktk, 1)
                            if e == 12 and B:
                                act.wait_ge(S.tini, g + 1)
                                ch(act.copy(tm[:, 0:TP], dps[:, 0, :]))
                                act.copy(tm[0:TS, TP:T], dps[0:TS, 3, 0:TS]).then_inc(S.tcop, 1)
                            if e == 13 and A:
                                act.wait_ge(S.gr, h + 1)
                                if later:
                                    act.wait_ge(S.lruout, h)
                                for th in range(2):
                                    c = slice(th * (CONVW // 2), (th + 1) * (CONVW // 2))
                                    m = act.activation(ry[:, c], gps[:, th, 0:CONVW // 2], ACT.Sigmoid, bias=pack[:, 17:18])
                                    if th == 0:
                                        ch(m)
                                m.then_inc(S.sigr, 1)
                            for l in range(1, LEVELS):
                                if e == 11 + 3 * l and B:
                                    act.wait_ge(S.qlev, g * NL + l)
                                    if l < 3:
                                        ch(act.copy(qm[0:TS, TP:T], dps[0:TS, 3, 0:TS]))
                                    act.copy(qm[:, 0:TP], dps[:, 0, :]).then_inc(S.qcop, 1)
                            if e == 16 and A:
                                tile_done(1)
                                if later:
                                    act.wait_ge(S.lrust, h * 32)
                                ch(act.activation(gy[:, 0:HT], gps[:, 2, 0:HT], ACT.Gelu_apprx_tanh))
                                act.activation(gy[:, HT:T], gps[:, 3, 0:HT], ACT.Gelu_apprx_tanh).then_inc(S.gely, 1)
                            if e == 15 and A:
                                act.wait_ge(S.ydone, h + 1)
                                ch(act.activation(la[:, 0:CONVW], ry[:, 0:CONVW], ACT.Exp, scale=-0.5))
                                act.activation(e2[:, 0:CONVW], ry[:, 0:CONVW], ACT.Exp, scale=-1.0).then_inc(S.lruexp, 1)
                            if e == 19 and A:
                                act.wait_ge(S.emdone, h + 1)
                                act.activation(em[:, 0:CONVW], em[:, 0:CONVW], ACT.Sqrt).then_inc(S.sqrt, 1)
                                act.wait_ge(S.gi, h + 1)
                                for th in range(2):
                                    c = slice(th * (CONVW // 2), (th + 1) * (CONVW // 2))
                                    m = act.activation(iu[:, c], gps[:, 2 + th, 0:CONVW // 2], ACT.Sigmoid,
                                                       bias=pack[:, 18:19])
                                    if th == 0:
                                        ch(m)
                                m.then_inc(S.sigi, 1)
                            if e == 20 and B:
                                act.wait_ge(S.rtt, g + 1)
                                act.copy(rs[0:TS, 1, :], dps[0:TS, 3, 320:320 + P]).then_inc(S.rcs, 1)
                            if e == 24 and A:
                                evacuate(2, 1, (S.cvv, h) if later else None, S.evq)
                            if e == 28 and A:
                                silu(e2, 0, S.cvq, S.slq)
                            if e == 32 and A:
                                evacuate(3, 0, (S.convx, h + 1), S.evk)
                            if e == 37 and A:
                                silu(em, 1, S.cvk, S.slk)
                            if e == 40 and A:
                                evacuate(4, 1, (S.cvq, h + 1), S.evv)
                            for t in range(NCH):
                                if e == 31 + 4 * t and B:
                                    act.wait_ge(S.rp, g * NCH + t + 1)
                                    act.copy(rs[:, 0, :], dps[:, 0, 0:P]).then_inc(S.rcp, 1)
                            if e == 31 and B:
                                act.wait_ge(S.sup1, g + 1)
                                act.dma_start(a["s_sample"][:, bass.ds(g, 1)].rearrange("b h p v -> p (b h) v"),
                                              sst[:, :, :]).then_inc(S.sst_out, 16)
                            if e == 45 and B:
                                act.wait_ge(S.op, g * NCH + NCH)
                                act.copy(kb[:, 0:TP], dps[:, 2, :]).then_inc(S.ocp, 1)
                                act.wait_ge(S.ocp, g + 1)
                                act.wait_ge(S.oss, g + 1)
                                act.activation(sqs[:, 0, :], kb[:, :], ACT.Square).then_inc(S.osq, 1)
                            if e == 47 and B:
                                act.wait_ge(S.onrm, g + 1)
                                for th in range(2):
                                    ch(act.activation(sqs[:, 1, th * HT:(th + 1) * HT], dps[:, th, 0:HT], ACT.Ln,
                                                      bias=eps[:, :], scale=1.0 / P))
                                act.activation(sqs[:, 1, :], sqs[:, 1, :], ACT.Exp, scale=-0.5).then_inc(S.oinv, 1)
                            if e == 47 and A:
                                silu(e2, 2, S.cvv, S.slv)
                        if B:
                            act.wait_ge(S.sup, g * NCH + NCH)
                            act.dma_start(row(a["s_prompt"], g), st[:, :]).then_inc(S.st_out, 16)
                            act.wait_ge(S.oout, g + 1)
                            out = mixD[H + g] if isinstance(g, int) else row(mixD, g + H)
                            act.dma_start(out, kb[:, :]).then_inc(S.o_out, 16)
                        if A:
                            act.wait_ge(S.cvv, h + 1)
                            act.dma_start(row(a["conv_t"], h), convs[:, :, :, :].rearrange("p a b c -> p (a b c)")
                                          ).then_inc(S.conv_out, 16)
                            tile_done(5)
                            ch(act.activation(zc[:, 0:HT], gps[:, 2, 0:HT], ACT.Silu))
                            act.activation(zc[:, HT:T], gps[:, 3, 0:HT], ACT.Silu).then_inc(S.evz, 1)

                    do_turns(act, body, W.act_steps, act_total, ACT_STEPS_A_TURN)
                    act.wait_ge(S.lrust, 32 * H)
                    act.wait_ge(S.st_out, 16 * H + 16)
                    act.wait_ge(S.o_out, 16 * H + 16)
                    act.wait_ge(S.sst_out, 16 * H + 16)
                    act.wait_ge(S.conv_out, 16 * H)

                @block.vector
                def _(dve):
                    tt, ts, stt = dve.tensor_tensor, dve.tensor_scalar, dve.scalar_tensor_tensor
                    for s_ in (S.o_out, S.st_out, S.sst_out):
                        dve.engine_nop().then_inc(s_, 16)

                    def tiles4(ap):
                        return ap.rearrange("p (t i) -> p t i", i=CH)

                    def over4(m):
                        return bc(m.unsqueeze(1), [P, NCH, CH])

                    def body(h, g, ch):
                        A, B = h is not None, g is not None
                        later = not isinstance(h, int) or h > 0
                        if A and not later:
                            ch(dve.memset(pads[:, :, 0:PL], 0.0))
                            ch(dve.memset(rst[:, TS:P], 0.0))
                            ch(dve.memset(um[:, T:NTT * P], 0.0))

                        def conv(n, pad, out, ready, done, bias=None):
                            src = pads[:, pad, :]
                            dve.wait_ge(ready, h + 1)
                            if n == 3:
                                dve.wait_ge(S.pack, h * 16 + 16)
                                if later:
                                    dve.wait_ge(S.conv_out, h * 16)
                            ch(dve.tensor_copy(padded(src, 0, PL), pack[:, 20 + n * 24:44 + n * 24].rearrange(
                                "p (b k) -> p b k", k=PL)))
                            ch(dve.tensor_copy(convs[:, n, 0, :], src[:, TP:TP + PL]))
                            ch(dve.tensor_copy(convs[:, n, 1:NC, :], padded(src, NS, PL)))
                            w = [pack[:, n * CW + k:n * CW + k + 1] for k in range(CW)]
                            if bias is None:
                                ch(ts(out[:, 0:CONVW], src[:, 0:CONVW], w[0], None, ALU.mult))
                            else:
                                ch(ts(out[:, 0:CONVW], src[:, 0:CONVW], w[0], bias, ALU.mult, ALU.add))
                            for k in range(1, CW):
                                m = stt(out[:, 0:CONVW], src[:, k:k + CONVW], w[k], out[:, 0:CONVW], ALU.mult, ALU.add)
                                if k < CW - 1:
                                    ch(m)
                            m.then_inc(done, 1)
                            dve.wait_ge(done, h + 1)

                        for e in range(SLOTS):
                            if e == 3 and B:
                                dve.wait_ge(S.rowsl, g * 16 + 16)
                                for t in range(NCH):
                                    ch(ts(dec[:, t, :], rows[:, 0, t * CH:(t + 1) * CH], gcol[:, bass.ds(g, 1), t],
                                          0.0, ALU.subtract, ALU.min))
                                ts(dec[0:TS, NCH, 0:TS], rows[0:TS, 0, TP:T], gcol[0:TS, bass.ds(g, 1), NCH],
                                   0.0, ALU.subtract, ALU.min).then_inc(S.mind, 1)
                                eg = rows[:, 2, :]
                                ch(dve.tensor_copy(eglast[:, 0:NCH], tiles4(eg[:, 0:TP])[:, :, CH - 1]))
                                ch(dve.tensor_copy(eglast[:, NCH:], samples(eg)[:, :, NS - 1]))
                                dve.wait_ge(S.invn, g + 1)
                                dve.wait_ge(S.o_out, g * 16 + 16)
                                ch(tt(kc, kc, sqs[:, 1, :], ALU.mult))
                                ch(stt(qc, qc, float(P) ** -0.5, sqs[:, 0, :], ALU.mult, ALU.mult))
                                ch(tt(kb[:, :], kc, rows[:, 1, :], ALU.mult))
                                ch(tt(vc, vc, rows[:, 1, :], ALU.mult))
                                ch(stt(nkeg[:, :], kb[:, :], -1.0, eg, ALU.mult, ALU.mult))
                                ch(tt(qg[:, :], qc, eg, ALU.mult))
                                ch(dve.tensor_copy(nkq[:, :, 0, :], samples(nkeg)))
                                ch(dve.tensor_copy(nkq[:, :, 1, :], samples(qg)))
                                tt(kgd[:, :], kc, rows[:, 3, :], ALU.mult).then_inc(S.prod, 1)
                                dve.wait_ge(S.prod, g + 1)
                                dve.wait_ge(S.st_out, g * 16 + 16)
                                dve.memset(st[:, :], 0.0).then_inc(S.stcl, 1)
                                dve.wait_ge(S.stcl, g + 1)
                            if e == 7 and B:
                                dve.wait_ge(S.expd, g + 1)
                                ch(tt(dec[:, 0:NCH, :], dec[:, 0:NCH, :], over4(const[:, C_INCL:C_INCL + CH]), ALU.mult))
                                ch(tt(dec[0:TS, NCH, 0:TS], dec[0:TS, NCH, 0:TS], const[0:TS, C_SINCL:C_SINCL + TS],
                                      ALU.mult))
                            if e == 9 and B:
                                dve.wait_ge(S.gram, g + 1)
                                d4, ds_ = dec[:, 0:NCH, :], dec[0:TS, NCH, 0:TS]
                                ch(tt(tiles4(lt[:, 0:TP]), tiles4(dps[:, 0, :]), d4, ALU.mult))
                                ch(tt(tiles4(att[:, 0:TP]), tiles4(dps[:, 1, :]), d4, ALU.mult))
                                ch(tt(lt[0:TS, TP:T], dps[0:TS, 2, 0:TS], ds_, ALU.mult))
                                ch(tt(att[0:TS, TP:T], dps[0:TS, 2, TS:2 * TS], ds_, ALU.mult))
                                ch(dve.tensor_copy(ktok[0:TS, NCH, :], dps[0:TS, 2, 2 * TS:2 * TS + P]))
                                ch(tt(tiles4(um[:, 0:TP]), tiles4(lt[:, 0:TP]), over4(const[:, C_LEVEL:C_LEVEL + P]), ALU.mult))
                                ch(tt(um[0:TS, TP:T], lt[0:TS, TP:T], const[0:TS, C_LEVEL:C_LEVEL + TS], ALU.mult))
                                ch(tt(tiles4(um[:, 0:TP]), over4(ident), tiles4(um[:, 0:TP]), ALU.subtract))
                                tt(um[0:TS, TP:T], const[0:TS, 0:TS], um[0:TS, TP:T], ALU.subtract).then_inc(S.uinit, 1)
                            for l in range(1, LEVELS):
                                if e == 9 + 3 * l and B and l > 1 or e == 9 and B and l == 1:
                                    if l > 1:
                                        dve.wait_ge(S.dlev, g * NL + l - 1)
                                        if l - 1 < 3:
                                            ch(tt(um[0:TS, TP:T], um[0:TS, TP:T], dps[0:TS, 3, 2 * TS:3 * TS], ALU.subtract))
                                            ch(tt(tm[0:TS, TP:T], tm[0:TS, TP:T], dps[0:TS, 3, TS:2 * TS], ALU.subtract))
                                        ch(tt(um[:, 0:TP], um[:, 0:TP], dps[:, 2, :], ALU.subtract))
                                        tt(tm[:, 0:TP], tm[:, 0:TP], dps[:, 1, :], ALU.subtract).then_inc(S.upd, 1)
                                        dve.wait_ge(S.upd, g * NL + l - 1)
                                    m = const[:, C_LEVEL + l * P:C_LEVEL + (l + 1) * P]
                                    if l < 3:
                                        ch(tt(lmask[0:TS, NCH, 0:TS], lt[0:TS, TP:T], m[0:TS, 0:TS], ALU.mult))
                                    tt(lmask[:, 0:NCH, :], tiles4(lt[:, 0:TP]), over4(m), ALU.mult).then_inc(S.lm, 1)
                                    dve.wait_ge(S.lm, g * NL + l)
                            if e == 30 and B:
                                dve.wait_ge(S.dlev, g * NL + NL)
                                tt(um[:, 0:TP], um[:, 0:TP], dps[:, 2, :], ALU.subtract).then_inc(S.upd, 1)
                                dve.wait_ge(S.upd, g * NL + NL)
                            if e == 10 and A:
                                conv(3, 0, xc, S.evx, S.convx, pack[:, 16:17])
                            if e == 13 and A:
                                dve.wait_ge(S.sigr, h + 1)
                                c = slice(0, CONVW)
                                ts(ry[:, c], ry[:, c], sp16[:, bass.ds(h, 1)], None, ALU.mult).then_inc(S.ydone, 1)
                                dve.wait_ge(S.ydone, h + 1)
                            if e == 16 and A:
                                ch(ts(iu[:, c], ry[:, c], 0.25, None, ALU.min))
                                ch(ts(em[:, c], iu[:, c], -1.0 / 720, None, ALU.mult))
                                for f in (120.0, -24.0, 6.0, -2.0, 1.0):
                                    ch(stt(em[:, c], em[:, c], 1.0 / f, iu[:, c], ALU.add, ALU.mult))
                                dve.wait_ge(S.lruexp, h + 1)
                                ch(ts(e2[:, c], e2[:, c], -1.0, 1.0, ALU.mult, ALU.add))
                                ch(stt(e2[:, c], ry[:, c], 0.25, e2[:, c], ALU.is_ge, ALU.mult))
                                tt(em[:, c], em[:, c], e2[:, c], ALU.max).then_inc(S.emdone, 1)
                            if e == 14 and B:
                                dve.wait_ge(S.xs, g + 1)
                                x = dps[:, 3, 192:320].rearrange("p (b k s) -> p b k s", k=2, s=NS)
                                ch(dve.tensor_copy(samples(kb), x[:, :, 1, :]))
                                tt(rst[:, 0:TS].rearrange("p (b s) -> p b s", b=NB), x[:, :, 0, :], samples(vc),
                                   ALU.add).then_inc(S.rts, 1)
                            if e == 22 and A:
                                dve.wait_ge(S.sqrt, h + 1)
                                dve.wait_ge(S.sigi, h + 1)
                                ch(dve.memset(em[:, 0:1], 1.0))
                                ch(tt(iu[:, c], iu[:, c], em[:, c], ALU.mult))
                                ch(tt(iu[:, c], iu[:, c], xc[:, c], ALU.mult))
                                before = lambda t: t[:, SB0 - 1:SB0 - 1 + NB * SP].rearrange(
                                    "p (b s) -> p b s", b=NB)[:, :, 0]
                                ch(dve.memset(before(la), 0.0))
                                ch(dve.tensor_copy(before(iu), pack[:, 372:380]))
                                dve.tensor_tensor_scan(ry[:, c], la[:, c], iu[:, c], 0.0, ALU.mult,
                                                       ALU.add).then_inc(S.scan, 1)
                                dve.wait_ge(S.scan, h + 1)
                                if later:
                                    dve.wait_ge(S.lrust, h * 32)
                                ch(dve.tensor_copy(hlast[:, 0:1], ry[:, TP - 1:TP]))
                                ch(dve.tensor_copy(hlast[:, 1:NC], padded(ry, NS - 1, 1)[:, :, 0]))
                                dve.wait_ge(S.gely, h + 1)
                                ch(tt(gy[:, 0:TP], gy[:, 0:TP], ry[:, 0:TP], ALU.mult))
                                tt(samples(gy), samples(gy), padded(ry, 0, NS), ALU.mult).then_inc(S.lruout, 1)
                                dve.wait_ge(S.lruout, h + 1)
                            if e == 23 and B:
                                dve.wait_ge(S.vsm, g + 1)
                                ch(dve.tensor_copy(vn[0:TS, 1, :], dps[0:TS, 3, 192:320]))
                                tt(vmask[0:TS, :, :], bc(vn[0:TS, 1, :].unsqueeze(1), [TS, NB, P]),
                                   bc(const[0:TS, C_BM:C_BM + NB].unsqueeze(2), [TS, NB, P]), ALU.mult).then_inc(S.vms, 1)
                                dve.wait_ge(S.vms, g + 1)
                            if e == 26 and B:
                                dve.wait_ge(S.ats, g + 1)
                                tt(kb[:, TP:T], kb[:, TP:T], dps[:, 3, 448:512], ALU.add).then_inc(S.oss, 1)
                                dve.wait_ge(S.oss, g + 1)
                            for n, e_n in ((0, 27), (1, 29)):
                                if e == e_n and B:
                                    v = sst[:, n * 4:n * 4 + 4, :]
                                    w = eglast[:, NCH + n * 4:NCH + n * 4 + 4].unsqueeze(2)
                                    ch(tt(v, v, bc(w, [P, 4, P]), ALU.mult))
                                    dve.wait_ge((S.dss0, S.dss1)[n], g + 1)
                                    tt(v, v, dps[:, 3, :].rearrange("p (b v) -> p b v", v=P),
                                       ALU.add).then_inc((S.sup0, S.sup1)[n], 1)
                            if e == 25 and A:
                                conv(0, 1, e2, S.evq, S.cvq)
                            if e == 34 and A:
                                conv(1, 0, em, S.evk, S.cvk)
                            for t in range(NCH):
                                if e == 32 + 4 * t and B:
                                    dve.wait_ge(S.vp, g * NCH + t + 1)
                                    dve.tensor_copy(vn[:, 0, :], dps[:, 1, 0:P]).then_inc(S.vcp, 1)
                                if e == 33 + 4 * t and B:
                                    dve.wait_ge(S.op, g * NCH + t + 1)
                                    stt(st[:, :], st[:, :], eglast[:, t:t + 1], dps[:, 3, 0:P], ALU.mult,
                                        ALU.add).then_inc(S.sup, 1)
                                    dve.wait_ge(S.sup, g * NCH + t + 1)
                            if e == 42 and A:
                                dve.wait_ge(S.slq, h + 1)
                                conv(2, 1, e2, S.evv, S.cvv)
                            if e == 47 and B:
                                dve.wait_ge(S.oinv, g + 1)
                                dve.wait_ge(S.ocp, g + 1)
                                ch(stt(kb[:, :], kb[:, :], dnw, sqs[:, 1, :], ALU.mult, ALU.mult))
                                tt(kb[:, :], kb[:, :], zc, ALU.mult).then_inc(S.oout, 1)
                                dve.wait_ge(S.oout, g + 1)

                    do_turns(dve, body, W.dve_steps, dve_total, DVE_STEPS_A_TURN)

        N4 = 2 + 12 * H
        X = Sems()
        X.saved, = sems(stack, "x_saved")
        at4 = [after]
        x1T = sb("x1T", [P, KT, T], at=at4)
        p5at = at4[0]
        rB2 = sb("rB2", [P, T], at=at4)
        amod2 = sb("amod2", [P, KT, NC], at=at4)
        tmp2 = sb("tmp2", [P, 2, T], at=at4)
        stage = sb("stage", [P, 2, T], at=at4)
        xin = sb("xin", [P, 2, T], at=at4)
        sq4 = sb("sq4", [P, 2, T], at=at4)

        def halves2(t):
            return t.rearrange("p (a t) -> p a t", a=2)

        def square_sums(pe, S, sq, m, first, last):
            pe.wait_ge(S.sq, m + 1)
            slot = sq
            for th in range(2):
                r = pe.matmul(dps[:, th, 0:HT], ones[:, :], slot[:, th * HT:(th + 1) * HT], start=first, stop=last)
            r.then_inc(S.sqpe, 1)

        with ExitStack() as c4:
            S = Sems()
            S.mix0, S.mix1, S.mhi, S.mlo, S.xl0 = sems(c4, "p4_mix0", "p4_mix1", "p4_mhi", "p4_mlo", "p4_xl0")
            S.xl1, S.x1, S.sq, S.sqpe = sems(c4, "p4_xl1", "p4_x1", "p4_sq", "p4_sqpe")
            s_mix, s_xl = [S.mix0, S.mix1], [S.xl0, S.xl1]
            with nc.Block() as block:
                @block.sync
                def _(sp):
                    for k in range(KT):
                        if k >= 2:
                            sp.wait_ge(S.mlo, k - 1)
                        sp.dma_start(stage[:, k % 2, :], mixD[k]).then_inc(s_mix[k % 2], 16)
                        if k == 1:
                            for n in range(2):
                                load_half(sp, a["w_out"][n], Nth(N4 + n))
                                sp.dma_start(xin[:, n, :], a["x_t"][:, n, :]).then_inc(s_xl[n], 16)
                    for n in range(2, 4):
                        load_half(sp, a["w_out"][n], Nth(N4 + n))
                    with sp.Fori(1, KT // 2) as i:
                        for j in range(4):
                            load_half(sp, row(a["w_out"], i * 4 + j), Nth(N4 + j, i, 4))
                            if j < 2:
                                sp.wait_ge(S.x1, i * 2 + (j - 1))
                                sp.dma_start(xin[:, j, :], a["x_t"][:, bass.ds(i * 2 + j, 1), :].rearrange(
                                    "p k t -> p (k t)")).then_inc(s_xl[j], 16)
                    sp.wait_ge(S.x1, KT)
                    sp.dma_start(x1D, x1T[:, :, :]).then_inc(X.saved, 16)

                @block.scalar
                def _(act):
                    ch = Chain(act, W.act_steps, act_total)
                    for k in range(KT):
                        act.wait_ge(s_mix[k % 2], 16 * (k // 2 + 1))
                        act.copy(act_hi[:, k, :], stage[:, k % 2, :]).then_inc(S.mhi, 1)
                        if k in (2, 3):
                            split_hi(act, Nth(N4 + k - 2))
                    for j in (2, 3):
                        split_hi(act, Nth(N4 + j))
                    with act.Fori(1, KT // 2) as i:
                        for j in range(4):
                            split_hi(act, Nth(N4 + j, i, 4))
                    act.wait_ge(S.sqpe, KT)
                    ch(act.activation(halves2(rB2[:, :]), dps[:, 0:2, 0:HT], ACT.Ln, bias=eps[:, :], scale=1.0 / D))
                    ch(act.activation(rB2[:, :], rB2[:, :], ACT.Exp, scale=-0.5))

                @block.gpsimd
                def _(pool):
                    for j in range(4):
                        split_lo(pool, Nth(N4 + j))
                    with pool.Fori(1, KT // 2) as i:
                        for j in range(4):
                            split_lo(pool, Nth(N4 + j, i, 4))

                @block.tensor
                def _(pe):
                    pe.wait_ge(S.mlo, KT)

                    def tile(m, k, pair):
                        if not (isinstance(m, int) and m < 2):
                            pe.wait_ge(S.x1, m - 1)
                        for half in range(2):
                            gemm_part(pe, k.plus(half), half, pair, 0, 8)

                    tile(0, Nth(N4), 0)
                    tile(1, Nth(N4 + 2), 1)
                    square_sums(pe, S, sq4[:, 0, :], 0, True, False)
                    with pe.Fori(1, KT // 2) as i:
                        tile(i * 2, Nth(N4, i, 4), 0)
                        square_sums(pe, S, sq4[:, 1, :], i * 2 - 1, False, False)
                        tile(i * 2 + 1, Nth(N4 + 2, i, 4), 1)
                        square_sums(pe, S, sq4[:, 0, :], i * 2, False, False)
                    square_sums(pe, S, sq4[:, 1, :], KT - 1, False, True)

                @block.vector
                def _(dve):
                    ch = Chain(dve, W.dve_steps, dve_total)
                    for k in range(KT):
                        dve.wait_ge(S.mhi, k + 1)
                        dve.tensor_tensor(act_lo[:, k, :], stage[:, k % 2, :], act_hi[:, k, :].bitcast(F32),
                                          ALU.subtract).then_inc(S.mlo, 1)

                    def residual(m, i, s):
                        n = N4 + 2 * s + 2
                        dve.wait_ge(W.used, n + i * 4)
                        dve.wait_ge(s_xl[s], i * 16 + 16)
                        at = bass.ds(m, 1)
                        x1 = x1T[:, at, :].rearrange("p k t -> p (k t)")
                        gate = modT[:, bass.ds(m + 2 * KT, 1), :].rearrange("p k n -> p (k n)")
                        pr = 2 * s
                        last = gps[:, pr + 1, TP - HT:HT].rearrange("p (b s) -> p b s", b=NB)
                        ch(dve.tensor_tensor(samples(x1), last, bc(gate[:, 1:NC].unsqueeze(2), [P, NB, NS]), ALU.mult))
                        ch(dve.tensor_tensor(x1[:, TP:T], x1[:, TP:T], xin[:, s, TP:T], ALU.add))
                        ch(dve.scalar_tensor_tensor(x1[:, 0:HT], gps[:, pr, 0:HT], gate[:, 0:1], xin[:, s, 0:HT],
                                                    ALU.mult, ALU.add))
                        dve.scalar_tensor_tensor(x1[:, HT:TP], gps[:, pr + 1, 0:TP - HT], gate[:, 0:1],
                                                 xin[:, s, HT:TP], ALU.mult, ALU.add).then_inc(S.x1, 1)
                        dve.wait_ge(S.x1, m + 1)
                        if not (isinstance(m, int) and m < 2):
                            dve.wait_ge(S.sqpe, m - 1)
                        dve.tensor_tensor(sq4[:, s, :], x1, x1, ALU.mult).then_inc(S.sq, 1)

                    residual(0, 0, 0)
                    residual(1, 0, 1)
                    with dve.Fori(1, KT // 2) as i:
                        ch.enter(i - 1, 6)
                        residual(i * 2, i, 0)
                        residual(i * 2 + 1, i, 1)
                    ch.leave(KT // 2 - 1)

        modulate(KT, x1T, rB2, amod2, tmp2, normw[1], 3 * KT, 4 * KT)

        N5 = N4 + 2 * KT
        at5 = [p5at]
        slots = sb("slots", [P, NTT, 3, H * TOPK], at=at5)
        p6at = at5[0]
        qt = sb("qt", [P, 2, T], at=at5)
        keys = sb("keys", [P, 2, NKEY], at=at5)
        sc = sb("sc", [P, 2, NTT, NKEY], at=at5)
        sc2 = sb("sc2", [P, NTT, NKEY], at=at5)
        topv = sb("topv", [P, NTT, 2, TOPK], at=at5)
        topi = sb("topi", [P, NTT, 2, TOPK], U32, at=at5)
        topf = sb("topf", [P, NTT, 2, TOPK], at=at5)
        cand = sb("cand", [P, NTT, TOPK, TOPK], at=at5)
        cand2 = sb("cand2", [P, NTT, TOPK, TOPK], at=at5)
        bestv = sb("bestv", [P, NTT, TOPK], at=at5)
        pos = sb("pos", [P, NTT, TOPK], U32, at=at5)
        part = sb("part", [P, 2, NTT, TOPK], U32, at=at5)
        partf = sb("partf", [P, 2, NTT, TOPK], at=at5)
        gsum = sb("gsum", [P, NTT, H], at=at5)
        carrier = sb("carrier", [P, 3], at=at5)
        with ExitStack() as c5:
            S = Sems()
            S.key0, S.key1, S.qev, S.score, S.scev = sems(c5, "p5_key0", "p5_key1", "p5_qev", "p5_score", "p5_scev")
            S.topk0, S.topk1, S.go, S.gmax, S.gexp = sems(c5, "p5_topk0", "p5_topk1", "p5_go", "p5_gmax", "p5_gexp")
            s_key, s_topk = [S.key0, S.key1], [S.topk0, S.topk1]

            def head_turns(eng, body, ch=None, steps=0):
                body(0)
                with eng.Fori(1, H - 1) as h:
                    if ch:
                        ch.enter(h - 1, steps)
                    body(h)
                if ch:
                    ch.leave(H - 2)
                body(H - 1)

            def wq_half(h, j):
                return Nth(N5 + 4 * h + j) if isinstance(h, int) else Nth(N5 + j, h, 4)

            with nc.Block() as block:
                @block.sync
                def _(sp):
                    def body(h):
                        for j in range(4):
                            load_half(sp, row(a["w_q"], h * 4 + j), wq_half(h, j))
                            if j % 2:
                                s = j // 2
                                if not isinstance(h, int) or h:
                                    sp.wait_ge(S.score, h * 2 + (s - 1))
                                sp.dma_start(keys[:, s, :], row(a["keys"], h * 2 + s)).then_inc(s_key[s], 16)

                    head_turns(sp, body)

                @block.gpsimd
                def _(pool):
                    def body(h):
                        for j in range(4):
                            split_lo(pool, wq_half(h, j))

                    head_turns(pool, body)

                @block.tensor
                def _(pe):
                    def scores(h, s):
                        m = h * 2 + s
                        pe.wait_ge(S.qev, m + 1)
                        pe.wait_ge(s_key[s], h * 16 + 16)
                        if not isinstance(h, int) or h:
                            pe.wait_ge(S.scev, m - 1)
                        for t in range(NTT):
                            n = CH if t < NCH else TS
                            o = dps[:, 2 * s, t * CH:(t + 1) * CH] if t < NCH else dps[0:TS, 2 * s + 1, 0:NKEY]
                            r = pe.matmul(o, qt[:, s, t * CH:t * CH + n], keys[:, s, :], start=True, stop=True)
                        r.then_inc(S.score, 1)

                    def body(h):
                        later = not isinstance(h, int) or h > 0
                        for s in range(2):
                            if later:
                                pe.wait_ge(S.qev, h * 2 + (s - 1))
                            for half in range(2):
                                gemm_part(pe, wq_half(h, 2 * s + half), half, s, 0, 8)
                            if s == 0 and later:
                                scores(h - 1, 1)
                            if s == 1:
                                scores(h, 0)

                    head_turns(pe, body)
                    scores(H - 1, 1)

                @block.scalar
                def _(act):
                    ch = Chain(act, W.act_steps, act_total)

                    def take_scores(h, s):
                        act.wait_ge(S.score, h * 2 + s + 1)
                        if not isinstance(h, int) or h:
                            act.wait_ge(s_topk[s], h)
                        ch(act.copy(sc[:, s, 0:NCH, :], dps[:, 2 * s, :].rearrange("p (t n) -> p t n", n=NKEY)))
                        act.copy(sc[0:TS, s, NCH, :], dps[0:TS, 2 * s + 1, 0:NKEY]).then_inc(S.scev, 1)

                    def body(h):
                        later = not isinstance(h, int) or h > 0
                        last = isinstance(h, int) and h == H - 1
                        for s in range(2):
                            for j in (2 * s + 2, 2 * s + 3):
                                if not (last and s):
                                    split_hi(act, wq_half(h, j))
                            act.wait_ge(W.used, wq_half(h, 2 * s + 1).n + 1)
                            if later:
                                act.wait_ge(S.score, h * 2 + (s - 1))
                            act.copy(halves2(qt[:, s, :]), gps[:, 2 * s:2 * s + 2, 0:HT]).then_inc(S.qev, 1)
                            if s == 0 and later:
                                take_scores(h - 1, 1)
                            if s == 1:
                                take_scores(h, 0)

                    act.wait_ge(S.go, 1)
                    split_hi(act, wq_half(0, 0))
                    split_hi(act, wq_half(0, 1))
                    body(0)
                    with act.Fori(1, H - 1) as h:
                        ch.enter(h - 1, 2)
                        body(h)
                    ch.leave(H - 2)
                    body(H - 1)
                    take_scores(H - 1, 1)
                    act.wait_ge(S.gmax, 1)
                    act.activation(slots[:, :, 2, :], slots[:, :, 2, :], ACT.Exp).then_inc(S.gexp, 1)

                @block.vector
                def _(dve):
                    dve.memset(sc[:, :, NCH, :], 0.0).then_inc(S.go, 1)
                    dve.wait_ge(S.go, 1)

                    def carry(n=0):
                        dve.memset(carrier[:, n:n + 1], 0.0)

                    ch = Chain(dve, W.dve_steps, dve_total, carry)

                    def each(fn):
                        for t in range(NTT):
                            m = fn(t)
                        ch(m)

                    def top16(values, less, v, i):
                        each(lambda t: dve.max(v(t)[:, 0:8], values(t)))
                        each(lambda t: dve.max_index(i(t)[:, 0:8], v(t)[:, 0:8], values(t)))
                        each(lambda t: dve.match_replace(less(t), v(t)[:, 0:8], values(t), LOW))
                        each(lambda t: dve.max(v(t)[:, 8:16], less(t)))
                        each(lambda t: dve.max_index(i(t)[:, 8:16], v(t)[:, 8:16], less(t)))

                    def body(h):
                        for s in range(2):
                            dve.wait_ge(S.scev, h * 2 + s + 1)
                            carry(1 + s)
                            top16(lambda t: sc[:, s, t, :], lambda t: sc2[:, t, :], lambda t: topv[:, t, s, :],
                                  lambda t: topi[:, t, s, :])
                            dve.tensor_copy(topf[:, :, s, :], topi[:, :, s, :]).then_inc(s_topk[s], 1)
                            dve.wait_ge(s_topk[s], h + 1)
                        full = [P, NTT, TOPK, TOPK]
                        ch(dve.tensor_tensor(cand[:, :, :, :], bc(topv[:, :, 0, :].unsqueeze(3), full),
                                             bc(topv[:, :, 1, :].unsqueeze(2), full), ALU.add))
                        flat = lambda c: lambda t: c[:, t, :, :].rearrange("p a b -> p (a b)")
                        top16(flat(cand), flat(cand2), lambda t: bestv[:, t, :], lambda t: pos[:, t, :])
                        mine = bass.ds(h * TOPK, TOPK)
                        ch(dve.tensor_copy(slots[:, :, 2, mine], bestv[:, :, :]))
                        ch(dve.tensor_scalar(part[:, 0], pos[:, :, :], 4, None, ALU.logical_shift_right))
                        ch(dve.tensor_scalar(part[:, 1], pos[:, :, :], TOPK - 1, None, ALU.bitwise_and))
                        ch(dve.tensor_copy(partf[:, :, :, :], part[:, :, :, :]))
                        ramp = const[:, C_IOTA:C_IOTA + TOPK].unsqueeze(1).unsqueeze(1)
                        for s in range(2):
                            ch(dve.tensor_tensor(cand[:, :, :, :], bc(partf[:, s].unsqueeze(3), full),
                                                 bc(ramp, full), ALU.is_equal))
                            ch(dve.tensor_tensor(cand[:, :, :, :], cand[:, :, :, :],
                                                 bc(topf[:, :, s, :].unsqueeze(2), full), ALU.mult))
                            ch(dve.tensor_reduce(slots[:, :, s, mine], cand[:, :, :, :], AX.X, ALU.add))

                    head_turns(dve, body, ch, 26)
                    g = slots[:, :, 2, :].rearrange("p t (h k) -> p t h k", k=TOPK)
                    ch(dve.tensor_copy(gsum[:, :, :], g[:, :, :, 0]))
                    dve.tensor_tensor(g, g, bc(gsum[:, :, :].unsqueeze(3), [P, NTT, H, TOPK]),
                                      ALU.subtract).then_inc(S.gmax, 1)
                    dve.wait_ge(S.gexp, 1)
                    ch(dve.tensor_reduce(gsum[:, :, :], g, AX.X, ALU.add))
                    ch(dve.reciprocal(gsum[:, :, :], gsum[:, :, :]))
                    ch(dve.tensor_tensor(g, g, bc(gsum[:, :, :].unsqueeze(3), [P, NTT, H, TOPK]), ALU.mult))


        OCT = 8
        QUAD = 4
        OPB = GB // OCT
        at6 = [p6at]
        slotT = sb("slotT", [P, 3, T], at=at6)
        ga = sb("ga", [P, 2, OCT, NKEY], at=at6)
        gb = sb("gb", [P, 2, OCT, NKEY], at=at6)
        gst = [sb("gst0", [P, NKEY, GB], at=[raw_at]), sb("gst1", [P, NKEY, GB], at=[after])]
        with ExitStack() as c6:
            S = Sems()
            S.tr, S.trev, S.first, S.apool, S.advec = sems(c6, "p6_tr", "p6_trev", "p6_first", "p6_apool", "p6_advec")
            S.b, S.mm, S.ev, S.out0, S.out1 = sems(c6, "p6_b", "p6_mm", "p6_ev", "p6_out0", "p6_out1")
            s_out = [S.out0, S.out1]

            with nc.Block() as block:
                @block.sync
                def _(sp):
                    with sp.Fori(0, NGB // 2) as i:
                        for b in range(2):
                            sp.wait_ge(S.ev, i * (4 * OPB) + (4 + 2 * OPB * (b + 1)))
                            sp.dma_start(gateD[bass.ds(i * 2 + b, 1)].rearrange("b j i t -> (b j) (i t)"),
                                         gst[b][:, :, :].rearrange("p i t -> p (i t)")).then_inc(s_out[b], 16)
                    for b in range(2):
                        sp.wait_ge(s_out[b], 16 + 16 * (NGB // 2))

                @block.tensor
                def _(pe):
                    for k in range(3):
                        for t in range(NCH):
                            pe.transpose(dps[:, k, t * CH:(t + 1) * CH], slots[:, t, k, :], ident)
                        m = pe.transpose(dps[:, 3, k * TS:(k + 1) * TS], slots[0:TS, NCH, k, :], const[0:TS, 0:TS])
                    m.then_inc(S.tr, 1)
                    pe.wait_ge(S.trev, 4)
                    with pe.Fori(0, NGB // 2) as i:
                        for o in range(2 * OPB):
                            pe.wait_ge(S.apool if o % 2 else S.advec, i * OPB + (o // 2 + 1))
                            pe.wait_ge(S.b, i * (2 * OPB) + (o + 1))
                            for q in range(2):
                                bank = 2 * o + q
                                pe.wait_ge(S.ev, i * (4 * OPB) + (bank + 1))
                                for t in range(QUAD):
                                    m = pe.matmul(dps[:, bank % 4, t * NKEY:(t + 1) * NKEY],
                                                  gb[:, o % 2, q * QUAD + t, :], ga[:, o % 2, q * QUAD + t, :],
                                                  start=True, stop=True)
                                m.then_inc(S.mm, 1)

                @block.scalar
                def _(act):
                    act.wait_ge(S.tr, 1)
                    for k in range(3):
                        act.copy(slotT[:, k, 0:TP], dps[:, k, :]).then_inc(S.trev, 1)
                    act.copy(slotT[:, :, TP:T], dps[:, 3, 0:3 * TS].rearrange("p (k t) -> p k t", k=3)
                             ).then_inc(S.trev, 1)
                    act.wait_ge(X.saved, 16)
                    with act.Fori(0, NGB // 2) as i:
                        for b in range(2):
                            act.wait_ge(s_out[b], i * 16 + 16)
                            for n in range(2 * OPB):
                                bank = 2 * OPB * b + n
                                act.wait_ge(S.mm, i * (4 * OPB) + (4 + bank + 1))
                                act.copy(gst[b][:, :, n * QUAD:(n + 1) * QUAD],
                                         dps[:, bank % 4, :].rearrange("p (t i) -> p i t", i=NKEY)
                                         ).then_inc(S.ev, 1)

                def compare(out, kind, at):
                    full = [P, OCT, NKEY]
                    return nc.vector.tensor_tensor(out, bc(slotT[:, kind, at].unsqueeze(2), full),
                                             bc(const[:, C_IOTA:C_IOTA + NKEY].unsqueeze(1), full), ALU.is_equal)

                def times_gate(eng, o, at):
                    return eng.tensor_tensor(ga[:, o % 2], ga[:, o % 2],
                                             bc(slotT[:, 2, at].unsqueeze(2), [P, OCT, NKEY]), ALU.mult)

                def tokens(i, o):
                    return bass.ds(i * (2 * GB) + o * OCT, OCT)

                @block.gpsimd
                def _(pool):
                    pool.wait_ge(S.trev, 4)
                    with pool.Fori(0, NGB // 2) as i:
                        for o in range(1, 2 * OPB, 2):
                            pool.wait_ge(S.first, i * OPB + (o + 1) // 2)
                            times_gate(pool, o, tokens(i, o)).then_inc(S.apool, 1)

                @block.vector
                def _(dve):
                    for n in range(4):
                        dve.engine_nop().then_inc(S.mm, 1)
                        dve.engine_nop().then_inc(S.ev, 1)
                    for b in range(2):
                        dve.engine_nop().then_inc(s_out[b], 16)
                    ch = Chain(dve, W.dve_steps, dve_total)
                    dve.wait_ge(S.trev, 4)
                    with dve.Fori(0, NGB // 2) as i:
                        ch.enter(i, OPB)
                        for o in range(2 * OPB):
                            dve.wait_ge(S.mm, i * (4 * OPB) + (2 * o + 2))
                            m = compare(ga[:, o % 2], 0, tokens(i, o))
                            if o % 2:
                                m.then_inc(S.first, 1)
                            else:
                                ch(m)
                                times_gate(dve, o, tokens(i, o)).then_inc(S.advec, 1)
                            compare(gb[:, o % 2], 1, tokens(i, o)).then_inc(S.b, 1)
                    ch.leave(NGB // 2)

        N7 = N5 + 4 * H
        at7 = [after]
        outacc = sb("outacc", [P, KT, T], at=at7)
        gate = sb("gate", [P, 2, NGB, 2, GB], at=at7)
        chi = sb("chi", [P, 2, NG, T], F32R, at=at7)
        clo = sb("clo", [P, 2, NG, T], F32R, at=at7)
        gel = sb("gel", [P, 2, T], at=at7)
        with ExitStack() as c7:
            S = Sems()
            S.gate0, S.gate1, S.gel, S.gated, S.chi = sems(c7, "p7_gate0", "p7_gate1", "p7_gel", "p7_gated", "p7_chi")
            S.clo, S.vd, S.acc, S.zero = sems(c7, "p7_clo", "p7_vd", "p7_acc", "p7_zero")
            s_gate = [S.gate0, S.gate1]

            def first_u(g, i=None):
                return Nth(N7 + max(0, 16 * g - 8)) if i is None else Nth(N7 + 16 * g - 8, i, 32)

            def first_v(g, i=None):
                if i is None:
                    return Nth(N7 + min(16 * g + 16, 2 * 8 * NGRP - 8))
                return Nth(N7 + 16 * g + 16, i, 32)

            def groups(eng, A, B):
                A(0, 0, first_u(0), first_u(1))
                with eng.Fori(0, NGRP // 2 - 1) as i:
                    A(i * 2 + 1, 1, first_u(1, i), first_v(0, i))
                    B(i * 2, 0, first_v(0, i), first_u(2, i))
                    A(i * 2 + 2, 0, first_u(2, i), first_v(1, i))
                    B(i * 2 + 1, 1, first_v(1, i), first_u(3, i))
                A(NGRP - 1, 1, first_u(NGRP - 1), first_v(NGRP - 2))
                B(NGRP - 2, 0, first_v(NGRP - 2), first_v(NGRP - 1))
                B(NGRP - 1, 1, first_v(NGRP - 1), None)

            def later(g, n=1):
                return not isinstance(g, int) or g >= n

            with nc.Block() as block:
                @block.sync
                def _(sp):
                    def A(g, buf, k, after):
                        for j in range(2 * NG):
                            if j % 4 == 0:
                                pair = j // 4
                                if later(g):
                                    sp.wait_ge(S.gated, g * NG + (2 * pair - 2))
                                sp.dma_start(gate[:, pair].rearrange("p b c t -> p b (c t)"),
                                             gateD[:, :, bass.ds(g * NG + 2 * pair, 2), :].rearrange(
                                                 "b j i t -> j b (i t)")).then_inc(s_gate[pair], 16)
                            load_half(sp, row(a["u"], g * 8 + j), k.plus(j))

                    def B(g, buf, k, after):
                        for s in range(8):
                            load_half(sp, row(a["v"], g * 8 + s), k.plus(s))

                    groups(sp, A, B)

                @block.gpsimd
                def _(pool):
                    def both(g, buf, k, after):
                        for j in range(8):
                            split_lo(pool, k.plus(j))

                    groups(pool, both, both)

                @block.tensor
                def _(pe):
                    def A(g, buf, k, after):
                        for c in range(NG):
                            if later(g) or c >= 2:
                                pe.wait_ge(S.gel, g * NG + (c - 1))
                            for half in range(2):
                                gemm_part(pe, k.plus(2 * c + half), half, c % 2, 0, 8)

                    def B(g, buf, k, after):
                        pe.wait_ge(S.clo, g * NG + NG)
                        for s in range(8):
                            pe.wait_ge(W.lo, k.plus(s).n + 1)
                            slot = k.plus(s).slot
                            for dt in range(2):
                                pe.wait_ge(S.acc, g * KT + (2 * s + dt + 1))
                                for c in range(NG):
                                    cols = slice(c * 2 * P + dt * P, c * 2 * P + (dt + 1) * P)
                                    for n, (w, x) in enumerate(((whi, chi), (whi, clo), (wlo, chi))):
                                        for th in range(2):
                                            m = pe.matmul(dps[:, 2 * dt + th, 0:HT], w[:, slot, cols],
                                                          x[:, buf, c, th * HT:(th + 1) * HT],
                                                          start=(c == 0 and n == 0), stop=(c == NG - 1 and n == 2))
                                m.then_inc((S.vd, W.used)[dt], 1)

                    groups(pe, A, B)

                @block.scalar
                def _(act):
                    def A(g, buf, k, after):
                        for c in range(NG):
                            for j in (2 * c + 2, 2 * c + 3):
                                split_hi(act, k.plus(j) if j < 8 else after.plus(j - 8))
                            act.wait_ge(W.used, k.plus(2 * c + 1).n + 1)
                            if later(g) or c >= 2:
                                act.wait_ge(S.clo, g * NG + (c - 1))
                            act.activation(halves2(gel[:, c % 2, :]), gps[:, 2 * (c % 2):2 * (c % 2) + 2, 0:HT],
                                           ACT.Gelu_apprx_tanh).then_inc(S.gel, 1)
                            act.wait_ge(S.gated, g * NG + (c + 1))
                            act.copy(chi[:, buf, c, :], gel[:, c % 2, :]).then_inc(S.chi, 1)

                    def B(g, buf, k, after):
                        for s in range(8):
                            if s < 6:
                                split_hi(act, k.plus(s + 2))
                            elif after is not None:
                                split_hi(act, after.plus(s - 6))

                    for j in range(2):
                        split_hi(act, first_u(0).plus(j))
                    groups(act, A, B)

                @block.vector
                def _(dve):
                    dve.memset(outacc[:, :, :], 0.0).then_inc(S.zero, 1)
                    dve.wait_ge(S.zero, 1)
                    for n in range(2):
                        dve.engine_nop().then_inc(S.acc, 1)

                    def A(g, buf, k, after):
                        for c in range(NG):
                            dve.wait_ge(S.gel, g * NG + (c + 1))
                            dve.wait_ge(s_gate[c // 2], g * 16 + 16)
                            ge = gel[:, c % 2, :].rearrange("p (b t) -> p b t", t=GB)
                            dve.tensor_tensor(ge, ge, gate[:, c // 2, :, c % 2, :], ALU.mult).then_inc(S.gated, 1)
                            dve.wait_ge(S.chi, g * NG + (c + 1))
                            dve.tensor_tensor(clo[:, buf, c, :], gel[:, c % 2, :], chi[:, buf, c, :].bitcast(F32),
                                              ALU.subtract).then_inc(S.clo, 1)

                    def B(g, buf, k, after):
                        dve.wait_ge(S.acc, g * KT + 2)
                        for s in range(8):
                            for dt in range(2):
                                if dt == 0:
                                    dve.wait_ge(S.vd, g * 8 + (s + 1))
                                else:
                                    dve.wait_ge(W.used, k.plus(s).n + 1)
                                out = halves2(outacc[:, 2 * s + dt, :])
                                dve.tensor_tensor(out, out, dps[:, 2 * dt:2 * dt + 2, 0:HT], ALU.add
                                                  ).then_inc(S.acc, 1)

                    groups(dve, A, B)

        at8 = [act_at]
        x2T = sb("x2T", [P, KT, T], at=at8)
        sq8 = sb("sq8", [P, 2, T], at=at8)
        rB3 = sb("rB3", [P, T], at=at8)
        with ExitStack() as c8:
            S = Sems()
            S.x1, S.x2, S.sq, S.sqpe, S.rstd = sems(c8, "p8_x1", "p8_x2", "p8_sq", "p8_sqpe", "p8_rstd")
            S.y, S.out = sems(c8, "p8_y", "p8_out")
            with nc.Block() as block:
                @block.sync
                def _(sp):
                    for k in range(0, KT, 4):
                        sp.dma_start(x2T[:, k:k + 4, :], x1D[:, k:k + 4, :]).then_inc(S.x1, 16)
                        sp.wait_ge(S.x1, 4 * k + 16)
                    for k in range(0, KT, 2):
                        sp.wait_ge(S.y, k + 2)
                        sp.dma_start(a["y_t"][:, k:k + 2, :], x2T[:, k:k + 2, :]).then_inc(S.out, 16)
                    sp.wait_ge(S.out, 16 * (KT // 2))

                @block.vector
                def _(dve):
                    ch = Chain(dve, W.dve_steps, dve_total)
                    for k in range(KT):
                        if k % 4 == 0:
                            dve.wait_ge(S.x1, 4 * k + 16)
                        gate2 = modT[:, 5 * KT + k, :]
                        out = outacc[:, k, :]
                        ch(dve.tensor_tensor(samples(out), samples(out), bc(gate2[:, 1:NC].unsqueeze(2), [P, NB, NS]),
                                             ALU.mult))
                        ch(dve.tensor_tensor(x2T[:, k, TP:T], x2T[:, k, TP:T], out[:, TP:T], ALU.add))
                        dve.scalar_tensor_tensor(x2T[:, k, 0:TP], out[:, 0:TP], gate2[:, 0:1], x2T[:, k, 0:TP],
                                                 ALU.mult, ALU.add).then_inc(S.x2, 1)
                    dve.wait_ge(S.x2, KT)
                    dve.wait_ge(S.rstd, 1)
                    for k in range(KT):
                        dve.scalar_tensor_tensor(x2T[:, k, :], x2T[:, k, :], normw[2][:, k:k + 1], rB3[:, :],
                                                 ALU.mult, ALU.mult).then_inc(S.y, 1)

                @block.scalar
                def _(act):
                    ch = Chain(act, W.act_steps, act_total)
                    for k in range(KT):
                        act.wait_ge(S.x2, k + 1)
                        if k >= 2:
                            act.wait_ge(S.sqpe, k - 1)
                        act.activation(sq8[:, k % 2, :], x2T[:, k, :], ACT.Square).then_inc(S.sq, 1)
                    act.wait_ge(S.sqpe, KT)
                    ch(act.activation(halves2(rB3[:, :]), dps[:, 0:2, 0:HT], ACT.Ln, bias=eps[:, :], scale=1.0 / D))
                    act.activation(rB3[:, :], rB3[:, :], ACT.Exp, scale=-0.5).then_inc(S.rstd, 1)

                @block.tensor
                def _(pe):
                    for k in range(KT):
                        square_sums(pe, S, sq8[:, k % 2, :], k, k == 0, k == KT - 1)


def layout(i):
    np_ = lambda name: np.asarray(i[name])
    cols = lambda v, n: np.ascontiguousarray(v.reshape(n, P).T)

    def halves(w):
        m = w.shape[1] // P
        return np.ascontiguousarray(w.reshape(2, 8, P, m, P).transpose(3, 0, 2, 1, 4)).reshape(2 * m, P, HALF)

    x = np.concatenate([np_("x_prompt").reshape(TP, D), np_("x_sample").reshape(TS, D)])
    c = np.concatenate([np_("c_prompt"), np_("c_sample")])
    w_in = np_("w_in")[0]
    qkv, z, ba = 2 * H * P, 5 * H * P, 6 * H * P
    tiles = []
    for h in range(H):
        for at in (0, H * P, qkv, qkv + H * P, qkv + 2 * H * P, z):
            tiles.append(w_in[:, at + h * P:at + (h + 1) * P])
    w_ba = np.zeros((D, P), w_in.dtype)
    w_ba[:, 0:H] = w_in[:, ba:ba + H]
    w_ba[:, 32:32 + H] = w_in[:, ba + H:ba + 2 * H]
    dcw, lcw = np_("dn_conv_w")[0], np_("lru_conv_w")[0]
    dst, lst = np_("state_dn_conv")[0], np_("state_lru_conv")[0]
    pack = np.zeros((H, P, PACK), w_in.dtype)
    for h in range(H):
        s = slice(h * P, (h + 1) * P)
        for n in range(3):
            ch = slice((n * H + h) * P, (n * H + h + 1) * P)
            pack[h, :, n * CW:(n + 1) * CW] = dcw[:, ch].T
            pack[h, :, 20 + n * 24:20 + (n + 1) * 24] = dst[:, :, ch].transpose(2, 0, 1).reshape(P, 24)
        pack[h, :, 12:16] = lcw[:, s].T
        pack[h, :, 92:116] = lst[:, :, s].transpose(2, 0, 1).reshape(P, 24)
        pack[h, :, 16] = np_("lru_conv_b")[0, s]
        pack[h, :, 17] = np_("lru_ba")[0, s]
        pack[h, :, 18] = np_("lru_bx")[0, s]
        pack[h, :, 116:244] = np_("lru_wa")[0, h]
        pack[h, :, 244:372] = np_("lru_wx")[0, h]
        pack[h, :, 372:380] = np_("state_lru_h")[0][:, s].T
    u = np_("peer_u")[0].reshape(NKEY, P, 2, 8, P).transpose(0, 2, 4, 3, 1)
    v = np_("peer_v")[0].reshape(NGRP, NG, P, 8, 2 * P).transpose(0, 3, 2, 1, 4)
    return {
        "consts": constants(),
        "vecs": np.concatenate([cols(np_("b_ada")[0], NM), cols(np_("norm_mix_w")[0], KT),
                                cols(np_("norm_ffn_w")[0], KT), cols(np_("final_norm_w"), KT),
                                np_("dn_norm_w")[0][:, None]], axis=1),
        "c_t": np.ascontiguousarray(c.reshape(NC, KT, P).transpose(2, 1, 0)),
        "x_t": np.ascontiguousarray(x.reshape(T, KT, P).transpose(2, 1, 0)),
        "w_ada": np_("w_ada")[0],
        "lam_t": cols(np_("lru_lambda")[0], H),
        "head_v": np.stack([np_("dn_A_log")[0], np_("dn_dt_bias")[0]], axis=1),
        "w_ba": halves(w_ba),
        "w_in": halves(np.concatenate(tiles, axis=1)),
        "pack": pack,
        "dn_s": np_("state_dn_S")[0],
        "w_out": halves(np_("w_out")[0]),
        "w_q": halves(np_("peer_wq")[0]),
        "keys": np.ascontiguousarray(np_("peer_subkeys")[0].transpose(0, 1, 3, 2)).reshape(2 * H, P, NKEY),
        "u": np.ascontiguousarray(u).reshape(2 * NKEY, P, HALF),
        "v": np.ascontiguousarray(v).reshape(8 * NGRP, P, HALF),
    }


OUTS = {
    "y_t": (P, KT, T),
    "conv_t": (H, P, 4 * NC * PL),
    "lru_h_t": (H, P, NC),
    "s_prompt": (H, P, P),
    "s_sample": (NB, H, P, P),
}


def unlayout(r):
    y = r["y_t"].transpose(2, 1, 0).reshape(T, D)
    conv = r["conv_t"].reshape(H, P, 4, NC, PL)
    dn = conv[:, :, 0:3].transpose(3, 4, 2, 0, 1).reshape(NC, PL, 3 * H * P)
    lc = conv[:, :, 3].transpose(2, 3, 0, 1).reshape(NC, PL, H * P)
    lh = r["lru_h_t"].transpose(2, 0, 1).reshape(NC, H * P)
    own = lambda v: np.ascontiguousarray(v)
    return (own(y[:TP].reshape(1, TP, D)), own(y[TP:].reshape(NB, NS, D)),
            own(lc[None, 0:1]), own(lh[None, 0:1]), own(dn[None, 0:1]), own(r["s_prompt"][None, None]),
            own(lc[None, 1:]), own(lh[None, 1:]), own(dn[None, 1:]), own(r["s_sample"][None]))


def kernel(**inputs):
    import concourse.bacc as bacc
    from concourse.bass_utils import run_bass_kernel_spmd

    nc = bacc.Bacc("TRN2", target_bir_lowering=False, num_devices=1)
    arrays, aps = {}, {}
    for name, v in layout(inputs).items():
        arrays[f"in_{name}"] = v
        aps[name] = nc.dram_tensor(f"in_{name}", v.shape, mybir.dt.from_np(v.dtype), kind="ExternalInput").ap()
    for name, shape in OUTS.items():
        aps[name] = nc.dram_tensor(f"out_{name}", shape, F32, kind="ExternalOutput").ap()
    build(nc, aps)
    r = run_bass_kernel_spmd(nc, [arrays], core_ids=[0])
    return unlayout({name: r.results[0][f"out_{name}"] for name in OUTS})
```

```python
from contextlib import ExitStack

import numpy as np

import concourse.bass as bass
from concourse import mybir

ALU = mybir.AluOpType
ACT = mybir.ActivationFunctionType
AX = mybir.AxisListType
F32 = mybir.dt.float32
F32R = mybir.dt.float32r
U32 = mybir.dt.uint32

P = 128
D = 2048
KT = D // P
TP = 512
NB, NS = 8, 8
TS = NB * NS
T = TP + TS
HT = T // 2
NC = 1 + NB
H = 8
CW = 4
PL = CW - 1
SP = PL + NS
PADW = PL + TP + NB * SP
CONVW = PADW - PL
SB0 = PL + TP
CH = 128
NCH = TP // CH
NTT = NCH + 1
EPS = 1e-6
NM = 6 * D // P
HALF = 8 * P
NKEY = 128
TOPK = 16
NG = 4
NGRP = NKEY // NG
GB = 36
NGB = T // GB
PACK = 5 * CW + 4 * NB * PL + 2 * P + NB
ACT_STEPS_A_TURN = 27
DVE_STEPS_A_TURN = 81
LOW = -3.0e38
AHEAD = 2
NBANK = 512

C_ID, C_LEVEL, C_INCL, C_SINCL, C_BM, C_IOTA, CONSTS = 0, 128, 128 + 7 * 128, 1152, 1216, 1224, 1352
LEVELS = 7


def constants():
    c = np.zeros((P, CONSTS), np.float32)
    j, i = np.meshgrid(np.arange(P), np.arange(P), indexing="ij")
    c[:, C_ID:C_ID + P] = np.eye(P)
    for n in range(LEVELS):
        s = 1 << n
        c[:, C_LEVEL + n * P:C_LEVEL + (n + 1) * P] = (i // (2 * s) == j // (2 * s)) & (i // s % 2 == 1) & (j // s % 2 == 0)
    c[:, C_INCL:C_INCL + P] = j <= i
    c[:TS, C_SINCL:C_SINCL + TS] = ((j <= i) & (j // NS == i // NS))[:TS, :TS]
    for b in range(NB):
        c[b * NS:(b + 1) * NS, C_BM + b] = 1
    c[:, C_IOTA:C_IOTA + P] = np.arange(P)[None, :]
    return c


class Chain:

    def __init__(self, eng, sem, total, carry=None):
        self.eng, self.sem, self.total, self.base, self.n, self.carry = eng, sem, total, total[0], 0, carry

    def __call__(self, ins):
        ins.then_inc(self.sem, 1)
        self.n += 1
        self.eng.wait_ge(self.sem, self.base + self.n)
        if isinstance(self.base, int):
            self.total[0] = self.base + self.n
        if self.carry:
            self.carry()

    def enter(self, i, steps):
        self.start, self.steps = self.base + self.n, steps
        self.base, self.n = self.start + i * steps, 0

    def leave(self, turns):
        assert self.n == self.steps, f"{self.n} steps in a turn"
        self.base, self.n = self.start + turns * self.steps, 0
        self.total[0] = self.base


class Sems:
    pass


class Nth:

    def __init__(self, c, i=0, per=0):
        self.c, self.i, self.per = c, i, per
        self.n = c + i * per
        self.raw, self.slot = c % 2, c % 4
        assert per % 4 == 0

    def plus(self, j):
        return Nth(self.c + j, self.i, self.per)

    def loads(self):
        return 16 * (self.c // 2 + 1) + self.i * (8 * self.per)


def row(t, i):
    if isinstance(i, int):
        return t[i]
    r = t[bass.ds(i, 1)]
    return r.rearrange("a p f -> (a p) f") if len(t.shape) == 3 else r.rearrange("a p k f -> (a p) k f")


def build(nc, a):
    stack = ExitStack()
    with stack:
        base = [(nc.sbuf_base + 31) // 32 * 32]

        def sb(name, shape, dt=F32, at=None):
            at = base if at is None else at
            n = 4
            for x in shape[1:]:
                n *= x
            t = nc.alloc_sbuf_tensor_at(name, list(shape), dt, offset=at[0])
            at[0] += (n + 31) // 32 * 32
            assert at[0] <= nc.sbuf_usable_end, (name, at[0])
            return t

        def ps(name, shape):
            return stack.enter_context(nc.psum_tensor(name, list(shape), F32))

        const = sb("const", [P, CONSTS])
        ones = sb("ones", [P, P])
        modT = sb("modT", [P, NM, NC])
        vecs = sb("vecs", [P, NM + 3 * KT + 1])
        eps = sb("eps", [P, 1])
        raw_at = base[0]
        raw = sb("raw", [P, 2, HALF])
        whi = sb("whi", [P, 4, HALF], F32R)
        wlo = sb("wlo", [P, 4, HALF], F32R)
        ident = const[:, C_ID:C_ID + P]
        bada = vecs[:, 0:NM]
        normw = [vecs[:, NM + n * KT:NM + (n + 1) * KT] for n in range(3)]
        dnw = vecs[:, NM + 3 * KT:NM + 3 * KT + 1]
        act_hi = sb("act_hi", [P, KT, T], F32R)
        act_lo = sb("act_lo", [P, KT, T], F32R)
        after = base[0]
        act_at = after - 2 * KT * T * 4

        gps = ps("gps", [P, 4, NBANK])
        dps = ps("dps", [P, 4, NBANK])

        mixD = nc.dram_tensor("mixD", [2 * H, P, T], F32, kind="Internal").ap()
        x1D = nc.dram_tensor("x1D", [P, KT, T], F32, kind="Internal").ap()
        rowsD = nc.dram_tensor("rowsD", [H, 4, T], F32, kind="Internal").ap()
        gateD = nc.dram_tensor("gateD", [NGB, P, NKEY, GB], F32, kind="Internal").ap()

        def sems(ctx, *names):
            return [ctx.enter_context(nc.semaphore(n)) for n in names]

        W = Sems()
        W.loaded0, W.loaded1, W.hi, W.lo, W.used = sems(stack, "w_loaded0", "w_loaded1", "w_hi", "w_lo", "w_used")
        W.act_steps, W.dve_steps = sems(stack, "w_act_steps", "w_dve_steps")
        act_total, dve_total = [0], [0]
        w_loaded = [W.loaded0, W.loaded1]

        def load_half(sp, src, k):
            if not (isinstance(k.n, int) and k.n < 2):
                sp.wait_ge(W.lo, k.n - 1)
            sp.dma_start(raw[:, k.raw, :], src).then_inc(w_loaded[k.raw], 16)

        def split_hi(act, k):
            act.wait_ge(w_loaded[k.raw], k.loads())
            if not (isinstance(k.n, int) and k.n < 4):
                act.wait_ge(W.used, k.n - 3)
            act.copy(whi[:, k.slot, :], raw[:, k.raw, :]).then_inc(W.hi, 1)

        def split_lo(pool, k):
            pool.wait_ge(W.hi, k.n + 1)
            pool.tensor_tensor(wlo[:, k.slot, :], raw[:, k.raw, :], whi[:, k.slot, :].bitcast(F32),
                               ALU.subtract).then_inc(W.lo, 1)

        def gemm_part(pe, k, half, pair, first, count, ready=None):
            if first == 0:
                pe.wait_ge(W.lo, k.n + 1)
            for kk in range(first, first + count):
                kt = half * 8 + kk
                if ready:
                    ready(pe, kt)
                hi, lo = (w[:, k.slot, kk * P:(kk + 1) * P] for w in (whi, wlo))
                for n, (w, x) in enumerate(((hi, act_hi), (hi, act_lo), (lo, act_hi))):
                    for th in range(2):
                        m = pe.matmul(gps[:, 2 * pair + th, 0:HT], w, x[:, kt, th * HT:(th + 1) * HT],
                                      start=(kt == 0 and n == 0), stop=(kt == KT - 1 and n == 2))
            if first + count == 8:
                m.then_inc(W.used, 1)
            return m

        def bc(ap, shape):
            return ap.broadcast_to(list(shape))

        def samples(ap):
            return ap[:, TP:T].rearrange("p (b s) -> p b s", b=NB)

        def padded(ap, first, count):
            return ap[:, SB0:SB0 + NB * SP].rearrange("p (b s) -> p b s", b=NB)[:, :, first:first + count]

        ctx0 = stack.enter_context(ExitStack())
        S = Sems()
        S.consts, S.x, S.c, S.silu, S.ones = sems(ctx0, "p0_consts", "p0_x", "p0_c", "p0_silu", "p0_ones")
        S.sq, S.sqpe, S.stat, S.wada0, S.wada1 = sems(ctx0, "p0_sq", "p0_sqpe", "p0_stat", "p0_wada0", "p0_wada1")
        S.mm, S.rows, S.tr, S.added = sems(ctx0, "p0_mm", "p0_rows", "p0_tr", "p0_added")
        at2 = [after]
        gcol = sb("gcol", [P, H, NTT], at=at2)
        sp16 = sb("sp16", [P, H], at=at2)
        p3at = at2[0]
        lam = sb("lam", [P, H], at=at2)
        headv = sb("headv", [P, 2], at=at2)
        big = [sb(f"big{n}", [P, T], at=at2) for n in range(6)]
        small = [sb(f"small{n}", [P, H], at=at2) for n in range(5)]
        rowT = sb("rowT", [P, 4, T], at=at2)
        at0 = [act_at]
        wada = sb("wada", [P, 2, KT, NBANK], at=at0)
        at0 = [at2[0]]
        xT = sb("xT", [P, KT, T], at=at0)
        rB = sb("rB", [P, T], at=at0)
        amod = sb("amod", [P, KT, NC], at=at0)
        tmp = sb("tmp", [P, 4, T], at=at0)
        arow = sb("arow", [P, 2, NBANK], at=at0)
        ct = sb("ct", [P, KT, NC], at=at0)
        cs = sb("cs", [P, KT, NC], at=at0)
        sq = sb("sq", [P, 2, T], at=at0)
        s_wada = [S.wada0, S.wada1]
        NGA = 6 * D // NBANK
        w_ada_v = a["w_ada"].rearrange("(k p) n -> p k n", p=P)

        with nc.Block() as block:
            @block.sync
            def _(sp):
                sp.dma_start(const[:, :], a["consts"]).then_inc(S.consts, 16)
                sp.dma_start(vecs[:, :], a["vecs"]).then_inc(S.consts, 16)
                sp.dma_start(ct[:, :, :], a["c_t"]).then_inc(S.c, 16)
                sp.dma_start(xT[:, :, :], a["x_t"]).then_inc(S.x, 16)

                def load(g, slot):
                    sp.dma_start(wada[:, slot], w_ada_v[:, :, bass.ds(g * NBANK, NBANK)]).then_inc(s_wada[slot], 16)

                load(0, 0)
                load(1, 1)
                with sp.Fori(1, NGA // 2) as i:
                    for s in range(2):
                        sp.wait_ge(S.mm, i * 2 + (s - 1))
                        load(i * 2 + s, s)
                for n in range(2):
                    load_half(sp, a["w_ba"][n], Nth(n))

            @block.gpsimd
            def _(pool):
                for n in range(2):
                    split_lo(pool, Nth(n))

            @block.scalar
            def _(act):
                ch = Chain(act, W.act_steps, act_total)
                act.wait_ge(S.c, 16)
                act.activation(cs[:, :, :], ct[:, :, :], ACT.Silu).then_inc(S.silu, 1)
                act.wait_ge(S.x, 16)
                for k in range(KT):
                    if k >= 2:
                        act.wait_ge(S.sqpe, k - 1)
                    act.activation(sq[:, k % 2, :], xT[:, k, :], ACT.Square).then_inc(S.sq, 1)
                act.wait_ge(S.ones, 3)
                act.wait_ge(S.stat, 1)
                for th in range(2):
                    ch(act.activation(rB[:, th * HT:(th + 1) * HT], dps[:, th, 0:HT], ACT.Ln, bias=eps[:, :],
                                      scale=1.0 / D))
                ch(act.activation(rB[:, :], rB[:, :], ACT.Exp, scale=-0.5))
                for n in range(2):
                    split_hi(act, Nth(n))

            @block.tensor
            def _(pe):
                pe.wait_ge(S.ones, 3)
                for k in range(KT):
                    pe.wait_ge(S.sq, k + 1)
                    for th in range(2):
                        m = pe.matmul(dps[:, th, 0:HT], ones[:, :], sq[:, k % 2, th * HT:(th + 1) * HT],
                                      start=(k == 0), stop=(k == KT - 1))
                    m.then_inc(S.sqpe, 1)
                pe.matmul(dps[:, 3, 0:1], ones[:, :], ones[:, 0:1], start=True, stop=True).then_inc(S.stat, 1)
                pe.wait_ge(S.silu, 1)
                pe.wait_ge(S.consts, 32)

                def products(g, slot, half):
                    pe.wait_ge(s_wada[slot], half)
                    if not (isinstance(g, int) and g < 2):
                        pe.wait_ge(S.rows, g - 1)
                    for k in range(KT):
                        m = pe.matmul(gps[0:NC, slot, :], cs[:, k, :], wada[:, slot, k, :],
                                      start=(k == 0), stop=(k == KT - 1))
                    m.then_inc(S.mm, 1)

                def turn(g, slot):
                    pe.wait_ge(S.rows, g + 1)
                    if not (isinstance(g, int) and g < 2):
                        pe.wait_ge(S.added, g - 1)
                    for c in range(4):
                        m = pe.transpose(gps[:, 2 + slot, c * P:(c + 1) * P],
                                         arow[:, slot, c * P:(c + 1) * P], ident)
                    m.then_inc(S.tr, 1)

                products(0, 0, 16)
                products(1, 1, 16)
                turn(0, 0)
                with pe.Fori(1, NGA // 2) as i:
                    products(i * 2, 0, i * 16 + 16)
                    turn(i * 2 - 1, 1)
                    products(i * 2 + 1, 1, i * 16 + 16)
                    turn(i * 2, 0)
                turn(NGA - 1, 1)

            @block.vector
            def _(dve):
                dve.memset(ones[:, :], 1.0).then_inc(S.ones, 1)
                dve.memset(eps[:, :], EPS).then_inc(S.ones, 1)
                dve.memset(arow[:, :, :], 0.0).then_inc(S.ones, 1)
                dve.wait_ge(S.ones, 3)
                dve.wait_ge(S.consts, 32)

                def copy_row(g, slot):
                    dve.wait_ge(S.mm, g + 1)
                    if not (isinstance(g, int) and g < 2):
                        dve.wait_ge(S.tr, g - 1)
                    dve.tensor_copy(arow[0:NC, slot, :], gps[0:NC, slot, :]).then_inc(S.rows, 1)

                def add_bias(g, slot):
                    dve.wait_ge(S.tr, g + 1)
                    turned = gps[:, 2 + slot, :].rearrange("p (c n) -> p c n", n=P)[:, :, 0:NC]
                    dve.tensor_tensor(modT[:, bass.ds(g * 4, 4), :], turned,
                                      bc(bada[:, bass.ds(g * 4, 4)].unsqueeze(2), [P, 4, NC]),
                                      ALU.add).then_inc(S.added, 1)

                copy_row(0, 0)
                copy_row(1, 1)
                add_bias(0, 0)
                with dve.Fori(1, NGA // 2) as i:
                    copy_row(i * 2, 0)
                    add_bias(i * 2 - 1, 1)
                    copy_row(i * 2 + 1, 1)
                    add_bias(i * 2, 0)
                add_bias(NGA - 1, 1)
                dve.wait_ge(S.added, NGA)

        M = Sems()
        M.h, M.hi, M.lo_dve, M.lo_pool = sems(stack, "mod_h", "mod_hi", "mod_lo_dve", "mod_lo_pool")
        M.scales, M.normed, M.prompt = sems(stack, "mod_scales", "mod_normed", "mod_prompt")

        def modulate(before, src, rstd, amod, tmp, weight, shift, scale):
            on_dve = [k for k in range(KT) if k % 3 != 0]

            def rest(eng, k):
                return eng.tensor_tensor(act_lo[:, k, :], tmp[:, k % 4, :], act_hi[:, k, :].bitcast(F32), ALU.subtract)

            def lo_count(k):
                mine = on_dve if k in on_dve else [j for j in range(KT) if j not in on_dve]
                done = len(on_dve) if k in on_dve else KT - len(on_dve)
                return (M.lo_dve if k in on_dve else M.lo_pool), before // KT * done + mine.index(k) + 1

            def dve_part(dve):
                ch = Chain(dve, W.dve_steps, dve_total)
                ch(dve.tensor_scalar(amod[:, :, :], modT[:, scale:scale + KT, :], 1.0, None, ALU.add))
                dve.tensor_tensor(amod[:, :, :], amod[:, :, :],
                                  bc(weight.unsqueeze(2), [P, KT, NC]), ALU.mult).then_inc(M.scales, 1)
                dve.wait_ge(M.scales, before // KT + 1)
                for k in range(KT + 2):
                    if k < KT:
                        t = tmp[:, k % 4, :]
                        if k >= 4:
                            dve.wait_ge(*lo_count(k - 4))
                        dve.tensor_tensor(t, src[:, k, :], rstd[:, :], ALU.mult).then_inc(M.normed, 1)
                        dve.wait_ge(M.normed, before + k + 1)
                        ch(dve.tensor_tensor(samples(t), samples(t),
                                             bc(amod[:, k, 1:NC].unsqueeze(2), [P, NB, NS]), ALU.mult))
                        dve.tensor_tensor(samples(t), samples(t), bc(modT[:, shift + k, 1:NC].unsqueeze(2), [P, NB, NS]),
                                          ALU.add).then_inc(M.h, 1)
                    if k - 2 in on_dve:
                        dve.wait_ge(M.hi, before + k - 1)
                        rest(dve, k - 2).then_inc(M.lo_dve, 1)

            def act_part(act):
                act.wait_ge(M.scales, before // KT + 1)
                for k in range(KT):
                    t = tmp[:, k % 4, :]
                    act.wait_ge(M.normed, before + k + 1)
                    act.activation(t[:, 0:TP], t[:, 0:TP], ACT.Identity, bias=modT[:, shift + k, 0:1],
                                   scale=amod[:, k, 0:1]).then_inc(M.prompt, 1)
                    act.wait_ge(M.prompt, before + k + 1)
                    act.wait_ge(M.h, before + k + 1)
                    act.copy(act_hi[:, k, :], t).then_inc(M.hi, 1)

            def pool_part(pool):
                for k in range(KT):
                    if k not in on_dve:
                        pool.wait_ge(M.hi, before + k + 1)
                        rest(pool, k).then_inc(M.lo_pool, 1)

            def pe_part(pe, k):
                pe.wait_ge(*lo_count(k))

            return dve_part, act_part, pool_part, pe_part

        first_h = modulate(0, xT, rB, amod, tmp, normw[0], 0, KT)

        with ExitStack() as c2:
            S = Sems()
            S.in_, S.mm, S.beta, S.araw, S.ea = sems(c2, "p2_in_", "p2_mm", "p2_beta", "p2_araw", "p2_ea")
            S.el, S.eg, S.rows, S.out, S.tr = sems(c2, "p2_el", "p2_eg", "p2_rows", "p2_out", "p2_tr")
            S.gsummed, S.alog, S.edl = sems(c2, "p2_gsummed", "p2_alog", "p2_edl")
            with nc.Block() as block:
                @block.sync
                def _(sp):
                    sp.dma_start(lam[:, :], a["lam_t"]).then_inc(S.in_, 16)
                    sp.dma_start(headv[0:H, :], a["head_v"]).then_inc(S.in_, 16)
                    for n in range(2 * AHEAD + 2):
                        load_half(sp, a["w_in"][n], Nth(2 + n))
                    sp.wait_ge(S.rows, 1)
                    sp.dma_start(rowsD, rowT[0:H, :, :]).then_inc(S.out, 16)
                    sp.wait_ge(S.out, 16)

                @block.gpsimd
                def _(pool):
                    first_h[2](pool)
                    for n in range(2 * AHEAD + 2):
                        split_lo(pool, Nth(2 + n))

                @block.tensor
                def _(pe):
                    for n in range(2):
                        m = gemm_part(pe, Nth(n), n, 1, 0, 8, first_h[3])
                    pe.matmul(dps[:, 3, 0:1], ones[:, :], ones[:, 0:1], start=True, stop=True).then_inc(S.mm, 1)
                    for tile in range(AHEAD):
                        if tile == 1:
                            pe.wait_ge(S.beta, 2)
                            pe.wait_ge(S.araw, 2)
                        for half in range(2):
                            gemm_part(pe, Nth(2 + 2 * tile + half), half, tile, 0, 8)
                    pe.wait_ge(S.gsummed, 1)
                    for t in range(NTT):
                        n = min(CH, T - t * CH)
                        m = pe.transpose(dps[0:n, 0, t * H:(t + 1) * H], rowT[0:H, 0, t * CH:t * CH + n],
                                         const[0:H, 0:H])
                    m.then_inc(S.tr, 1)

                @block.scalar
                def _(act):
                    ch = Chain(act, W.act_steps, act_total)
                    act.wait_ge(S.in_, 32)
                    first_h[1](act)
                    for n in range(2):
                        split_hi(act, Nth(2 + n))
                    act.activation(headv[0:H, 0:1], headv[0:H, 0:1], ACT.Exp).then_inc(S.alog, 1)
                    ch(act.activation(small[0][:, :], lam[:, :], ACT.Abs))
                    act.activation(small[0][:, :], small[0][:, :], ACT.Exp, scale=-1.0).then_inc(S.el, 1)
                    act.wait_ge(S.mm, 1)
                    for th in range(2):
                        cols = slice(th * HT, (th + 1) * HT)
                        act.activation(rowT[0:H, 1, cols], gps[0:H, 2 + th, 0:HT], ACT.Sigmoid).then_inc(S.beta, 1)
                        act.copy(big[0][0:H, cols], gps[32:32 + H, 2 + th, 0:HT]).then_inc(S.araw, 1)
                    for n in (4, 5):
                        split_hi(act, Nth(n))
                    act.wait_ge(S.ea, 1)
                    ch(act.activation(big[1][0:H, :], big[0][0:H, :], ACT.Abs))
                    act.activation(big[1][0:H, :], big[1][0:H, :], ACT.Exp, scale=-1.0).then_inc(S.ea, 1)
                    act.wait_ge(S.gsummed, 1)
                    act.activation(rowT[0:H, 2, :], rowT[0:H, 0, :], ACT.Exp).then_inc(S.eg, 1)
                    act.wait_ge(S.edl, 1)
                    ch(act.activation(rowT[0:H, 3, :], rowT[0:H, 3, :], ACT.Exp))
                    for n in range(6, 2 * AHEAD + 4):
                        split_hi(act, Nth(n))
                    act.wait_ge(S.eg, 1)
                    act.wait_ge(S.beta, 2)
                    act.activation(big[5][0:H, 0:1], rowT[0:H, 3, 0:1], ACT.Copy).then_inc(S.rows, 1)

                @block.vector
                def _(dve):
                    first_h[0](dve)
                    ch = Chain(dve, W.dve_steps, dve_total)

                    def log1p(e, s, s2, p, out):
                        ch(dve.tensor_scalar(s, e, 2.0, None, ALU.add))
                        ch(dve.reciprocal(s, s))
                        ch(dve.tensor_tensor(s, s, e, ALU.mult))
                        ch(dve.tensor_tensor(s2, s, s, ALU.mult))
                        ch(dve.tensor_scalar(p, s2, 1.0 / 17, None, ALU.mult))
                        for n in range(15, 1, -2):
                            ch(dve.scalar_tensor_tensor(p, p, 1.0 / n, s2, ALU.add, ALU.mult))
                        ch(dve.scalar_tensor_tensor(p, p, 1.0, s, ALU.add, ALU.mult))
                        ch(dve.tensor_scalar(out, p, 2.0, None, ALU.mult))

                    dve.wait_ge(S.in_, 32)
                    dve.wait_ge(S.el, 1)
                    s = [t[:, :] for t in small]
                    log1p(s[0], s[1], s[2], s[3], s[4])
                    ch(dve.tensor_scalar(s[1], lam[:, :], -1.0, 0.0, ALU.mult, ALU.max))
                    ch(dve.tensor_tensor(s[1], s[1], s[4], ALU.add))
                    ch(dve.tensor_scalar(sp16[:, :], s[1], 16.0, None, ALU.mult))
                    dve.wait_ge(S.araw, 2)
                    b = [t[0:H, :] for t in big]
                    dve.tensor_scalar(b[0], b[0], headv[0:H, 1:2], None, ALU.add).then_inc(S.ea, 1)
                    dve.wait_ge(S.ea, 2)
                    log1p(b[1], b[2], b[3], b[4], b[5])
                    ch(dve.scalar_tensor_tensor(b[1], b[0], 0.0, b[5], ALU.max, ALU.add))
                    dve.wait_ge(S.alog, 1)
                    ch(dve.tensor_scalar(b[1], b[1], headv[0:H, 0:1], -1.0, ALU.mult, ALU.mult))
                    ch(dve.memset(b[2], 1.0))
                    ch(dve.memset(b[2][:, 0:TP].rearrange("p (c t) -> p c t", t=CH)[:, :, 0:1], 0.0))
                    ch(dve.memset(samples(b[2])[:, :, 0:1], 0.0))
                    dve.tensor_tensor_scan(rowT[0:H, 0, :], b[2], b[1], 0.0, ALU.mult, ALU.add).then_inc(S.gsummed, 1)
                    dve.wait_ge(S.gsummed, 1)
                    for src, out, w in ((rowT[0:H, 0, 0:TP], rowT[0:H, 3, 0:TP], CH),
                                        (rowT[0:H, 0, TP:T], rowT[0:H, 3, TP:T], NS)):
                        v = src.rearrange("p (c t) -> p c t", t=w)
                        ch(dve.tensor_tensor(out.rearrange("p (c t) -> p c t", t=w),
                                             bc(v[:, :, w - 1:w], v.shape), v, ALU.subtract))
                    dve.engine_nop().then_inc(S.edl, 1)
                    dve.wait_ge(S.tr, 1)
                    ch(dve.memset(gcol[:, :, :], 0.0))
                    ch(dve.tensor_copy(gcol[:, :, 0:NCH].rearrange("p h t -> p t h"),
                                       dps[:, 0, 0:NCH * H].rearrange("p (t h) -> p t h", h=H)))
                    ch(dve.tensor_copy(gcol[0:TS, :, NCH], dps[0:TS, 0, NCH * H:NTT * H]))

        at3 = [p3at]
        rows = sb("rows", [P, 4, T], at=at3)
        pack = sb("pack", [P, PACK], at=at3)
        pads = sb("pads", [P, 2, PADW], at=at3)
        qkvz = sb("qkvz", [P, 4, T], at=at3)
        gy = sb("gy", [P, T], at=at3)
        xc, ry, iu, la, e2, em = (sb(n, [P, PADW], at=at3) for n in ("xc", "ry", "iu", "la", "e2", "em"))
        convs = sb("convs", [P, 4, NC, PL], at=at3)
        hlast = sb("hlast", [P, NC], at=at3)
        sqs = sb("sqs", [P, 2, T], at=at3)
        kb = sb("kb", [P, T], at=at3)
        nkeg = sb("nkeg", [P, T], at=at3)
        qg = sb("qg", [P, T], at=at3)
        kgd = sb("kgd", [P, T], at=at3)
        nkq = sb("nkq", [P, NB, 2, NS], at=at3)
        eglast = sb("eglast", [P, NCH + NB], at=at3)
        dec = sb("dec", [P, NCH + 1, CH], at=at3)
        lt = sb("lt", [P, T], at=at3)
        att = sb("att", [P, T], at=at3)
        ktok = sb("ktok", [P, NTT, P], at=at3)
        tm = sb("tm", [P, T], at=at3)
        qm = sb("qm", [P, T], at=at3)
        um = sb("um", [P, NTT * P], at=at3)
        vmask = sb("vmask", [P, NB, P], at=at3)
        st = sb("st", [P, P], at=at3)
        sst = sb("sst", [P, NB, P], at=at3)
        rs = sb("rs", [P, 2, P], at=at3)
        vn = sb("vn", [P, 2, P], at=at3)
        rst = sb("rst", [P, P], at=at3)
        qc, kc, vc, zc = (qkvz[:, n, :] for n in range(4))
        lmask = sb("lmask", [P, NCH + 1, CH], at=at3)

        N4 = 2 + 12 * H
        MIXES = 5
        mixin = sb("mixin", [P, KT, T], at=[after - KT * T * 4])
        with ExitStack() as c3:
            S = Sems()
            S.mix, S.mixhi, S.mixlo, S.mixlast = sems(c3, "p3_mix", "p3_mixhi", "p3_mixlo", "p3_mixlast")
            S.pack, S.evx, S.convx, S.gr, S.gi = sems(c3, "p3_pack", "p3_evx", "p3_convx", "p3_gr", "p3_gi")
            S.sigr, S.sigi, S.gely, S.lruexp, S.ydone = \
                sems(c3, "p3_sigr", "p3_sigi", "p3_gely", "p3_lruexp", "p3_ydone")
            S.emdone, S.sqrt, S.scan, S.lruout, S.lrust = \
                sems(c3, "p3_emdone", "p3_sqrt", "p3_scan", "p3_lruout", "p3_lrust")
            S.evq, S.evk, S.evv, S.evz, S.cvq = sems(c3, "p3_evq", "p3_evk", "p3_evv", "p3_evz", "p3_cvq")
            S.cvk, S.cvv, S.slq = sems(c3, "p3_cvk", "p3_cvv", "p3_slq")
            S.rowsl, S.sq, S.nrm, S.invn, S.prod = sems(c3, "p3_rowsl", "p3_sq", "p3_nrm", "p3_invn", "p3_prod")
            S.gram, S.mind, S.expd, S.ktk, S.uinit = sems(c3, "p3_gram", "p3_mind", "p3_expd", "p3_ktk", "p3_uinit")
            S.tini, S.tcop, S.lm, S.qlev, S.qcop = sems(c3, "p3_tini", "p3_tcop", "p3_lm", "p3_qlev", "p3_qcop")
            S.dlev, S.upd, S.xs, S.rts, S.rtt = sems(c3, "p3_dlev", "p3_upd", "p3_xs", "p3_rts", "p3_rtt")
            S.rcs, S.vsm, S.vms, S.ats, S.oss = sems(c3, "p3_rcs", "p3_vsm", "p3_vms", "p3_ats", "p3_oss")
            S.dss0, S.dss1, S.sup0, S.sup1, S.rp = sems(c3, "p3_dss0", "p3_dss1", "p3_sup0", "p3_sup1", "p3_rp")
            S.rcp, S.vp, S.vcp, S.op, S.sup = sems(c3, "p3_rcp", "p3_vp", "p3_vcp", "p3_op", "p3_sup")
            S.ocp, S.osq, S.onrm, S.oinv, S.oout = sems(c3, "p3_ocp", "p3_osq", "p3_onrm", "p3_oinv", "p3_oout")
            S.sload, S.stcl, S.o_out, S.st_out, S.sst_out = \
                sems(c3, "p3_sload", "p3_stcl", "p3_o_out", "p3_st_out", "p3_sst_out")
            S.conv_out, = sems(c3, "p3_conv_out")
            NL = LEVELS - 1
            SLOTS = 48

            def do_turns(eng, body, sem=None, total=None, steps=0):
                ch = Chain(eng, sem, total or [0])
                body(0, None, ch)
                with eng.Fori(1, H - 1) as i:
                    ch.enter(i - 1, steps)
                    body(i, i - 1, ch)
                ch.leave(H - 2)
                body(H - 1, H - 2, ch)
                body(None, H - 1, ch)

            def head_half(h, j):
                return Nth(2 + 12 * h + j) if isinstance(h, int) else Nth(2 + j, h, 12)

            def prefetched(h, j):
                return isinstance(h, int) and h == 0 and j < 2 * AHEAD + 2

            with nc.Block() as block:
                @block.sync
                def _(sp):
                    def body(h, g, ch):
                        A, B = h is not None, g is not None
                        for j in range(12):
                            if j == 2 and A:
                                if not isinstance(h, int) or h:
                                    sp.wait_ge(S.cvv, h)
                                    sp.wait_ge(S.scan, h)
                                sp.dma_start(pack[:, :], row(a["pack"], h)).then_inc(S.pack, 16)
                            if j == 1 and B:
                                sp.wait_ge(S.sst_out, g * 16 + 16)
                                sp.dma_start(sst[:, :, :], a["dn_s"][:, bass.ds(g, 1)].rearrange(
                                    "b h p v -> p (b h) v")).then_inc(S.sload, 16)
                            if A and not prefetched(h, j):
                                load_half(sp, row(a["w_in"], h * 12 + j), head_half(h, j))
                            if j == 9 and A:
                                sp.wait_ge(S.lruout, h + 1)
                                sp.dma_start(row(mixD, h), gy[:, :]).then_inc(S.lrust, 16)
                                sp.dma_start(row(a["lru_h_t"], h), hlast[:, :]).then_inc(S.lrust, 16)
                                if B:
                                    sp.wait_ge(S.prod, g + 1)
                                r = rowsD[h:h + 1] if isinstance(h, int) else rowsD[bass.ds(h, 1)]
                                sp.dma_start(rows[:, :, :].rearrange("p r t -> p (r t)"),
                                             r.rearrange("h r t -> h (r t)").broadcast_to([P, 4 * T])
                                             ).then_inc(S.rowsl, 16)

                    do_turns(sp, body)
                    sp.wait_ge(W.used, N4)
                    sp.wait_ge(S.lrust, 32 * H)
                    sp.wait_ge(S.o_out, 16 * H)
                    for k in range(0, KT - 1, MIXES):
                        sp.dma_start(mixin[:, k:k + MIXES, :], mixD[k:k + MIXES].rearrange("k p t -> p k t")
                                     ).then_inc(S.mix, 16)
                        sp.wait_ge(S.mix, 16 * (k // MIXES + 1))
                    for n in range(2):
                        load_half(sp, a["w_out"][n], Nth(N4 + n))

                @block.gpsimd
                def _(pool):
                    def body(h, g, ch):
                        if h is not None:
                            for j in range(12):
                                if not prefetched(h, j):
                                    split_lo(pool, head_half(h, j))

                    do_turns(pool, body)
                    for k in range(KT - 1):
                        pool.wait_ge(S.mix, 16 * (k // MIXES + 1))
                        pool.tensor_copy(act_hi[:, k, :], mixin[:, k, :]).then_inc(S.mixhi, 1)
                        pool.wait_ge(S.mixhi, k + 1)
                        pool.tensor_tensor(act_lo[:, k, :], mixin[:, k, :], act_hi[:, k, :].bitcast(F32),
                                           ALU.subtract).then_inc(S.mixlo, 1)
                    for n in range(2):
                        k = Nth(N4 + n)
                        pool.wait_ge(w_loaded[k.raw], k.loads())
                        pool.wait_ge(W.used, k.n - 3)
                        pool.tensor_copy(whi[:, k.slot, :], raw[:, k.raw, :]).then_inc(W.hi, 1)
                        split_lo(pool, k)

                @block.tensor
                def _(pe):
                    def body(h, g, ch):
                        A, B = h is not None, g is not None
                        later = not isinstance(h, int) or h > 0
                        for e in range(SLOTS):
                            tile, part = e // 8, e % 8
                            pair = tile % 2
                            if A:
                                if part == 0:
                                    if tile < 2:
                                        if not isinstance(h, int) or h:
                                            pe.wait_ge((S.evv, S.evz)[tile], h)
                                    else:
                                        pe.wait_ge((S.sigr, S.sigi, S.evq, S.evk)[tile - 2], h + 1)
                                if later or tile >= AHEAD:
                                    gemm_part(pe, head_half(h, tile * 2 + part // 4), part // 4, pair, part % 4 * 2, 2)
                            if e == 3 and B:
                                pe.wait_ge(S.sq, g + 1)
                                for n in range(2):
                                    for th in range(2):
                                        m = pe.matmul(dps[:, 2 * n + th, 0:HT], ones[:, :],
                                                      sqs[:, n, th * HT:(th + 1) * HT], start=True, stop=True)
                                m.then_inc(S.nrm, 1)
                            if e == 9 and B:
                                pe.wait_ge(S.prod, g + 1)
                                for t in range(NTT):
                                    n = CH if t < NCH else TS
                                    c = slice(t * CH, t * CH + n)
                                    o = (dps[:, 0, c], dps[:, 1, c], dps[:, 3, c]) if t < NCH else (
                                        dps[0:TS, 2, 0:TS], dps[0:TS, 2, TS:2 * TS], dps[0:TS, 2, 2 * TS:2 * TS + P])
                                    pe.matmul(o[0], kc[:, c], kb[:, c], start=True, stop=True)
                                    pe.matmul(o[1], kc[:, c], qc[:, c], start=True, stop=True)
                                    m = pe.transpose(o[2], kgd[:, c], ident)
                                m.then_inc(S.gram, 1)
                            if e == 14 and A:
                                pe.wait_ge(S.convx, h + 1)
                                pe.wait_ge(S.evx, h + 1)
                                for th in range(2):
                                    m = pe.matmul(gps[:, th, 0:CONVW // 2], pack[:, 116:244],
                                                  xc[:, th * (CONVW // 2):(th + 1) * (CONVW // 2)], start=True, stop=True)
                                m.then_inc(S.gr, 1)
                            if e == 12 and B:
                                pe.wait_ge(S.uinit, g + 1)
                                pe.wait_ge(S.ktk, g + 1)
                                for t in range(NCH):
                                    c = slice(t * CH, (t + 1) * CH)
                                    pe.transpose(dps[:, 0, c], um[:, c], ident)
                                pe.transpose(dps[0:TS, 3, 0:TS], um[0:TS, TP:T], const[0:TS, 0:TS]).then_inc(S.tini, 1)
                            if e == 13 and B:
                                pe.wait_ge(S.sload, g * 16 + 16)
                                pe.wait_ge(S.tcop, g + 1)
                                for b in range(NB):
                                    m = pe.matmul(dps[:, 3, 192 + b * 16:192 + (b + 1) * 16], sst[:, b, :],
                                                  nkq[:, b, :, :], start=True, stop=True)
                                m.then_inc(S.xs, 1)
                            for l in range(1, LEVELS):
                                if e == 12 + 3 * (l - 1) + 2 and B:
                                    pe.wait_ge(S.lm, g * (LEVELS - 1) + l)
                                    if l == 1:
                                        pe.wait_ge(S.rts, g + 1)
                                    else:
                                        pe.wait_ge(S.upd, g * (LEVELS - 1) + l - 1)
                                    for t in range(NCH + (l < 3)):
                                        n, c = (CH, slice(t * CH, (t + 1) * CH)) if t < NCH else (TS, slice(TP, T))
                                        o = dps[:, 0, c] if t < NCH else dps[0:TS, 3, 0:TS]
                                        m = pe.matmul(o, lmask[0:n, t, 0:n], tm[0:n, c], start=True, stop=True)
                                    m.then_inc(S.qlev, 1)
                                if e == 12 + 3 * (l - 1) + 3 and B:
                                    pe.wait_ge(S.qcop, g * (LEVELS - 1) + l)
                                    for t in range(NCH + (l < 3)):
                                        n, c = (CH, slice(t * CH, (t + 1) * CH)) if t < NCH else (TS, slice(TP, T))
                                        o = (dps[:, 1, c], dps[:, 2, c]) if t < NCH else (
                                            dps[0:TS, 3, TS:2 * TS], dps[0:TS, 3, 2 * TS:3 * TS])
                                        if l < LEVELS - 1:
                                            pe.matmul(o[0], um[0:n, c], qm[0:n, c], start=True, stop=True)
                                        m = pe.matmul(o[1], qm[0:n, c], um[0:n, c], start=True, stop=True)
                                    m.then_inc(S.dlev, 1)
                            if e == 18 and A:
                                pe.wait_ge(S.gely, h + 1)
                                for th in range(2):
                                    m = pe.matmul(gps[:, 2 + th, 0:CONVW // 2], pack[:, 244:372],
                                                  xc[:, th * (CONVW // 2):(th + 1) * (CONVW // 2)], start=True, stop=True)
                                m.then_inc(S.gi, 1)
                            if e == 19 and B:
                                pe.wait_ge(S.upd, g * NL + 2)
                                pe.transpose(dps[:, 3, 320:320 + P], rst[:, :], ident).then_inc(S.rtt, 1)
                            if e == 22 and B:
                                pe.wait_ge(S.rcs, g + 1)
                                pe.wait_ge(S.upd, g * (LEVELS - 1) + 2)
                                pe.matmul(dps[:, 3, 192:192 + P], um[0:TS, TP:TP + P], rs[0:TS, 1, :], start=True,
                                          stop=True).then_inc(S.vsm, 1)
                            if e == 25 and B:
                                pe.wait_ge(S.vms, g + 1)
                                pe.matmul(dps[:, 3, 448:512], vn[0:TS, 1, :], att[0:TS, TP:T], start=True,
                                          stop=True).then_inc(S.ats, 1)
                            for t in range(NCH):
                                if e == 31 + 4 * t and B:
                                    c = slice(t * CH, (t + 1) * CH)
                                    pe.matmul(dps[:, 0, 0:P], vc[:, c], ident, start=True, stop=False)
                                    pe.wait_ge(S.stcl if t == 0 else S.sup, g + 1 if t == 0 else g * NCH + t)
                                    pe.matmul(dps[:, 0, 0:P], nkeg[:, c], st[:, :], start=False,
                                              stop=True).then_inc(S.rp, 1)
                                if e == 32 + 4 * t and B:
                                    pe.wait_ge(S.rcp, g * NCH + t + 1)
                                    c = slice(t * CH, (t + 1) * CH)
                                    if t == 0:
                                        pe.wait_ge(S.upd, g * (LEVELS - 1) + LEVELS - 1)
                                    pe.matmul(dps[:, 1, 0:P], um[:, c], rs[:, 0, :], start=True,
                                              stop=True).then_inc(S.vp, 1)
                                if e == 33 + 4 * t and B:
                                    pe.wait_ge(S.vcp, g * NCH + t + 1)
                                    c = slice(t * CH, (t + 1) * CH)
                                    pe.matmul(dps[:, 2, c], st[:, :], qg[:, c], start=True, stop=False)
                                    pe.matmul(dps[:, 2, c], vn[:, 0, :], att[:, c], start=False, stop=True)
                                    if t == 0:
                                        pe.wait_ge(S.sup1, g + 1)
                                    pe.matmul(dps[:, 3, 0:P], ktok[:, t, :], vn[:, 0, :], start=True,
                                              stop=True).then_inc(S.op, 1)
                            for n, e_n in ((0, 27), (1, 29)):
                                if e == e_n and B:
                                    if n == 0:
                                        pe.wait_ge(S.oss, g + 1)
                                    else:
                                        pe.wait_ge(S.sup0, g + 1)
                                    pe.matmul(dps[:, 3, :], ktok[0:TS, NCH, :], vmask[0:TS, n * 4:n * 4 + 4, :],
                                              start=True, stop=True).then_inc((S.dss0, S.dss1)[n], 1)
                            if e == 46 and B:
                                pe.wait_ge(S.osq, g + 1)
                                pe.wait_ge(S.sup, g * NCH + NCH)
                                for th in range(2):
                                    m = pe.matmul(dps[:, th, 0:HT], ones[:, :], sqs[:, 0, th * HT:(th + 1) * HT],
                                                  start=True, stop=True)
                                m.then_inc(S.onrm, 1)

                    do_turns(pe, body)

                @block.scalar
                def _(act):
                    def split(h, j):
                        split_hi(act, head_half(h, j))

                    def body(h, g, ch):
                        A, B = h is not None, g is not None
                        later = not isinstance(h, int) or h > 0
                        last = isinstance(h, int) and h == H - 1

                        def tile_done(tile):
                            act.wait_ge(W.used, head_half(h, 2 * tile + 1).n + 1)

                        def evacuate(tile, n, before, done):
                            tile_done(tile)
                            if before is not None:
                                act.wait_ge(*before)
                            pr = 2 * (tile % 2)
                            ch(act.copy(pads[:, n, PL:PL + HT], gps[:, pr, 0:HT]))
                            ch(act.copy(pads[:, n, PL + HT:PL + TP], gps[:, pr + 1, 0:TP - HT]))
                            act.copy(padded(pads[:, n, :], PL, NS),
                                     gps[:, pr + 1, TP - HT:HT].rearrange("p (b s) -> p b s", b=NB)).then_inc(done, 1)

                        def silu(src, n, conv, done=None):
                            act.wait_ge(conv, h + 1)
                            if B:
                                act.wait_ge(S.gram if n < 2 else S.rp, g + 1 if n < 2 else g * NCH + NCH)
                            ch(act.activation(qkvz[:, n, 0:TP], src[:, 0:TP], ACT.Silu))
                            m = act.activation(samples(qkvz[:, n, :]), padded(src, 0, NS), ACT.Silu)
                            if done:
                                m.then_inc(done, 1)

                        for e in range(SLOTS):
                            if e == 0 and B:
                                ch(act.activation(sqs[:, 0, :], qc, ACT.Square))
                                act.activation(sqs[:, 1, :], kc, ACT.Square).then_inc(S.sq, 1)
                            if A and e % 4 == 0 and not (last and e >= 40) and not prefetched(h, e // 4 + 2):
                                split(h, e // 4 + 2)
                            if e == 3 and B:
                                act.wait_ge(S.nrm, g + 1)
                                for n in range(2):
                                    for th in range(2):
                                        ch(act.activation(sqs[:, n, th * HT:(th + 1) * HT], dps[:, 2 * n + th, 0:HT],
                                                          ACT.Ln, bias=eps[:, :]))
                                act.activation(sqs[:, :, :], sqs[:, :, :], ACT.Exp, scale=-0.5).then_inc(S.invn, 1)
                            if e == 6 and B:
                                act.wait_ge(S.mind, g + 1)
                                ch(act.activation(dec[:, 0:NCH, :], dec[:, 0:NCH, :], ACT.Exp))
                                act.activation(dec[0:TS, NCH, 0:TS], dec[0:TS, NCH, 0:TS], ACT.Exp).then_inc(S.expd, 1)
                            if e == 8 and A:
                                evacuate(0, 0, (S.cvk, h) if later else None, S.evx)
                            if e == 9 and B:
                                act.wait_ge(S.gram, g + 1)
                                act.copy(ktok[:, 0:NCH, :], dps[:, 3, :].rearrange("p (t d) -> p t d", d=P)
                                         ).then_inc(S.ktk, 1)
                            if e == 12 and B:
                                act.wait_ge(S.tini, g + 1)
                                ch(act.copy(tm[:, 0:TP], dps[:, 0, :]))
                                act.copy(tm[0:TS, TP:T], dps[0:TS, 3, 0:TS]).then_inc(S.tcop, 1)
                            if e == 13 and A:
                                act.wait_ge(S.gr, h + 1)
                                if later:
                                    act.wait_ge(S.lruout, h)
                                for th in range(2):
                                    c = slice(th * (CONVW // 2), (th + 1) * (CONVW // 2))
                                    m = act.activation(ry[:, c], gps[:, th, 0:CONVW // 2], ACT.Sigmoid, bias=pack[:, 17:18])
                                    if th == 0:
                                        ch(m)
                                m.then_inc(S.sigr, 1)
                            for l in range(1, LEVELS):
                                if e == 11 + 3 * l and B:
                                    act.wait_ge(S.qlev, g * NL + l)
                                    if l < 3:
                                        ch(act.copy(qm[0:TS, TP:T], dps[0:TS, 3, 0:TS]))
                                    act.copy(qm[:, 0:TP], dps[:, 0, :]).then_inc(S.qcop, 1)
                            if e == 16 and A:
                                tile_done(1)
                                if later:
                                    act.wait_ge(S.lrust, h * 32)
                                ch(act.activation(gy[:, 0:HT], gps[:, 2, 0:HT], ACT.Gelu_apprx_tanh))
                                act.activation(gy[:, HT:T], gps[:, 3, 0:HT], ACT.Gelu_apprx_tanh).then_inc(S.gely, 1)
                            if e == 17 and A:
                                act.wait_ge(S.ydone, h + 1)
                                ch(act.activation(la[:, 0:CONVW], ry[:, 0:CONVW], ACT.Exp, scale=-0.5))
                                act.activation(e2[:, 0:CONVW], ry[:, 0:CONVW], ACT.Exp, scale=-1.0).then_inc(S.lruexp, 1)
                            if e == 22 and A:
                                act.wait_ge(S.emdone, h + 1)
                                act.activation(em[:, 0:CONVW], em[:, 0:CONVW], ACT.Sqrt).then_inc(S.sqrt, 1)
                                act.wait_ge(S.gi, h + 1)
                                for th in range(2):
                                    c = slice(th * (CONVW // 2), (th + 1) * (CONVW // 2))
                                    m = act.activation(iu[:, c], gps[:, 2 + th, 0:CONVW // 2], ACT.Sigmoid,
                                                       bias=pack[:, 18:19])
                                    if th == 0:
                                        ch(m)
                                m.then_inc(S.sigi, 1)
                            if e == 20 and B:
                                act.wait_ge(S.rtt, g + 1)
                                act.copy(rs[0:TS, 1, :], dps[0:TS, 3, 320:320 + P]).then_inc(S.rcs, 1)
                            if e == 24 and A:
                                evacuate(2, 1, (S.cvv, h) if later else None, S.evq)
                            if e == 28 and A:
                                silu(e2, 0, S.cvq, S.slq)
                            if e == 32 and A:
                                evacuate(3, 0, (S.convx, h + 1), S.evk)
                            if e == 37 and A:
                                silu(em, 1, S.cvk)
                            if e == 40 and A:
                                evacuate(4, 1, (S.cvq, h + 1), S.evv)
                            for t in range(NCH):
                                if e == 31 + 4 * t and B:
                                    act.wait_ge(S.rp, g * NCH + t + 1)
                                    act.copy(rs[:, 0, :], dps[:, 0, 0:P]).then_inc(S.rcp, 1)
                            if e == 31 and B:
                                act.wait_ge(S.sup1, g + 1)
                                act.dma_start(a["s_sample"][:, bass.ds(g, 1)].rearrange("b h p v -> p (b h) v"),
                                              sst[:, :, :]).then_inc(S.sst_out, 16)
                            if e == 45 and B:
                                act.wait_ge(S.op, g * NCH + NCH)
                                act.copy(kb[:, 0:TP], dps[:, 2, :]).then_inc(S.ocp, 1)
                                act.wait_ge(S.ocp, g + 1)
                                act.wait_ge(S.oss, g + 1)
                                act.activation(sqs[:, 0, :], kb[:, :], ACT.Square).then_inc(S.osq, 1)
                            if e == 47 and B:
                                act.wait_ge(S.onrm, g + 1)
                                for th in range(2):
                                    ch(act.activation(sqs[:, 1, th * HT:(th + 1) * HT], dps[:, th, 0:HT], ACT.Ln,
                                                      bias=eps[:, :], scale=1.0 / P))
                                act.activation(sqs[:, 1, :], sqs[:, 1, :], ACT.Exp, scale=-0.5).then_inc(S.oinv, 1)
                            if e == 47 and A:
                                silu(e2, 2, S.cvv)
                        if B:
                            act.wait_ge(S.sup, g * NCH + NCH)
                            act.dma_start(row(a["s_prompt"], g), st[:, :]).then_inc(S.st_out, 16)
                            act.wait_ge(S.oout, g + 1)
                            out = mixD[H + g] if isinstance(g, int) else row(mixD, g + H)
                            act.dma_start(out, kb[:, :]).then_inc(S.o_out, 16)
                        if A:
                            act.wait_ge(S.cvv, h + 1)
                            act.dma_start(row(a["conv_t"], h), convs[:, :, :, :].rearrange("p a b c -> p (a b c)")
                                          ).then_inc(S.conv_out, 16)
                            tile_done(5)
                            ch(act.activation(zc[:, 0:HT], gps[:, 2, 0:HT], ACT.Silu))
                            act.activation(zc[:, HT:T], gps[:, 3, 0:HT], ACT.Silu).then_inc(S.evz, 1)

                    do_turns(act, body, W.act_steps, act_total, ACT_STEPS_A_TURN)
                    act.copy(act_hi[:, KT - 1, :], kb[:, :]).then_inc(S.mixlast, 1)
                    act.wait_ge(S.lrust, 32 * H)
                    act.wait_ge(S.st_out, 16 * H + 16)
                    act.wait_ge(S.o_out, 16 * H + 16)
                    act.wait_ge(S.sst_out, 16 * H + 16)
                    act.wait_ge(S.conv_out, 16 * H)

                @block.vector
                def _(dve):
                    tt, ts, stt = dve.tensor_tensor, dve.tensor_scalar, dve.scalar_tensor_tensor
                    for s_ in (S.o_out, S.st_out, S.sst_out):
                        dve.engine_nop().then_inc(s_, 16)

                    def tiles4(ap):
                        return ap.rearrange("p (t i) -> p t i", i=CH)

                    def over4(m):
                        return bc(m.unsqueeze(1), [P, NCH, CH])

                    def body(h, g, ch):
                        A, B = h is not None, g is not None
                        later = not isinstance(h, int) or h > 0
                        if A and not later:
                            ch(dve.memset(pads[:, :, 0:PL], 0.0))
                            ch(dve.memset(rst[:, TS:P], 0.0))
                            ch(dve.memset(um[:, T:NTT * P], 0.0))

                        def conv(n, pad, out, ready, done, bias=None):
                            src = pads[:, pad, :]
                            dve.wait_ge(ready, h + 1)
                            if n == 3:
                                dve.wait_ge(S.pack, h * 16 + 16)
                                if later:
                                    dve.wait_ge(S.conv_out, h * 16)
                            ch(dve.tensor_copy(padded(src, 0, PL), pack[:, 20 + n * 24:44 + n * 24].rearrange(
                                "p (b k) -> p b k", k=PL)))
                            ch(dve.tensor_copy(convs[:, n, 0, :], src[:, TP:TP + PL]))
                            ch(dve.tensor_copy(convs[:, n, 1:NC, :], padded(src, NS, PL)))
                            w = [pack[:, n * CW + k:n * CW + k + 1] for k in range(CW)]
                            if bias is None:
                                ch(ts(out[:, 0:CONVW], src[:, 0:CONVW], w[0], None, ALU.mult))
                            else:
                                ch(ts(out[:, 0:CONVW], src[:, 0:CONVW], w[0], bias, ALU.mult, ALU.add))
                            for k in range(1, CW):
                                m = stt(out[:, 0:CONVW], src[:, k:k + CONVW], w[k], out[:, 0:CONVW], ALU.mult, ALU.add)
                                if k < CW - 1:
                                    ch(m)
                            m.then_inc(done, 1)
                            dve.wait_ge(done, h + 1)

                        for e in range(SLOTS):
                            if e == 3 and B:
                                dve.wait_ge(S.rowsl, g * 16 + 16)
                                for t in range(NCH):
                                    ch(ts(dec[:, t, :], rows[:, 0, t * CH:(t + 1) * CH], gcol[:, bass.ds(g, 1), t],
                                          0.0, ALU.subtract, ALU.min))
                                ts(dec[0:TS, NCH, 0:TS], rows[0:TS, 0, TP:T], gcol[0:TS, bass.ds(g, 1), NCH],
                                   0.0, ALU.subtract, ALU.min).then_inc(S.mind, 1)
                                eg = rows[:, 2, :]
                                ch(dve.tensor_copy(eglast[:, 0:NCH], tiles4(eg[:, 0:TP])[:, :, CH - 1]))
                                ch(dve.tensor_copy(eglast[:, NCH:], samples(eg)[:, :, NS - 1]))
                                dve.wait_ge(S.invn, g + 1)
                                dve.wait_ge(S.o_out, g * 16 + 16)
                                ch(tt(kc, kc, sqs[:, 1, :], ALU.mult))
                                ch(stt(qc, qc, float(P) ** -0.5, sqs[:, 0, :], ALU.mult, ALU.mult))
                                ch(tt(kb[:, :], kc, rows[:, 1, :], ALU.mult))
                                ch(tt(vc, vc, rows[:, 1, :], ALU.mult))
                                ch(stt(nkeg[:, :], kb[:, :], -1.0, eg, ALU.mult, ALU.mult))
                                ch(tt(qg[:, :], qc, eg, ALU.mult))
                                ch(dve.tensor_copy(nkq[:, :, 0, :], samples(nkeg)))
                                ch(dve.tensor_copy(nkq[:, :, 1, :], samples(qg)))
                                tt(kgd[:, :], kc, rows[:, 3, :], ALU.mult).then_inc(S.prod, 1)
                                dve.wait_ge(S.prod, g + 1)
                                dve.wait_ge(S.st_out, g * 16 + 16)
                                dve.memset(st[:, :], 0.0).then_inc(S.stcl, 1)
                                dve.wait_ge(S.stcl, g + 1)
                            if e == 7 and B:
                                dve.wait_ge(S.expd, g + 1)
                                ch(tt(dec[:, 0:NCH, :], dec[:, 0:NCH, :], over4(const[:, C_INCL:C_INCL + CH]), ALU.mult))
                                ch(tt(dec[0:TS, NCH, 0:TS], dec[0:TS, NCH, 0:TS], const[0:TS, C_SINCL:C_SINCL + TS],
                                      ALU.mult))
                            if e == 9 and B:
                                dve.wait_ge(S.gram, g + 1)
                                d4, ds_ = dec[:, 0:NCH, :], dec[0:TS, NCH, 0:TS]
                                ch(tt(tiles4(lt[:, 0:TP]), tiles4(dps[:, 0, :]), d4, ALU.mult))
                                ch(tt(lt[0:TS, TP:T], dps[0:TS, 2, 0:TS], ds_, ALU.mult))
                                ch(tt(tiles4(um[:, 0:TP]), tiles4(lt[:, 0:TP]), over4(const[:, C_LEVEL:C_LEVEL + P]), ALU.mult))
                                ch(tt(um[0:TS, TP:T], lt[0:TS, TP:T], const[0:TS, C_LEVEL:C_LEVEL + TS], ALU.mult))
                                ch(tt(tiles4(um[:, 0:TP]), over4(ident), tiles4(um[:, 0:TP]), ALU.subtract))
                                tt(um[0:TS, TP:T], const[0:TS, 0:TS], um[0:TS, TP:T], ALU.subtract).then_inc(S.uinit, 1)
                            for l in range(1, LEVELS):
                                if e == 9 + 3 * l and B and l > 1 or e == 9 and B and l == 1:
                                    if l > 1:
                                        dve.wait_ge(S.dlev, g * NL + l - 1)
                                        if l - 1 < 3:
                                            ch(tt(um[0:TS, TP:T], um[0:TS, TP:T], dps[0:TS, 3, 2 * TS:3 * TS], ALU.subtract))
                                            ch(tt(tm[0:TS, TP:T], tm[0:TS, TP:T], dps[0:TS, 3, TS:2 * TS], ALU.subtract))
                                        ch(tt(um[:, 0:TP], um[:, 0:TP], dps[:, 2, :], ALU.subtract))
                                        tt(tm[:, 0:TP], tm[:, 0:TP], dps[:, 1, :], ALU.subtract).then_inc(S.upd, 1)
                                        dve.wait_ge(S.upd, g * NL + l - 1)
                                    m = const[:, C_LEVEL + l * P:C_LEVEL + (l + 1) * P]
                                    if l < 3:
                                        ch(tt(lmask[0:TS, NCH, 0:TS], lt[0:TS, TP:T], m[0:TS, 0:TS], ALU.mult))
                                    tt(lmask[:, 0:NCH, :], tiles4(lt[:, 0:TP]), over4(m), ALU.mult).then_inc(S.lm, 1)
                                    dve.wait_ge(S.lm, g * NL + l)
                                    if l == 1:
                                        ch(tt(tiles4(att[:, 0:TP]), tiles4(dps[:, 1, :]), d4, ALU.mult))
                                        ch(tt(att[0:TS, TP:T], dps[0:TS, 2, TS:2 * TS], ds_, ALU.mult))
                                        ch(dve.tensor_copy(ktok[0:TS, NCH, :], dps[0:TS, 2, 2 * TS:2 * TS + P]))
                            if e == 30 and B:
                                dve.wait_ge(S.dlev, g * NL + NL)
                                tt(um[:, 0:TP], um[:, 0:TP], dps[:, 2, :], ALU.subtract).then_inc(S.upd, 1)
                                dve.wait_ge(S.upd, g * NL + NL)
                            if e == 10 and A:
                                conv(3, 0, xc, S.evx, S.convx, pack[:, 16:17])
                            if e == 16 and A:
                                dve.wait_ge(S.sigr, h + 1)
                                c = slice(0, CONVW)
                                ts(ry[:, c], ry[:, c], sp16[:, bass.ds(h, 1)], None, ALU.mult).then_inc(S.ydone, 1)
                                dve.wait_ge(S.ydone, h + 1)
                                ch(ts(iu[:, c], ry[:, c], 0.25, None, ALU.min))
                                ch(ts(em[:, c], iu[:, c], -1.0 / 720, None, ALU.mult))
                            if e == 18 and A:
                                for f in (120.0, -24.0, 6.0):
                                    ch(stt(em[:, c], em[:, c], 1.0 / f, iu[:, c], ALU.add, ALU.mult))
                            if e == 20 and A:
                                for f in (-2.0, 1.0):
                                    ch(stt(em[:, c], em[:, c], 1.0 / f, iu[:, c], ALU.add, ALU.mult))
                                dve.wait_ge(S.lruexp, h + 1)
                                ch(ts(e2[:, c], e2[:, c], -1.0, 1.0, ALU.mult, ALU.add))
                                ch(stt(e2[:, c], ry[:, c], 0.25, e2[:, c], ALU.is_ge, ALU.mult))
                                tt(em[:, c], em[:, c], e2[:, c], ALU.max).then_inc(S.emdone, 1)
                            if e == 14 and B:
                                dve.wait_ge(S.xs, g + 1)
                                x = dps[:, 3, 192:320].rearrange("p (b k s) -> p b k s", k=2, s=NS)
                                ch(dve.tensor_copy(samples(kb), x[:, :, 1, :]))
                                tt(rst[:, 0:TS].rearrange("p (b s) -> p b s", b=NB), x[:, :, 0, :], samples(vc),
                                   ALU.add).then_inc(S.rts, 1)
                            if e == 23 and A:
                                dve.wait_ge(S.sqrt, h + 1)
                                dve.wait_ge(S.sigi, h + 1)
                                ch(dve.memset(em[:, 0:1], 1.0))
                                ch(tt(iu[:, c], iu[:, c], em[:, c], ALU.mult))
                                ch(tt(iu[:, c], iu[:, c], xc[:, c], ALU.mult))
                                before = lambda t: t[:, SB0 - 1:SB0 - 1 + NB * SP].rearrange(
                                    "p (b s) -> p b s", b=NB)[:, :, 0]
                                ch(dve.memset(before(la), 0.0))
                                ch(dve.tensor_copy(before(iu), pack[:, 372:380]))
                                dve.tensor_tensor_scan(ry[:, c], la[:, c], iu[:, c], 0.0, ALU.mult,
                                                       ALU.add).then_inc(S.scan, 1)
                                dve.wait_ge(S.scan, h + 1)
                                if later:
                                    dve.wait_ge(S.lrust, h * 32)
                                ch(dve.tensor_copy(hlast[:, 0:1], ry[:, TP - 1:TP]))
                                ch(dve.tensor_copy(hlast[:, 1:NC], padded(ry, NS - 1, 1)[:, :, 0]))
                                dve.wait_ge(S.gely, h + 1)
                                ch(tt(gy[:, 0:TP], gy[:, 0:TP], ry[:, 0:TP], ALU.mult))
                                tt(samples(gy), samples(gy), padded(ry, 0, NS), ALU.mult).then_inc(S.lruout, 1)
                                dve.wait_ge(S.lruout, h + 1)
                            if e == 23 and B:
                                dve.wait_ge(S.vsm, g + 1)
                                ch(dve.tensor_copy(vn[0:TS, 1, :], dps[0:TS, 3, 192:320]))
                                tt(vmask[0:TS, :, :], bc(vn[0:TS, 1, :].unsqueeze(1), [TS, NB, P]),
                                   bc(const[0:TS, C_BM:C_BM + NB].unsqueeze(2), [TS, NB, P]), ALU.mult).then_inc(S.vms, 1)
                                dve.wait_ge(S.vms, g + 1)
                            if e == 26 and B:
                                dve.wait_ge(S.ats, g + 1)
                                tt(kb[:, TP:T], kb[:, TP:T], dps[:, 3, 448:512], ALU.add).then_inc(S.oss, 1)
                                dve.wait_ge(S.oss, g + 1)
                            for n, e_n in ((0, 27), (1, 29)):
                                if e == e_n and B:
                                    v = sst[:, n * 4:n * 4 + 4, :]
                                    w = eglast[:, NCH + n * 4:NCH + n * 4 + 4].unsqueeze(2)
                                    ch(tt(v, v, bc(w, [P, 4, P]), ALU.mult))
                                    dve.wait_ge((S.dss0, S.dss1)[n], g + 1)
                                    tt(v, v, dps[:, 3, :].rearrange("p (b v) -> p b v", v=P),
                                       ALU.add).then_inc((S.sup0, S.sup1)[n], 1)
                            if e == 25 and A:
                                conv(0, 1, e2, S.evq, S.cvq)
                            if e == 34 and A:
                                conv(1, 0, em, S.evk, S.cvk)
                            for t in range(NCH):
                                if e == 32 + 4 * t and B:
                                    dve.wait_ge(S.vp, g * NCH + t + 1)
                                    dve.tensor_copy(vn[:, 0, :], dps[:, 1, 0:P]).then_inc(S.vcp, 1)
                                if e == 33 + 4 * t and B:
                                    dve.wait_ge(S.op, g * NCH + t + 1)
                                    stt(st[:, :], st[:, :], eglast[:, t:t + 1], dps[:, 3, 0:P], ALU.mult,
                                        ALU.add).then_inc(S.sup, 1)
                                    dve.wait_ge(S.sup, g * NCH + t + 1)
                            if e == 42 and A:
                                dve.wait_ge(S.slq, h + 1)
                                conv(2, 1, e2, S.evv, S.cvv)
                            if e == 47 and B:
                                dve.wait_ge(S.oinv, g + 1)
                                dve.wait_ge(S.ocp, g + 1)
                                ch(stt(kb[:, :], kb[:, :], dnw, sqs[:, 1, :], ALU.mult, ALU.mult))
                                tt(kb[:, :], kb[:, :], zc, ALU.mult).then_inc(S.oout, 1)
                                dve.wait_ge(S.oout, g + 1)

                    do_turns(dve, body, W.dve_steps, dve_total, DVE_STEPS_A_TURN)
                    dve.wait_ge(S.mixlast, 1)
                    dve.tensor_tensor(act_lo[:, KT - 1, :], kb[:, :], act_hi[:, KT - 1, :].bitcast(F32),
                                      ALU.subtract).then_inc(S.mixlo, 1)

        N5 = N4 + 2 * KT
        X = Sems()
        X.saved, = sems(stack, "x_saved")
        at4 = [after]
        x1T = sb("x1T", [P, KT, T], at=at4)
        rB2 = sb("rB2", [P, T], at=at4)
        amod2 = sb("amod2", [P, KT, NC], at=at4)
        tmp2 = sb("tmp2", [P, 4, T], at=at4)
        p5at = at4[0]
        xin = sb("xin", [P, 2, T], at=at4)
        sq4 = sb("sq4", [P, 2, T], at=at4)

        def halves2(t):
            return t.rearrange("p (a t) -> p a t", a=2)

        def square_sums(pe, S, sq, m, first, last, banks=dps):
            pe.wait_ge(S.sq, m + 1)
            for th in range(2):
                r = pe.matmul(banks[:, th, 0:HT], ones[:, :], sq[:, th * HT:(th + 1) * HT], start=first, stop=last)
            r.then_inc(S.sqpe, 1)

        with ExitStack() as c4:
            S = Sems()
            S.xl0, = sems(c4, "p4_xl0")
            S.xl1, S.x1, S.sq, S.sqpe = sems(c4, "p4_xl1", "p4_x1", "p4_sq", "p4_sqpe")
            s_xl = [S.xl0, S.xl1]
            with nc.Block() as block:
                @block.sync
                def _(sp):
                    for n in range(2):
                        sp.dma_start(xin[:, n, :], a["x_t"][:, n, :]).then_inc(s_xl[n], 16)
                    for n in range(2, 4):
                        load_half(sp, a["w_out"][n], Nth(N4 + n))
                    with sp.Fori(1, KT // 2) as i:
                        for j in range(4):
                            load_half(sp, row(a["w_out"], i * 4 + j), Nth(N4 + j, i, 4))
                            if j < 2:
                                sp.wait_ge(S.x1, i * 2 + (j - 1))
                                sp.dma_start(xin[:, j, :], a["x_t"][:, bass.ds(i * 2 + j, 1), :].rearrange(
                                    "p k t -> p (k t)")).then_inc(s_xl[j], 16)
                    for n in range(2):
                        load_half(sp, a["w_q"][n], Nth(N5 + n))
                    sp.wait_ge(S.x1, KT)
                    sp.dma_start(x1D, x1T[:, :, :]).then_inc(X.saved, 16)

                @block.scalar
                def _(act):
                    ch = Chain(act, W.act_steps, act_total)
                    for j in (2, 3):
                        split_hi(act, Nth(N4 + j))
                    with act.Fori(1, KT // 2) as i:
                        for j in range(4):
                            split_hi(act, Nth(N4 + j, i, 4))
                    for n in range(2):
                        split_hi(act, Nth(N5 + n))
                    act.wait_ge(S.sqpe, KT)
                    ch(act.activation(halves2(rB2[:, :]), dps[:, 0:2, 0:HT], ACT.Ln, bias=eps[:, :], scale=1.0 / D))
                    ch(act.activation(rB2[:, :], rB2[:, :], ACT.Exp, scale=-0.5))

                @block.gpsimd
                def _(pool):
                    for j in (2, 3):
                        split_lo(pool, Nth(N4 + j))
                    with pool.Fori(1, KT // 2) as i:
                        for j in range(4):
                            split_lo(pool, Nth(N4 + j, i, 4))
                    for n in range(2):
                        split_lo(pool, Nth(N5 + n))

                @block.tensor
                def _(pe):
                    def tile(m, k, pair):
                        if not (isinstance(m, int) and m < 2):
                            pe.wait_ge(S.x1, m - 1)
                        for half in range(2):
                            gemm_part(pe, k.plus(half), half, pair, 0, 8)

                    tile(0, Nth(N4), 0)
                    tile(1, Nth(N4 + 2), 1)
                    square_sums(pe, S, sq4[:, 0, :], 0, True, False)
                    with pe.Fori(1, KT // 2) as i:
                        tile(i * 2, Nth(N4, i, 4), 0)
                        square_sums(pe, S, sq4[:, 1, :], i * 2 - 1, False, False)
                        tile(i * 2 + 1, Nth(N4 + 2, i, 4), 1)
                        square_sums(pe, S, sq4[:, 0, :], i * 2, False, False)
                    square_sums(pe, S, sq4[:, 1, :], KT - 1, False, True)

                @block.vector
                def _(dve):
                    ch = Chain(dve, W.dve_steps, dve_total)
                    def residual(m, i, s):
                        n = N4 + 2 * s + 2
                        dve.wait_ge(W.used, n + i * 4)
                        dve.wait_ge(s_xl[s], i * 16 + 16)
                        at = bass.ds(m, 1)
                        x1 = x1T[:, at, :].rearrange("p k t -> p (k t)")
                        gate = modT[:, bass.ds(m + 2 * KT, 1), :].rearrange("p k n -> p (k n)")
                        pr = 2 * s
                        last = gps[:, pr + 1, TP - HT:HT].rearrange("p (b s) -> p b s", b=NB)
                        ch(dve.tensor_tensor(samples(x1), last, bc(gate[:, 1:NC].unsqueeze(2), [P, NB, NS]), ALU.mult))
                        ch(dve.tensor_tensor(x1[:, TP:T], x1[:, TP:T], xin[:, s, TP:T], ALU.add))
                        ch(dve.scalar_tensor_tensor(x1[:, 0:HT], gps[:, pr, 0:HT], gate[:, 0:1], xin[:, s, 0:HT],
                                                    ALU.mult, ALU.add))
                        dve.scalar_tensor_tensor(x1[:, HT:TP], gps[:, pr + 1, 0:TP - HT], gate[:, 0:1],
                                                 xin[:, s, HT:TP], ALU.mult, ALU.add).then_inc(S.x1, 1)
                        dve.wait_ge(S.x1, m + 1)
                        if not (isinstance(m, int) and m < 2):
                            dve.wait_ge(S.sqpe, m - 1)
                        dve.tensor_tensor(sq4[:, s, :], x1, x1, ALU.mult).then_inc(S.sq, 1)

                    residual(0, 0, 0)
                    residual(1, 0, 1)
                    with dve.Fori(1, KT // 2) as i:
                        ch.enter(i - 1, 6)
                        residual(i * 2, i, 0)
                        residual(i * 2 + 1, i, 1)
                    ch.leave(KT // 2 - 1)

        second_h = modulate(KT, x1T, rB2, amod2, tmp2, normw[1], 3 * KT, 4 * KT)

        N7 = N5 + 4 * H
        EARLY = 2
        at5 = [after]
        clo = sb("clo", [P, EARLY, NG, T], F32R, at=at5)
        early = sb("early", [P, EARLY, NG, T], at=[after])
        slots = sb("slots", [P, NTT, 3, H * TOPK], at=at5)
        p6at = at5[0]
        at5 = [p5at]
        qt = sb("qt", [P, 2, T], at=at5)
        keys = sb("keys", [P, 2, NKEY], at=at5)
        sc = sb("sc", [P, 2, NTT, NKEY], at=at5)
        sc2 = sb("sc2", [P, NTT, NKEY], at=at5)
        topv = sb("topv", [P, NTT, 2, TOPK], at=at5)
        topi = sb("topi", [P, NTT, 2, TOPK], U32, at=at5)
        topf = sb("topf", [P, NTT, 2, TOPK], at=at5)
        WIDE, NARROW = 4 * TOPK, 4
        NCAND = WIDE + (TOPK - 4) * NARROW
        cand = sb("cand", [P, NTT, NCAND], at=at5)
        cand2 = sb("cand2", [P, NTT, NCAND], at=at5)
        hot = sb("hot", [P, NTT, TOPK, TOPK], at=at5)
        bestv = sb("bestv", [P, NTT, TOPK], at=at5)
        pos = sb("pos", [P, NTT, TOPK], U32, at=at5)
        posf = sb("posf", [P, NTT, TOPK], at=at5)
        part = sb("part", [P, 4, NTT, TOPK], U32, at=at5)
        partf = sb("partf", [P, 4, NTT, TOPK], at=at5)
        gsum = sb("gsum", [P, NTT, H], at=at5)
        carrier = sb("carrier", [P, 3], at=at5)
        with ExitStack() as c5:
            S = Sems()
            S.key0, S.key1, S.qev, S.score, S.scev = sems(c5, "p5_key0", "p5_key1", "p5_qev", "p5_score", "p5_scev")
            S.topk0, S.topk1, S.go, S.gmax, S.gexp = sems(c5, "p5_topk0", "p5_topk1", "p5_go", "p5_gmax", "p5_gexp")
            S.early, = sems(c5, "p5_early")
            s_key, s_topk = [S.key0, S.key1], [S.topk0, S.topk1]

            def head_turns(eng, body, ch=None, steps=0):
                body(0)
                with eng.Fori(1, H - 1) as h:
                    if ch:
                        ch.enter(h - 1, steps)
                    body(h)
                if ch:
                    ch.leave(H - 2)
                body(H - 1)

            def wq_half(h, j):
                return Nth(N5 + 4 * h + j) if isinstance(h, int) else Nth(N5 + j, h, 4)

            def prefetched(h, j):
                return isinstance(h, int) and h == 0 and j < 2

            with nc.Block() as block:
                @block.sync
                def _(sp):
                    def body(h):
                        for j in range(4):
                            if not prefetched(h, j):
                                load_half(sp, row(a["w_q"], h * 4 + j), wq_half(h, j))
                            if j % 2:
                                s = j // 2
                                if not isinstance(h, int) or h:
                                    sp.wait_ge(S.score, h * 2 + (s - 1))
                                sp.dma_start(keys[:, s, :], row(a["keys"], h * 2 + s)).then_inc(s_key[s], 16)

                    head_turns(sp, body)
                    for n in range(8 * EARLY):
                        load_half(sp, a["u"][n], Nth(N7 + n))
                    for n in range(2):
                        load_half(sp, a["v"][n], Nth(N7 + 8 * EARLY + n))

                @block.gpsimd
                def _(pool):
                    def body(h):
                        for j in range(4):
                            if not prefetched(h, j):
                                split_lo(pool, wq_half(h, j))

                    second_h[2](pool)
                    head_turns(pool, body)
                    for n in range(8 * EARLY + 2):
                        split_lo(pool, Nth(N7 + n))

                @block.tensor
                def _(pe):
                    def scores(h, s):
                        m = h * 2 + s
                        pe.wait_ge(S.qev, m + 1)
                        pe.wait_ge(s_key[s], h * 16 + 16)
                        if not isinstance(h, int) or h:
                            pe.wait_ge(S.scev, m - 1)
                        for t in range(NTT):
                            n = CH if t < NCH else TS
                            o = dps[:, 2 * s, t * CH:(t + 1) * CH] if t < NCH else dps[0:TS, 2 * s + 1, 0:NKEY]
                            r = pe.matmul(o, qt[:, s, t * CH:t * CH + n], keys[:, s, :], start=True, stop=True)
                        r.then_inc(S.score, 1)

                    def body(h):
                        later = not isinstance(h, int) or h > 0
                        for s in range(2):
                            if later:
                                pe.wait_ge(S.qev, h * 2 + (s - 1))
                            for half in range(2):
                                gemm_part(pe, wq_half(h, 2 * s + half), half, s, 0, 8,
                                          None if later or s else second_h[3])
                            if s == 0 and later:
                                scores(h - 1, 1)
                            if s == 1:
                                scores(h, 0)

                    head_turns(pe, body)
                    scores(H - 1, 1)
                    pe.wait_ge(S.qev, 2 * H)
                    for c in range(EARLY * NG):
                        if c >= 2:
                            pe.wait_ge(S.early, c - 1)
                        for half in range(2):
                            gemm_part(pe, Nth(N7 + 2 * c + half), half, c % 2, 0, 8)

                @block.scalar
                def _(act):
                    ch = Chain(act, W.act_steps, act_total)

                    def take_scores(h, s):
                        act.wait_ge(S.score, h * 2 + s + 1)
                        if not isinstance(h, int) or h:
                            act.wait_ge(s_topk[s], h)
                        ch(act.copy(sc[:, s, 0:NCH, :], dps[:, 2 * s, :].rearrange("p (t n) -> p t n", n=NKEY)))
                        act.copy(sc[0:TS, s, NCH, :], dps[0:TS, 2 * s + 1, 0:NKEY]).then_inc(S.scev, 1)

                    def body(h):
                        later = not isinstance(h, int) or h > 0
                        for s in range(2):
                            for j in (2 * s + 2, 2 * s + 3):
                                split_hi(act, wq_half(h, j))
                            act.wait_ge(W.used, wq_half(h, 2 * s + 1).n + 1)
                            if later:
                                act.wait_ge(S.score, h * 2 + (s - 1))
                            act.copy(halves2(qt[:, s, :]), gps[:, 2 * s:2 * s + 2, 0:HT]).then_inc(S.qev, 1)
                            if s == 0 and later:
                                take_scores(h - 1, 1)
                            if s == 1:
                                take_scores(h, 0)

                    second_h[1](act)
                    act.wait_ge(S.go, 1)
                    body(0)
                    with act.Fori(1, H - 1) as h:
                        ch.enter(h - 1, 2)
                        body(h)
                    ch.leave(H - 2)
                    body(H - 1)
                    for j in (2, 3):
                        split_hi(act, Nth(N7 + j))
                    take_scores(H - 1, 1)
                    act.wait_ge(X.saved, 16)
                    for c in range(EARLY * NG):
                        if c:
                            for j in (2 * c + 2, 2 * c + 3):
                                split_hi(act, Nth(N7 + j))
                        act.wait_ge(W.used, N7 + 2 * c + 2)
                        act.activation(halves2(early[:, c // NG, c % NG, :]), gps[:, 2 * (c % 2):2 * (c % 2) + 2, 0:HT],
                                       ACT.Gelu_apprx_tanh).then_inc(S.early, 1)
                        if c == EARLY * NG - 3:
                            act.wait_ge(S.gmax, 1)
                            act.activation(slots[:, :, 2, :], slots[:, :, 2, :], ACT.Exp).then_inc(S.gexp, 1)

                @block.vector
                def _(dve):
                    dve.memset(sc[:, :, NCH, :], 0.0).then_inc(S.go, 1)
                    dve.wait_ge(S.go, 1)

                    second_h[0](dve)

                    def carry(n=0):
                        dve.memset(carrier[:, n:n + 1], 0.0)

                    ch = Chain(dve, W.dve_steps, dve_total, carry)

                    def each(fn):
                        for t in range(NTT):
                            m = fn(t)
                        ch(m)

                    def top16(values, less, v, i):
                        each(lambda t: dve.max(v(t)[:, 0:8], values(t)))
                        each(lambda t: dve.max_index(i(t)[:, 0:8], v(t)[:, 0:8], values(t)))
                        each(lambda t: dve.match_replace(less(t), v(t)[:, 0:8], values(t), LOW))
                        each(lambda t: dve.max(v(t)[:, 8:16], less(t)))
                        each(lambda t: dve.max_index(i(t)[:, 8:16], v(t)[:, 8:16], less(t)))

                    def body(h):
                        for s in range(2):
                            dve.wait_ge(S.scev, h * 2 + s + 1)
                            carry(1 + s)
                            top16(lambda t: sc[:, s, t, :], lambda t: sc2[:, t, :], lambda t: topv[:, t, s, :],
                                  lambda t: topi[:, t, s, :])
                            dve.tensor_copy(topf[:, :, s, :], topi[:, :, s, :]).then_inc(s_topk[s], 1)
                            dve.wait_ge(s_topk[s], h + 1)
                        for out, first, second in (
                                (cand[:, :, 0:WIDE], topv[:, :, 0, 0:4], topv[:, :, 1, :]),
                                (cand[:, :, WIDE:NCAND], topv[:, :, 0, 4:TOPK], topv[:, :, 1, 0:NARROW])):
                            both = [P, NTT, first.shape[2], second.shape[2]]
                            m = dve.tensor_tensor(out.rearrange("p t (a b) -> p t a b", b=both[3]),
                                                  bc(first.unsqueeze(3), both), bc(second.unsqueeze(2), both), ALU.add)
                        ch(m)
                        top16(lambda t: cand[:, t, :], lambda t: cand2[:, t, :], lambda t: bestv[:, t, :],
                              lambda t: pos[:, t, :])
                        mine = bass.ds(h * TOPK, TOPK)
                        dve.tensor_copy(slots[:, :, 2, mine], bestv[:, :, :])
                        dve.tensor_copy(posf[:, :, :], pos[:, :, :])
                        dve.tensor_scalar(part[:, 0], pos[:, :, :], 4, None, ALU.logical_shift_right)
                        dve.tensor_scalar(part[:, 1], pos[:, :, :], 2, None, ALU.logical_shift_right)
                        dve.tensor_scalar(part[:, 2], pos[:, :, :], 12, None, ALU.bitwise_and)
                        ch(dve.tensor_scalar(part[:, 3], pos[:, :, :], 3, None, ALU.bitwise_and))
                        ch(dve.tensor_copy(partf[:, :, :, :], part[:, :, :, :]))
                        dve.scalar_tensor_tensor(partf[:, 0], partf[:, 1], -12.0, partf[:, 0], ALU.add, ALU.max)
                        ch(dve.scalar_tensor_tensor(partf[:, 2], posf[:, :, :], float(WIDE), partf[:, 2], ALU.is_lt,
                                                    ALU.mult))
                        ch(dve.tensor_tensor(partf[:, 1], partf[:, 2], partf[:, 3], ALU.add))
                        full = [P, NTT, TOPK, TOPK]
                        ramp = const[:, C_IOTA:C_IOTA + TOPK].unsqueeze(1).unsqueeze(1)
                        for s in range(2):
                            ch(dve.tensor_tensor(hot[:, :, :, :], bc(partf[:, s].unsqueeze(3), full),
                                                 bc(ramp, full), ALU.is_equal))
                            ch(dve.tensor_tensor(hot[:, :, :, :], hot[:, :, :, :],
                                                 bc(topf[:, :, s, :].unsqueeze(2), full), ALU.mult))
                            ch(dve.tensor_reduce(slots[:, :, s, mine], hot[:, :, :, :], AX.X, ALU.add))

                    dve.wait_ge(X.saved, 16)
                    head_turns(dve, body, ch, 26)
                    g = slots[:, :, 2, :].rearrange("p t (h k) -> p t h k", k=TOPK)
                    ch(dve.tensor_copy(gsum[:, :, :], g[:, :, :, 0]))
                    dve.tensor_tensor(g, g, bc(gsum[:, :, :].unsqueeze(3), [P, NTT, H, TOPK]),
                                      ALU.subtract).then_inc(S.gmax, 1)
                    dve.wait_ge(S.gexp, 1)
                    ch(dve.tensor_reduce(gsum[:, :, :], g, AX.X, ALU.add))
                    ch(dve.reciprocal(gsum[:, :, :], gsum[:, :, :]))
                    ch(dve.tensor_tensor(g, g, bc(gsum[:, :, :].unsqueeze(3), [P, NTT, H, TOPK]), ALU.mult))


        OCT = 8
        QUAD = 4
        TURN = 4 * GB
        OCTS, QUADS = TURN // OCT, TURN // QUAD
        QPB = GB // QUAD
        at6 = [p6at]
        slotT = sb("slotT", [P, 3, T], at=at6)
        ga = sb("ga", [P, 2, OCT, NKEY], at=at6)
        gb = sb("gb", [P, 2, OCT, NKEY], at=at6)
        gst = [sb(f"gst{n}", [P, NKEY, GB], at=at6) for n in range(2)]
        with ExitStack() as c6:
            S = Sems()
            S.tr, S.trev, S.first, S.apool, S.advec = sems(c6, "p6_tr", "p6_trev", "p6_first", "p6_apool", "p6_advec")
            S.b, S.mm, S.ev, S.out0, S.out1 = sems(c6, "p6_b", "p6_mm", "p6_ev", "p6_out0", "p6_out1")
            s_out = [S.out0, S.out1]

            with nc.Block() as block:
                @block.sync
                def _(sp):
                    with sp.Fori(0, NGB // 4) as i:
                        for b in range(4):
                            sp.wait_ge(S.ev, i * QUADS + (4 + QPB * (b + 1)))
                            sp.dma_start(gateD[bass.ds(i * 4 + b, 1)].rearrange("b j i t -> (b j) (i t)"),
                                         gst[b % 2][:, :, :].rearrange("p i t -> p (i t)")).then_inc(s_out[b % 2], 16)
                    for b in range(2):
                        sp.wait_ge(s_out[b], 16 + 16 * (NGB // 2))

                @block.tensor
                def _(pe):
                    for k in range(3):
                        for t in range(NCH):
                            pe.transpose(dps[:, k, t * CH:(t + 1) * CH], slots[:, t, k, :], ident)
                        m = pe.transpose(dps[:, 3, k * TS:(k + 1) * TS], slots[0:TS, NCH, k, :], const[0:TS, 0:TS])
                    m.then_inc(S.tr, 1)
                    pe.wait_ge(S.trev, 4)
                    with pe.Fori(0, NGB // 4) as i:
                        for o in range(OCTS):
                            pe.wait_ge(S.apool if o % 2 else S.advec, i * (OCTS // 2) + (o // 2 + 1))
                            pe.wait_ge(S.b, i * OCTS + (o + 1))
                            for q in range(2):
                                bank = 2 * o + q
                                pe.wait_ge(S.ev, i * QUADS + (bank + 1))
                                for t in range(QUAD):
                                    m = pe.matmul(dps[:, bank % 4, t * NKEY:(t + 1) * NKEY],
                                                  gb[:, o % 2, q * QUAD + t, :], ga[:, o % 2, q * QUAD + t, :],
                                                  start=True, stop=True)
                                m.then_inc(S.mm, 1)

                @block.scalar
                def _(act):
                    act.wait_ge(S.tr, 1)
                    for k in range(3):
                        act.copy(slotT[:, k, 0:TP], dps[:, k, :]).then_inc(S.trev, 1)
                    act.copy(slotT[:, :, TP:T], dps[:, 3, 0:3 * TS].rearrange("p (k t) -> p k t", k=3)
                             ).then_inc(S.trev, 1)
                    with act.Fori(0, NGB // 4) as i:
                        for n in range(QUADS):
                            b, q = n // QPB, n % QPB
                            if q == 0:
                                act.wait_ge(s_out[b % 2], i * 32 + (b // 2 * 16 + 16))
                            act.wait_ge(S.mm, i * QUADS + (4 + n + 1))
                            act.copy(gst[b % 2][:, :, q * QUAD:(q + 1) * QUAD],
                                     dps[:, n % 4, :].rearrange("p (t i) -> p i t", i=NKEY)).then_inc(S.ev, 1)

                def compare(out, kind, at):
                    full = [P, OCT, NKEY]
                    return nc.vector.tensor_tensor(out, bc(slotT[:, kind, at].unsqueeze(2), full),
                                             bc(const[:, C_IOTA:C_IOTA + NKEY].unsqueeze(1), full), ALU.is_equal)

                def times_gate(eng, o, at):
                    return eng.tensor_tensor(ga[:, o % 2], ga[:, o % 2],
                                             bc(slotT[:, 2, at].unsqueeze(2), [P, OCT, NKEY]), ALU.mult)

                def tokens(i, o):
                    return bass.ds(i * TURN + o * OCT, OCT)

                @block.gpsimd
                def _(pool):
                    pool.wait_ge(S.trev, 4)
                    with pool.Fori(0, NGB // 4) as i:
                        for o in range(1, OCTS, 2):
                            pool.wait_ge(S.first, i * (OCTS // 2) + (o + 1) // 2)
                            times_gate(pool, o, tokens(i, o)).then_inc(S.apool, 1)

                @block.vector
                def _(dve):
                    for n in range(4):
                        dve.engine_nop().then_inc(S.mm, 1)
                        dve.engine_nop().then_inc(S.ev, 1)
                    for b in range(2):
                        dve.engine_nop().then_inc(s_out[b], 16)
                    ch = Chain(dve, W.dve_steps, dve_total)
                    dve.wait_ge(S.trev, 4)
                    with dve.Fori(0, NGB // 4) as i:
                        ch.enter(i, OCTS // 2)
                        for o in range(OCTS):
                            dve.wait_ge(S.mm, i * QUADS + (2 * o + 2))
                            m = compare(ga[:, o % 2], 0, tokens(i, o))
                            if o % 2:
                                m.then_inc(S.first, 1)
                            else:
                                ch(m)
                                times_gate(dve, o, tokens(i, o)).then_inc(S.advec, 1)
                            compare(gb[:, o % 2], 1, tokens(i, o)).then_inc(S.b, 1)
                    ch.leave(NGB // 4)

        at7 = [after + EARLY * NG * T * 4]
        outacc = sb("outacc", [P, KT, T], at=at7)
        gate = sb("gate", [P, 2, NGB, 2, GB], at=at7)
        chi = sb("chi", [P, 2, NG, T], F32R, at=at7)
        gel = sb("gel", [P, 2, T], at=at7)
        at8 = [act_at]
        x2T = sb("x2T", [P, KT, T], at=at8)
        sq8 = sb("sq8", [P, 2, T], at=at8)
        rB3 = sb("rB3", [P, T], at=at8)
        with ExitStack() as c7:
            S = Sems()
            S.gate0, S.gate1, S.gel, S.gated, S.chi = sems(c7, "p7_gate0", "p7_gate1", "p7_gel", "p7_gated", "p7_chi")
            S.clo, S.vd, S.acc, S.zero = sems(c7, "p7_clo", "p7_vd", "p7_acc", "p7_zero")
            S.x2, S.sq, S.sqpe = sems(c7, "p7_x2", "p7_sq", "p7_sqpe")
            s_gate = [S.gate0, S.gate1]

            def first_u(g, i):
                return Nth(N7 + 16 * g - 8, i, 32)

            def first_v(g, i=None):
                if i is None:
                    return Nth(N7 + min(16 * g + 16, 2 * 8 * NGRP - 8))
                return Nth(N7 + 16 * g + 16, i, 32)

            def groups(eng, A, B):
                with eng.Fori(0, NGRP // 2 - 1) as i:
                    B(i * 2, 0, first_v(0, i), first_u(2, i))
                    A(i * 2 + 2, 0, first_u(2, i), first_v(1, i))
                    B(i * 2 + 1, 1, first_v(1, i), first_u(3, i))
                    A(i * 2 + 3, 1, first_u(3, i), first_v(2, i))
                B(NGRP - 2, 0, first_v(NGRP - 2), first_v(NGRP - 1))
                B(NGRP - 1, 1, first_v(NGRP - 1), None)

            with nc.Block() as block:
                @block.sync
                def _(sp):
                    def load_gates(g, pair):
                        if not isinstance(g, int) or g:
                            sp.wait_ge(S.gated, g * NG + (2 * pair - 2))
                        sp.dma_start(gate[:, pair].rearrange("p b c t -> p b (c t)"),
                                     gateD[:, :, bass.ds(g * NG + 2 * pair, 2), :].rearrange(
                                         "b j i t -> j b (i t)")).then_inc(s_gate[pair], 16)

                    def A(g, buf, k, after):
                        for j in range(2 * NG):
                            if j % 4 == 0:
                                load_gates(g, j // 4)
                            if j < 6:
                                load_half(sp, row(a["u"], g * 8 + (j + 2)), k.plus(j + 2))
                            else:
                                load_half(sp, row(a["v"], g * 8 + (j - 6 - 8)), after.plus(j - 6))

                    def B(g, buf, k, after):
                        if after is None:
                            sp.wait_ge(W.used, N7 + 16 * NGRP - 16)
                        for s in range(8):
                            if after is None and s < 4:
                                sp.wait_ge(X.saved, 16 * s + 16)
                                sp.dma_start(x2T[:, 4 * s:4 * s + 4, :], x1D[:, 4 * s:4 * s + 4, :]
                                             ).then_inc(X.saved, 16)
                            if s < 6:
                                load_half(sp, row(a["v"], g * 8 + (s + 2)), k.plus(s + 2))
                            elif not isinstance(g, int):
                                load_half(sp, row(a["u"], g * 8 + (s - 6 + 16)), after.plus(s - 6))
                            elif after is not None:
                                load_half(sp, row(a["v"], g * 8 + (s - 6 + 8)), after.plus(s - 6))

                    for g in range(EARLY):
                        for pair in range(2):
                            load_gates(g, pair)
                    groups(sp, A, B)

                @block.gpsimd
                def _(pool):
                    def both(g, buf, k, after):
                        for j in range(2, 10):
                            if j < 8:
                                split_lo(pool, k.plus(j))
                            elif after is not None:
                                split_lo(pool, after.plus(j - 8))

                    pool.memset(outacc[:, :, :], 0.0).then_inc(S.zero, 1)
                    groups(pool, both, both)

                @block.tensor
                def _(pe):
                    def A(g, buf, k, after):
                        for c in range(NG):
                            pe.wait_ge(S.gel, g * NG + (c - 1))
                            for half in range(2):
                                gemm_part(pe, k.plus(2 * c + half), half, c % 2, 0, 8)

                    def B(g, buf, k, after):
                        pe.wait_ge(S.clo, g * NG + NG)
                        for s in range(8):
                            pe.wait_ge(W.lo, k.plus(s).n + 1)
                            slot = k.plus(s).slot
                            for dt in range(2):
                                pe.wait_ge(S.acc, g * KT + (2 * s + dt + 1))
                                for c in range(NG):
                                    cols = slice(c * 2 * P + dt * P, c * 2 * P + (dt + 1) * P)
                                    for n, (w, x) in enumerate(((whi, chi), (whi, clo), (wlo, chi))):
                                        for th in range(2):
                                            m = pe.matmul(dps[:, 2 * dt + th, 0:HT], w[:, slot, cols],
                                                          x[:, buf, c, th * HT:(th + 1) * HT],
                                                          start=(c == 0 and n == 0), stop=(c == NG - 1 and n == 2))
                                m.then_inc((S.vd, W.used)[dt], 1)
                            if after is None and s:
                                if s == 1:
                                    pe.wait_ge(S.gel, NKEY)
                                for n in (2 * s - 2, 2 * s - 1):
                                    square_sums(pe, S, sq8[:, n % 2, :], n, n == 0, False, gps)
                        if after is None:
                            for n in (KT - 2, KT - 1):
                                square_sums(pe, S, sq8[:, n % 2, :], n, False, n == KT - 1, gps)

                    groups(pe, A, B)

                @block.scalar
                def _(act):
                    def A(g, buf, k, after):
                        for c in range(NG):
                            for j in (2 * c + 2, 2 * c + 3):
                                split_hi(act, k.plus(j) if j < 8 else after.plus(j - 8))
                            act.wait_ge(W.used, k.plus(2 * c + 1).n + 1)
                            act.wait_ge(S.clo, g * NG + (c - 1))
                            act.activation(halves2(gel[:, c % 2, :]), gps[:, 2 * (c % 2):2 * (c % 2) + 2, 0:HT],
                                           ACT.Gelu_apprx_tanh).then_inc(S.gel, 1)
                            act.wait_ge(S.gated, g * NG + (c + 1))
                            act.copy(chi[:, buf, c, :], gel[:, c % 2, :]).then_inc(S.chi, 1)

                    def B(g, buf, k, after):
                        for s in range(8):
                            if s < 6:
                                split_hi(act, k.plus(s + 2))
                            elif after is not None:
                                split_hi(act, after.plus(s - 6))
                            if after is None:
                                for n in (2 * s, 2 * s + 1):
                                    act.wait_ge(S.x2, n + 1)
                                    if n >= 2:
                                        act.wait_ge(S.sqpe, n - 1)
                                    act.activation(sq8[:, n % 2, :], x2T[:, n, :], ACT.Square).then_inc(S.sq, 1)

                    for c in range(EARLY * NG):
                        act.wait_ge(S.gated, c + 1)
                        act.copy(chi[:, c // NG, c % NG, :], early[:, c // NG, c % NG, :]).then_inc(S.chi, 1)
                    groups(act, A, B)

                @block.vector
                def _(dve):
                    for n in range(2):
                        dve.engine_nop().then_inc(S.acc, 1)
                    for n in range(EARLY * NG):
                        dve.engine_nop().then_inc(S.gel, 1)

                    def gated(g, c, gel):
                        dve.wait_ge(s_gate[c // 2], g * 16 + 16)
                        ge = gel.rearrange("p (b t) -> p b t", t=GB)
                        dve.tensor_tensor(ge, ge, gate[:, c // 2, :, c % 2, :], ALU.mult).then_inc(S.gated, 1)

                    def rest(g, buf, c, gel):
                        dve.wait_ge(S.chi, g * NG + (c + 1))
                        dve.tensor_tensor(clo[:, buf, c, :], gel, chi[:, buf, c, :].bitcast(F32),
                                          ALU.subtract).then_inc(S.clo, 1)

                    def A(g, buf, k, after):
                        for c in range(NG):
                            dve.wait_ge(S.gel, g * NG + (c + 1))
                            gated(g, c, gel[:, c % 2, :])
                            rest(g, buf, c, gel[:, c % 2, :])

                    def B(g, buf, k, after):
                        dve.wait_ge(S.acc, g * KT + 2)
                        for s in range(8):
                            for dt in range(2):
                                if dt == 0:
                                    dve.wait_ge(S.vd, g * 8 + (s + 1))
                                else:
                                    dve.wait_ge(W.used, k.plus(s).n + 1)
                                out = halves2(outacc[:, 2 * s + dt, :])
                                dve.tensor_tensor(out, out, dps[:, 2 * dt:2 * dt + 2, 0:HT], ALU.add
                                                  ).then_inc(S.acc, 1)
                            if after is None:
                                dve.wait_ge(S.acc, g * KT + (2 * s + 4))
                                for n in (2 * s, 2 * s + 1):
                                    residual2(n)

                    ch = Chain(dve, W.dve_steps, dve_total)

                    def residual2(k):
                        dve.wait_ge(X.saved, 32 + k // 4 * 16)
                        gate2 = modT[:, 5 * KT + k, :]
                        out = outacc[:, k, :]
                        ch(dve.tensor_tensor(samples(out), samples(out), bc(gate2[:, 1:NC].unsqueeze(2), [P, NB, NS]),
                                             ALU.mult))
                        ch(dve.tensor_tensor(x2T[:, k, TP:T], x2T[:, k, TP:T], out[:, TP:T], ALU.add))
                        dve.scalar_tensor_tensor(x2T[:, k, 0:TP], out[:, 0:TP], gate2[:, 0:1], x2T[:, k, 0:TP],
                                                 ALU.mult, ALU.add).then_inc(S.x2, 1)

                    for g in range(EARLY):
                        for c in range(NG):
                            gated(g, c, early[:, g, c, :])
                        for c in range(NG):
                            rest(g, g, c, early[:, g, c, :])
                    dve.wait_ge(S.zero, 1)
                    groups(dve, A, B)

        with ExitStack() as c8:
            S = Sems()
            S.rstd, = sems(c8, "p8_rstd")
            S.y, S.out = sems(c8, "p8_y", "p8_out")
            with nc.Block() as block:
                @block.sync
                def _(sp):
                    for k in range(0, KT, 2):
                        sp.wait_ge(S.y, k + 2)
                        sp.dma_start(a["y_t"][:, k:k + 2, :], x2T[:, k:k + 2, :]).then_inc(S.out, 16)
                    sp.wait_ge(S.out, 16 * (KT // 2))

                @block.vector
                def _(dve):
                    dve.wait_ge(S.rstd, 1)
                    for k in range(KT):
                        dve.scalar_tensor_tensor(x2T[:, k, :], x2T[:, k, :], normw[2][:, k:k + 1], rB3[:, :],
                                                 ALU.mult, ALU.mult).then_inc(S.y, 1)

                @block.scalar
                def _(act):
                    ch = Chain(act, W.act_steps, act_total)
                    ch(act.activation(halves2(rB3[:, :]), gps[:, 0:2, 0:HT], ACT.Ln, bias=eps[:, :], scale=1.0 / D))
                    act.activation(rB3[:, :], rB3[:, :], ACT.Exp, scale=-0.5).then_inc(S.rstd, 1)


def layout(i):
    np_ = lambda name: np.asarray(i[name])
    cols = lambda v, n: np.ascontiguousarray(v.reshape(n, P).T)

    def halves(w):
        m = w.shape[1] // P
        return np.ascontiguousarray(w.reshape(2, 8, P, m, P).transpose(3, 0, 2, 1, 4)).reshape(2 * m, P, HALF)

    x = np.concatenate([np_("x_prompt").reshape(TP, D), np_("x_sample").reshape(TS, D)])
    c = np.concatenate([np_("c_prompt"), np_("c_sample")])
    w_in = np_("w_in")[0]
    qkv, z, ba = 2 * H * P, 5 * H * P, 6 * H * P
    tiles = []
    for h in range(H):
        for at in (0, H * P, qkv, qkv + H * P, qkv + 2 * H * P, z):
            tiles.append(w_in[:, at + h * P:at + (h + 1) * P])
    w_ba = np.zeros((D, P), w_in.dtype)
    w_ba[:, 0:H] = w_in[:, ba:ba + H]
    w_ba[:, 32:32 + H] = w_in[:, ba + H:ba + 2 * H]
    dcw, lcw = np_("dn_conv_w")[0], np_("lru_conv_w")[0]
    dst, lst = np_("state_dn_conv")[0], np_("state_lru_conv")[0]
    pack = np.zeros((H, P, PACK), w_in.dtype)
    for h in range(H):
        s = slice(h * P, (h + 1) * P)
        for n in range(3):
            ch = slice((n * H + h) * P, (n * H + h + 1) * P)
            pack[h, :, n * CW:(n + 1) * CW] = dcw[:, ch].T
            pack[h, :, 20 + n * 24:20 + (n + 1) * 24] = dst[:, :, ch].transpose(2, 0, 1).reshape(P, 24)
        pack[h, :, 12:16] = lcw[:, s].T
        pack[h, :, 92:116] = lst[:, :, s].transpose(2, 0, 1).reshape(P, 24)
        pack[h, :, 16] = np_("lru_conv_b")[0, s]
        pack[h, :, 17] = np_("lru_ba")[0, s]
        pack[h, :, 18] = np_("lru_bx")[0, s]
        pack[h, :, 116:244] = np_("lru_wa")[0, h]
        pack[h, :, 244:372] = np_("lru_wx")[0, h]
        pack[h, :, 372:380] = np_("state_lru_h")[0][:, s].T
    u = np_("peer_u")[0].reshape(NKEY, P, 2, 8, P).transpose(0, 2, 4, 3, 1)
    v = np_("peer_v")[0].reshape(NGRP, NG, P, 8, 2 * P).transpose(0, 3, 2, 1, 4)
    return {
        "consts": constants(),
        "vecs": np.concatenate([cols(np_("b_ada")[0], NM), cols(np_("norm_mix_w")[0], KT),
                                cols(np_("norm_ffn_w")[0], KT), cols(np_("final_norm_w"), KT),
                                np_("dn_norm_w")[0][:, None]], axis=1),
        "c_t": np.ascontiguousarray(c.reshape(NC, KT, P).transpose(2, 1, 0)),
        "x_t": np.ascontiguousarray(x.reshape(T, KT, P).transpose(2, 1, 0)),
        "w_ada": np_("w_ada")[0],
        "lam_t": cols(np_("lru_lambda")[0], H),
        "head_v": np.stack([np_("dn_A_log")[0], np_("dn_dt_bias")[0]], axis=1),
        "w_ba": halves(w_ba),
        "w_in": halves(np.concatenate(tiles, axis=1)),
        "pack": pack,
        "dn_s": np_("state_dn_S")[0],
        "w_out": halves(np_("w_out")[0]),
        "w_q": halves(np_("peer_wq")[0]),
        "keys": np.ascontiguousarray(np_("peer_subkeys")[0].transpose(0, 1, 3, 2)).reshape(2 * H, P, NKEY),
        "u": np.ascontiguousarray(u).reshape(2 * NKEY, P, HALF),
        "v": np.ascontiguousarray(v).reshape(8 * NGRP, P, HALF),
    }


OUTS = {
    "y_t": (P, KT, T),
    "conv_t": (H, P, 4 * NC * PL),
    "lru_h_t": (H, P, NC),
    "s_prompt": (H, P, P),
    "s_sample": (NB, H, P, P),
}


def unlayout(r):
    y = r["y_t"].transpose(2, 1, 0).reshape(T, D)
    conv = r["conv_t"].reshape(H, P, 4, NC, PL)
    dn = conv[:, :, 0:3].transpose(3, 4, 2, 0, 1).reshape(NC, PL, 3 * H * P)
    lc = conv[:, :, 3].transpose(2, 3, 0, 1).reshape(NC, PL, H * P)
    lh = r["lru_h_t"].transpose(2, 0, 1).reshape(NC, H * P)
    own = lambda v: np.ascontiguousarray(v)
    return (own(y[:TP].reshape(1, TP, D)), own(y[TP:].reshape(NB, NS, D)),
            own(lc[None, 0:1]), own(lh[None, 0:1]), own(dn[None, 0:1]), own(r["s_prompt"][None, None]),
            own(lc[None, 1:]), own(lh[None, 1:]), own(dn[None, 1:]), own(r["s_sample"][None]))


def kernel(**inputs):
    import concourse.bacc as bacc
    from concourse.bass_utils import run_bass_kernel_spmd

    nc = bacc.Bacc("TRN2", target_bir_lowering=False, num_devices=1)
    arrays, aps = {}, {}
    for name, v in layout(inputs).items():
        arrays[f"in_{name}"] = v
        aps[name] = nc.dram_tensor(f"in_{name}", v.shape, mybir.dt.from_np(v.dtype), kind="ExternalInput").ap()
    for name, shape in OUTS.items():
        aps[name] = nc.dram_tensor(f"out_{name}", shape, F32, kind="ExternalOutput").ap()
    build(nc, aps)
    r = run_bass_kernel_spmd(nc, [arrays], core_ids=[0])
    return unlayout({name: r.results[0][f"out_{name}"] for name in OUTS})
```
